# Optimizing a Trainium2 kernel written in Bass

```python
import jax, jax.numpy as jnp
from jax import lax
import numpy as np

D_MODEL = 1024
BATCH = 1
SEQ = 512
DEPTH = 2
DEC_BATCH = 1
DEC_SEQ = 256
PAST_LEN = 128

GRID_W = 64
EPS = 1e-6
GLA_HEADS = 4
GLA_KEY_DIM = D_MODEL // 2
GLA_VALUE_DIM = D_MODEL
GLA_DK = GLA_KEY_DIM // GLA_HEADS
GLA_DV = GLA_VALUE_DIM // GLA_HEADS
GATE_RANK = 16
GATE_NORMALIZER = 16.0
GLA_CHUNK = 64
ATT_HEAD_DIM = 64
ATT_Q_HEADS = D_MODEL // ATT_HEAD_DIM
ATT_KV_HEADS = 4
ATT_GROUP = ATT_Q_HEADS // ATT_KV_HEADS
ATT_Q_DIM = ATT_Q_HEADS * ATT_HEAD_DIM
ATT_KV_DIM = ATT_KV_HEADS * ATT_HEAD_DIM
ROPE_AXIS_DIM = ATT_HEAD_DIM // 2
ROPE_THETA = 10000.0
Q_BLOCK = 128
IN_SIZES = (GLA_KEY_DIM, GLA_KEY_DIM, GLA_VALUE_DIM, GATE_RANK, GATE_RANK, GLA_VALUE_DIM,
            ATT_Q_DIM, ATT_KV_DIM, ATT_KV_DIM, ATT_Q_DIM, D_MODEL, D_MODEL)
IN_DIM = sum(IN_SIZES)

kernel_name = 'hybrid_gla_axial_gqa_encoder'

def rmsnorm(x, g):
    xf = x.astype(jnp.float32)
    y = xf * lax.rsqrt(jnp.mean(xf * xf, axis=-1, keepdims=True) + EPS)
    return (y * g.astype(jnp.float32)).astype(x.dtype)

def split_points():
    pts, acc = [], 0
    for s in IN_SIZES[:-1]:
        acc += s
        pts.append(acc)
    return pts

def gla_scan(q, k, v, g, strict):
    B, H, T, dk = q.shape
    dv = v.shape[-1]
    n = T // GLA_CHUNK

    def to_chunks(a):
        return jnp.moveaxis(a.reshape(B, H, n, GLA_CHUNK, a.shape[-1]), 2, 0)

    idx = jnp.arange(GLA_CHUNK)
    mask = (idx[:, None] > idx[None, :]) if strict else (idx[:, None] >= idx[None, :])

    def step(S, inp):
        qi, ki, vi, gi = inp
        b = jnp.cumsum(gi, axis=2)
        diff = b[:, :, :, None, :] - b[:, :, None, :, :]
        decay = jnp.exp(jnp.where(mask[None, None, :, :, None], diff, -jnp.inf))
        A = jnp.einsum('bhic,bhjc,bhijc->bhij', qi, ki, decay)
        o = (jnp.einsum('bhij,bhjv->bhiv', A, vi)
             + jnp.einsum('bhic,bhcv->bhiv', qi * jnp.exp(b), S))
        b_last = b[:, :, -1:, :]
        S = (jnp.exp(b_last[:, :, 0, :])[..., None] * S
             + jnp.einsum('bhjc,bhjv->bhcv', ki * jnp.exp(b_last - b), vi))
        return S, o

    S0 = jnp.zeros((B, H, dk, dv), jnp.float32)
    _, o = lax.scan(step, S0, (to_chunks(q), to_chunks(k), to_chunks(v), to_chunks(g)))
    return jnp.moveaxis(o, 0, 2).reshape(B, H, T, dv)

def gla_branch(qa, ka, va, gfl, gbl, za, w_gate_f, b_gate_f, w_gate_b, b_gate_b,
               gla_norm_g, w_branch_a):
    B, T, _ = qa.shape

    def heads(a, d):
        return a.reshape(B, T, GLA_HEADS, d).transpose(0, 2, 1, 3).astype(jnp.float32)

    q = heads(qa, GLA_DK) * (GLA_DK ** -0.5)
    k = heads(ka, GLA_DK)
    v = heads(va, GLA_DV)
    gf = heads(jax.nn.log_sigmoid((gfl @ w_gate_f + b_gate_f).astype(jnp.float32)) / GATE_NORMALIZER, GLA_DK)
    gb = heads(jax.nn.log_sigmoid((gbl @ w_gate_b + b_gate_b).astype(jnp.float32)) / GATE_NORMALIZER, GLA_DK)
    flip = lambda a: jnp.flip(a, axis=2)
    o_f = gla_scan(q, k, v, gf, False)
    o_b = flip(gla_scan(flip(q), flip(k), flip(v), flip(gb), True))
    o = (o_f + o_b).transpose(0, 2, 1, 3)
    o = rmsnorm(o, gla_norm_g).reshape(B, T, GLA_VALUE_DIM).astype(za.dtype)
    return (o * jax.nn.silu(za)) @ w_branch_a

def axial_rope_angles(T):
    rows = T // GRID_W
    r = jnp.repeat(jnp.arange(rows, dtype=jnp.float32), GRID_W)
    c = jnp.tile(jnp.arange(GRID_W, dtype=jnp.float32), rows)
    nf = ROPE_AXIS_DIM // 2
    inv = ROPE_THETA ** (-jnp.arange(nf, dtype=jnp.float32) / nf)
    return r[:, None] * inv, c[:, None] * inv

def rotate(xs, ang):
    half = xs.shape[-1] // 2
    cos = jnp.cos(ang)[None, :, None, :]
    sin = jnp.sin(ang)[None, :, None, :]
    x1, x2 = xs[..., :half], xs[..., half:]
    return jnp.concatenate([x1 * cos - x2 * sin, x2 * cos + x1 * sin], axis=-1)

def apply_axial_rope(x, ang_r, ang_c):
    xf = x.astype(jnp.float32)
    out = jnp.concatenate([rotate(xf[..., :ROPE_AXIS_DIM], ang_r),
                           rotate(xf[..., ROPE_AXIS_DIM:], ang_c)], axis=-1)
    return out.astype(x.dtype)

def block_attention(q, k, v):
    B, T, _, dh = q.shape
    nb = T // Q_BLOCK
    qb = jnp.moveaxis(q.reshape(B, nb, Q_BLOCK, ATT_KV_HEADS, ATT_GROUP, dh), 1, 0)
    scale = ATT_HEAD_DIM ** -0.5

    def one(qblk):
        s = jnp.einsum('bqkgd,bskd->bkgqs', qblk, k).astype(jnp.float32) * scale
        p = jax.nn.softmax(s, axis=-1)
        return jnp.einsum('bkgqs,bskd->bqkgd', p.astype(v.dtype), v)

    o = lax.map(one, qb)
    return jnp.moveaxis(o, 0, 1).reshape(B, T, ATT_Q_DIM)

def attn_branch(qb, kb, vb, zb, q_norm_g, k_norm_g, w_branch_b):
    B, T, _ = qb.shape
    q = rmsnorm(qb.reshape(B, T, ATT_Q_HEADS, ATT_HEAD_DIM), q_norm_g)
    k = rmsnorm(kb.reshape(B, T, ATT_KV_HEADS, ATT_HEAD_DIM), k_norm_g)
    v = vb.reshape(B, T, ATT_KV_HEADS, ATT_HEAD_DIM)
    ang_r, ang_c = axial_rope_angles(T)
    q = apply_axial_rope(q, ang_r, ang_c)
    k = apply_axial_rope(k, ang_r, ang_c)
    o = block_attention(q, k, v)
    return (o * jax.nn.silu(zb)) @ w_branch_b

def layer(x, norm_g, w_in, w_gate_f, b_gate_f, w_gate_b, b_gate_b, gla_norm_g,
          q_norm_g, k_norm_g, w_branch_a, w_branch_b, w_out):
    h = rmsnorm(x, norm_g)
    proj = h @ w_in
    qa, ka, va, gfl, gbl, za, qb, kb, vb, zb, ma, mb = jnp.split(proj, split_points(), axis=-1)
    ya = gla_branch(qa, ka, va, gfl, gbl, za, w_gate_f, b_gate_f, w_gate_b, b_gate_b,
                    gla_norm_g, w_branch_a)
    yb = attn_branch(qb, kb, vb, zb, q_norm_g, k_norm_g, w_branch_b)
    merged = jax.nn.sigmoid(ma) * ya + jax.nn.sigmoid(mb) * yb
    return x + merged @ w_out

def trunk(x, norm_g, w_in, w_gate_f, b_gate_f, w_gate_b, b_gate_b, gla_norm_g,
          q_norm_g, k_norm_g, w_branch_a, w_branch_b, w_out, final_norm_g):
    for l in range(DEPTH):
        x = layer(x, norm_g[l], w_in[l], w_gate_f[l], b_gate_f[l], w_gate_b[l], b_gate_b[l],
                  gla_norm_g[l], q_norm_g[l], k_norm_g[l], w_branch_a[l], w_branch_b[l], w_out[l])
    return rmsnorm(x, final_norm_g)

def setup_inputs(seed: int = 0) -> dict:
    key = jax.random.key(seed)
    ks = jax.random.split(key, 16)
    f32 = jnp.float32
    nrm = lambda k, shape, s: jax.random.normal(k, shape, f32) * s
    return {
        'x_prompt': nrm(ks[0], (BATCH, SEQ, D_MODEL), 1.0),
        'x_sample': nrm(ks[1], (DEC_BATCH, DEC_SEQ, D_MODEL), 1.0),
        'norm_g': 1.0 + nrm(ks[2], (DEPTH, D_MODEL), 0.02),
        'w_in': nrm(ks[3], (DEPTH, D_MODEL, IN_DIM), D_MODEL ** -0.5),
        'w_gate_f': nrm(ks[4], (DEPTH, GATE_RANK, GLA_KEY_DIM), GATE_RANK ** -0.5),
        'b_gate_f': nrm(ks[5], (DEPTH, GLA_KEY_DIM), 0.1),
        'w_gate_b': nrm(ks[6], (DEPTH, GATE_RANK, GLA_KEY_DIM), GATE_RANK ** -0.5),
        'b_gate_b': nrm(ks[7], (DEPTH, GLA_KEY_DIM), 0.1),
        'gla_norm_g': 1.0 + nrm(ks[8], (DEPTH, GLA_DV), 0.02),
        'q_norm_g': 1.0 + nrm(ks[9], (DEPTH, ATT_HEAD_DIM), 0.02),
        'k_norm_g': 1.0 + nrm(ks[10], (DEPTH, ATT_HEAD_DIM), 0.02),
        'w_branch_a': nrm(ks[11], (DEPTH, GLA_VALUE_DIM, D_MODEL), GLA_VALUE_DIM ** -0.5),
        'w_branch_b': nrm(ks[12], (DEPTH, ATT_Q_DIM, D_MODEL), ATT_Q_DIM ** -0.5),
        'w_out': nrm(ks[13], (DEPTH, D_MODEL, D_MODEL), D_MODEL ** -0.5),
        'final_norm_g': 1.0 + nrm(ks[14], (D_MODEL,), 0.02),
    }

def reference(x_prompt, x_sample, norm_g, w_in, w_gate_f, b_gate_f, w_gate_b, b_gate_b,
              gla_norm_g, q_norm_g, k_norm_g, w_branch_a, w_branch_b, w_out, final_norm_g):
    y_prompt = trunk(x_prompt, norm_g, w_in, w_gate_f, b_gate_f, w_gate_b, b_gate_b, gla_norm_g,
                     q_norm_g, k_norm_g, w_branch_a, w_branch_b, w_out, final_norm_g)
    y_sample = trunk(x_sample, norm_g, w_in, w_gate_f, b_gate_f, w_gate_b, b_gate_b, gla_norm_g,
                     q_norm_g, k_norm_g, w_branch_a, w_branch_b, w_out, final_norm_g)
    return (y_prompt, y_sample)


_drawn_inputs = setup_inputs


def setup_inputs(seed=0):
    import zlib

    import numpy as np

    out = dict(_drawn_inputs(seed))
    spreads = {}
    factors = {'norm_g': 2.878,
     'b_gate_f': 3.768,
     'b_gate_b': 4.066,
     'gla_norm_g': 6.425,
     'q_norm_g': 8.0,
     'k_norm_g': 8.0,
     'final_norm_g': 2.877}
    for name, (base, spread) in spreads.items():
        noise = np.random.default_rng([zlib.crc32(name.encode()), seed]).standard_normal(out[name].shape)
        drawn = base * np.exp(spread * noise) if base else spread * noise
        out[name] = __import__('jax').numpy.asarray(drawn.astype(out[name].dtype))
    for name, factor in factors.items():
        out[name] = (out[name] * factor).astype(out[name].dtype)
    return out
```

```python
from contextlib import contextmanager

import numpy as np

import concourse.bass as bass
from concourse import mybir

F32 = mybir.dt.float32
F32R = mybir.dt.float32r
U8 = mybir.dt.uint8
ALU = mybir.AluOpType
ACT = mybir.ActivationFunctionType
AX = mybir.AxisListType

P = 128
D = 1024
KT = D // P
SEQS = (512, 256)
TOK = sum(SEQS)
NT = TOK // P
NTP = SEQS[0] // P
DEPTH = 2
EPS = 1e-6
HALF = 512
FH = TOK // 2
GH, GK, GV = 4, 128, 256
RANK = 16
GATE_NORM = 16.0
LEVELS = (1, 2, 4, 8, 16, 32, 64, 128, 256)
NMASK = 7
AH, KVH, DH = 16, 4, 64
GROUP = AH // KVH
GRID_W, ROPE_THETA = 64, 10000.0
UNITS = NTP + 1
C_QKV, C_GATES, C_ZA, C_QB, C_ZB, C_MA, C_MB = 0, 2048, 2080, 3104, 4640, 5664, 6688
RING = 4
SKEW = 3
BGW = 256
BG_BANK = 5
J_Q, J_K, J_V, J_ZB, J_ZA, J_MA, J_MB, NBG = 0, 4, 5, 6, 10, 10, 14, 18
BG_STEPS = (1, 2, 3, 5, 6, 7, 10, 11, 12, 13, 15, 16, 17, 18)

BASE = 16512
R_X = BASE
R_ACT = R_X + NT * D * 4
R_W = R_ACT + 2 * KT * TOK * 4
R_V = R_W + 3 * RING * HALF * 4
R_M = R_V + NT * D * 4
R_O = R_M + NT * D * 4
R_G = R_O + 2 * KT * TOK * 4
R_S = R_G + NT * HALF * 4
ROW = TOK * 4


PER_TURN = {
    "sync gla projections": {
        "w_lo_done": 8},
    "sync gla background": {
        "w_lo_done": 16},
    "sync rope background": {
        "w_lo_done": 8},
    "sync attention background": {
        "w_lo_done": 16},
    "sync gla branch": {
        "w_lo_done": 8},
    "sync attention branch": {
        "w_lo_done": 8},
    "sync output": {
        "w_lo_done": 8},
    "sync layer": {
        "w_lo_done": 264},
    "tensor gla qk": {
        "w_lo_done": 8, "drained": 8},
    "tensor gla v": {
        "w_lo_done": 8, "drained": 6},
    "tensor gla head": {
        "act_phase": 1, "dve_phase": 1, "pool_phase": 1, "w_lo_done": 16, "bg_free": 2, "gla_fix": 1,
        "prod_free": 10, "q_ready": 9, "k_ready": 9, "a_ready": 1},
    "tensor rope background": {
        "w_lo_done": 8, "bg_free": 1},
    "tensor attention group": {
        "act_phase": 1, "dve_phase": 1, "pool_phase": 1, "w_lo_done": 16, "bg_free": 2, "k_staged": 2,
        "q_staged": 4, "q_stack": 8, "k_stack": 2, "exp_done": 20, "pr_t_even": 10, "o_drained": 4, "pr_t_odd":
        10},
    "tensor gla branch": {
        "w_lo_done": 8, "drained": 6},
    "tensor attention branch": {
        "w_lo_done": 8, "drained": 6},
    "tensor output": {
        "w_lo_done": 8, "drained": 6},
    "tensor layer": {
        "hn_ready": 6, "turn_free": 48, "act_phase": 17, "dve_phase": 17, "pool_phase": 17, "w_lo_done": 264,
        "drained": 66, "bg_free": 22, "gla_fix": 4, "prod_free": 40, "q_ready": 36, "k_ready": 36, "a_ready": 4,
        "k_staged": 8, "q_staged": 16, "q_stack": 32, "k_stack": 8, "exp_done": 80, "pr_t_even": 40,
        "o_drained": 16, "pr_t_odd": 40},
    "scalar gla projections": {
        "w_used": 8, "w_slot0": 32, "w_slot1": 32, "w_slot2": 32, "w_slot3": 32},
    "scalar gla head": {
        "w_used": 16, "w_slot0": 64, "w_slot1": 64, "w_slot2": 64, "act_chain": 1, "pe_phase": 1, "dve_phase":
        1, "pool_phase": 1, "w_slot3": 64, "gla_fix": 1, "gate_ready": 1, "gate_abs": 2, "lev_diff": 9,
        "stored": 32, "bg_free": 2, "gla_o": 1},
    "scalar attention group": {
        "w_used": 16, "w_slot0": 64, "w_slot1": 64, "w_slot2": 64, "pe_phase": 1, "dve_phase": 1, "pool_phase":
        1, "w_slot3": 64, "stored": 32, "bg_free": 2, "neg_max": 20, "pr_turned": 20, "pv_done": 20},
    "scalar gla branch": {
        "w_used": 8, "w_slot0": 32, "w_slot1": 32, "w_slot2": 32, "w_slot3": 32},
    "scalar attention branch": {
        "w_used": 8, "w_slot0": 32, "w_slot1": 32, "w_slot2": 32, "w_slot3": 32},
    "scalar layer": {
        "w_used": 264, "w_slot0": 1056, "w_slot1": 1056, "w_slot2": 1056, "stat_v": 3, "act_chain": 7, "turned":
        48, "pe_phase": 17, "dve_phase": 17, "pool_phase": 17, "w_slot3": 1056, "gemm_ready": 66, "drained": 66,
        "gla_fix": 4, "gate_ready": 4, "gate_abs": 8, "lev_diff": 36, "stored": 288, "bg_free": 22, "gla_o": 4,
        "qkv_in": 96, "sq_used": 18, "sil_used": 4, "neg_max": 80, "pr_turned": 80, "pv_done": 80, "gates_in":
        192},
    "gpsimd gla projections": {
        "w_hi_done": 8},
    "gpsimd gla head": {
        "w_hi_done": 16, "pe_phase": 1, "act_phase": 1, "dve_phase": 1, "lev_exp": 9, "prod": 10},
    "gpsimd attention group": {
        "w_hi_done": 16, "pe_phase": 1, "act_phase": 1, "dve_phase": 1, "k_staged": 2, "pool_chain": 4,
        "q_turned": 8},
    "gpsimd gla branch": {
        "w_hi_done": 8},
    "gpsimd attention branch": {
        "w_hi_done": 8},
    "gpsimd layer": {
        "w_hi_done": 264, "pe_phase": 17, "act_phase": 17, "dve_phase": 17, "lev_exp": 36, "prod": 40, "tables":
        1, "qkv_in": 96, "rot2_free": 18, "k_staged": 8, "pool_chain": 16, "q_turned": 32},
    "vector gla qk": {
        "gemm_ready": 8},
    "vector gla v": {
        "gemm_ready": 6},
    "vector gla head": {
        "stat_sum": 1, "dve_chain": 2, "pe_phase": 1, "act_phase": 1, "pool_phase": 1, "gla_fix": 1,
        "gate_ready": 1, "gate_abs": 2, "gate_log": 1, "lev_exp": 9, "prod": 10, "prod_free": 10, "k_ready": 9},
    "vector attention group": {
        "dve_chain": 24, "pe_phase": 1, "act_phase": 1, "pool_phase": 1, "k_turned": 2, "q_turned": 8, "score":
        20, "pr_turned": 20, "pv_done": 20},
    "vector gla branch": {
        "gemm_ready": 6, "zb_ready": 2, "sig_ready": 2},
    "vector attention branch": {
        "dve_chain": 6, "gemm_ready": 6, "sig_ready": 2},
    "vector output": {
        "gemm_ready": 6},
    "vector layer": {
        "stat_sum": 5, "stat_y0": 3, "dve_chain": 166, "param": 256, "turn_hi": 48, "pe_phase": 17, "act_phase":
        17, "pool_phase": 17, "gemm_ready": 66, "gla_fix": 4, "gate_ready": 4, "gate_abs": 8, "gate_log": 4,
        "lev_exp": 36, "prod": 40, "prod_free": 40, "k_ready": 36, "tables": 1, "sq_ready": 18, "rot2_ready":
        18, "rot2_free": 18, "sil_ready": 4, "k_turned": 8, "q_turned": 32, "score": 80, "pr_turned": 80,
        "pv_done": 80, "zb_ready": 4, "sig_ready": 8},
}

WRONG = {}


class Counts:

    def __init__(self, who, eng, **start):
        self.who, self.eng, self.start = who, eng, start
        self.base, self.n = {}, {}

    def __call__(self, name, by=1):
        self.skip(name, by)
        return self.base[name] + self.n[name]

    def skip(self, name, by):
        self.base.setdefault(name, self.start.get(name, 0))
        self.n[name] = self.n.get(name, 0) + by

    def peek(self, name, more):
        self.skip(name, 0)
        return self.base[name] + (self.n[name] + more)

    @contextmanager
    def repeat(self, times, loop):
        per = PER_TURN.get(f"{self.who} {loop}", {})
        with self.eng.Fori(0, times) as i:
            for name in per:
                self.skip(name, 0)
            base, n = dict(self.base), dict(self.n)
            for name, by in per.items():
                self.base[name] = base[name] + n[name] + i * by
                self.n[name] = 0
            yield i
            found = {}
            for name in self.n:
                by = self.n[name] - (0 if name in per else n.get(name, 0))
                if by:
                    found[name] = by
            if found != per:
                WRONG[f"{self.who} {loop}"] = found
        for name in self.n:
            self.base[name] = base.get(name, self.start.get(name, 0))
            self.n[name] = n.get(name, 0) + times * found.get(name, 0)


class Semaphores:

    def __init__(self, nc):
        sem = nc.alloc_semaphore
        self.pe_phase = sem("pe_phase")
        self.act_phase = sem("act_phase")
        self.dve_phase = sem("dve_phase")
        self.pool_phase = sem("pool_phase")
        self.passed = sem("passed")
        self.w_hi_done = sem("w_hi_done")
        self.w_lo_done = sem("w_lo_done")
        self.w_used = sem("w_used")
        self.gemm_ready = sem("gemm_ready")
        self.drained = sem("drained")
        self.bg_free = sem("bg_free")
        self.stored = sem("stored")
        self.sil_ready = sem("sil_ready")
        self.sil_used = sem("sil_used")
        self.qkv_in = sem("qkv_in")
        self.gates_in = sem("gates_in")
        self.x_in = sem("x_in")
        self.param = sem("param")
        self.y_ready = sem("y_ready")
        self.out_done = sem("out_done")
        self.act_chain = sem("act_chain")
        self.dve_chain = sem("dve_chain")
        self.pool_chain = sem("pool_chain")
        self.stat_sum = sem("stat_sum")
        self.stat_v = sem("stat_v")
        self.stat_y0 = sem("stat_y0")
        self.hn_ready = sem("hn_ready")
        self.turned = sem("turned")
        self.turn_hi = sem("turn_hi")
        self.turn_free = sem("turn_free")
        self.gla_fix = sem("gla_fix")
        self.gate_ready = sem("gate_ready")
        self.gate_abs = sem("gate_abs")
        self.gate_log = sem("gate_log")
        self.lev_diff = sem("lev_diff")
        self.lev_exp = sem("lev_exp")
        self.q_ready = sem("q_ready")
        self.k_ready = sem("k_ready")
        self.prod = sem("prod")
        self.prod_free = sem("prod_free")
        self.a_ready = sem("a_ready")
        self.gla_o = sem("gla_o")
        self.zb_ready = sem("zb_ready")
        self.sig_ready = sem("sig_ready")
        self.sq_ready = sem("sq_ready")
        self.sq_used = sem("sq_used")
        self.tables = sem("tables")
        self.rot2_ready = sem("rot2_ready")
        self.rot2_free = sem("rot2_free")
        self.k_staged = sem("k_staged")
        self.k_turned = sem("k_turned")
        self.k_stack = sem("k_stack")
        self.q_staged = sem("q_staged")
        self.q_turned = sem("q_turned")
        self.q_stack = sem("q_stack")
        self.score = sem("score")
        self.neg_max = sem("neg_max")
        self.exp_done = sem("exp_done")
        self.pr_turned = sem("pr_turned")
        self.pr_t_even = sem("pr_t_even")
        self.pr_t_odd = sem("pr_t_odd")
        self.pv_done = sem("pv_done")
        self.o_drained = sem("o_drained")
        self.w_slot = [sem(f"w_slot{i}") for i in range(RING)]


def trunk(nc, x_prompt, x_sample, norm_g, w_in, w_gate_f, b_gate_f, w_gate_b, b_gate_b, gla_norm_g,
          q_norm_g, k_norm_g, w_branch_a, w_branch_b, w_out, final_norm_g,
          identity, masks, rope_cos, rope_sin, y_prompt, y_sample):
    def sb(name, shape, offset, dtype=F32):
        return nc.alloc_sbuf_tensor_at(name, shape, dtype, offset=offset)

    def view(t, start, *dims):
        row = 1
        for n in t.shape[1:]:
            row *= n
        return bass.AP(t, start, [[row, P]] + [list(d) for d in dims])

    def rows_of(a, start, n):
        return bass.AP(a.tensor, start, [[0, P], [1, n]])

    x = sb("x", [P, NT, D], R_X)
    act_hi = sb("act_hi", [P, KT, TOK], R_ACT, F32R)
    act_lo = sb("act_lo", [P, KT, TOK], R_ACT + KT * ROW, F32R)
    w_raw = sb("w_raw", [P, RING, HALF], R_W)
    w_hi = sb("w_hi", [P, RING, HALF], R_W + RING * HALF * 4, F32R)
    w_lo = sb("w_lo", [P, RING, HALF], R_W + 2 * RING * HALF * 4, F32R)
    va = sb("va", [P, NT, D], R_V)
    qk_t = sb("qk_t", [P, GH, 2, TOK], R_M)
    q = sb("q", [P, NT, D], R_M)
    ma = sb("ma", [P, NT, D], R_ACT)
    zb = sb("zb", [P, NT, D], R_ACT + NT * D * 4)
    mb = sb("mb", [P, NT, D], R_M)
    merged = sb("merged", [P, NT, D], R_V)
    stg = sb("stg", [P, NT, BGW], R_G)
    proj = nc.dram_tensor("proj", [P, NBG, NT, BGW], F32, kind="Internal")
    o_hi = sb("o_hi", [P, KT, TOK], R_O, F32R)
    o_lo = sb("o_lo", [P, KT, TOK], R_O + KT * ROW, F32R)
    g_row = sb("g_row", [P, D], R_O)
    hn = sb("hn", [P, 2, D], R_O + D * 4)
    y_out = sb("y_out", [P, NT, D], R_O + 4 * D * 4)
    mask_raw = sb("mask_raw", [P, NMASK, P], R_V)
    ce = sb("ce", [P, 2, TOK], R_O)
    lev = sb("lev", [P, 2, 2, TOK], R_O + 2 * ROW)
    qk = sb("qk", [P, 2, 2, TOK], R_O + 6 * ROW)
    gl_t = sb("gl_t", [2 * RANK, TOK], R_O + 10 * ROW)
    amat = sb("amat", [P, NT, P], R_O + 11 * ROW)
    aoff1 = sb("aoff1", [P, NT, P], R_O + 12 * ROW)
    aoff2 = sb("aoff2", [P, NTP, 2, P], R_O + 13 * ROW)
    junk_gla = sb("junk_gla", [P, NT, GV], R_O + 2 * ROW)
    wg_fix = sb("wg_fix", [2 * RANK, 2, GK], R_G + NT * BGW * 4)
    wg = sb("wg", [2 * RANK, 2, GH * GK], R_G + NT * BGW * 4 + 2 * GK * 4)
    kv = sb("kv", [P, NT, 2, KVH, DH], R_O)
    k_hh = sb("k_hh", [P, TOK], R_O + 4 * ROW, F32R)
    k_ll = sb("k_ll", [P, TOK], R_O + 5 * ROW, F32R)
    q_hl = sb("q_hl", [P, 2, TOK], R_O + 6 * ROW, F32R)
    q_st = sb("q_st", [P, 2, NT, 2, DH], R_O + 8 * ROW, F32R)
    k_st = sb("k_st", [P, 2, NT, 2, DH], R_O + 10 * ROW, F32R)
    v_grp = sb("v_grp", [P, NT, DH], R_O + 12 * ROW)
    pr = sb("pr", [P, 2, HALF], R_O + 12 * ROW + NT * DH * 4)
    pr_t = sb("pr_t", [P, 2, HALF], R_O + 12 * ROW + NT * DH * 4 + 2 * HALF * 4)
    R_T = R_O + 4 * ROW
    cs = sb("cs", [P, 2, 2, NT, DH], R_T)
    cs_raw = sb("cs_raw", [P, 2, NT, DH], R_T + 4 * NT * DH * 4)
    rot1 = sb("rot1", [P, HALF], R_T + 6 * NT * DH * 4)
    rot2 = sb("rot2", [P, HALF], R_T + 6 * NT * DH * 4 + HALF * 4)
    sq = sb("sq", [P, 2, HALF], R_T + 6 * NT * DH * 4 + 2 * HALF * 4)
    g_qk = sb("g_qk", [P, 2, DH], R_T + 6 * NT * DH * 4 + 4 * HALF * 4)
    gv_row = sb("gv_row", [P, GV], R_T + 6 * NT * DH * 4 + 4 * HALF * 4 + 2 * DH * 4)
    NSTAT = NT * (AH + KVH)
    ident = sb("ident", [P, P], R_S)
    mask = sb("mask", [P, NMASK, P], R_S + P * 4, U8)
    st = sb("st", [P, 5, NSTAT], R_S + P * 4 + NMASK * P)
    bg = sb("bg", [P, 2, GH], R_S + P * 4 + NMASK * P + 5 * NSTAT * 4)
    bg_fix = sb("bg_fix", [P, 2], R_S + P * 4 + NMASK * P + 5 * NSTAT * 4 + 32)
    ps = nc.alloc_psum_tensor("ps", [P, 8 * HALF], F32)

    def bank(b, n=HALF):
        return ps[:, b * HALF:b * HALF + n]

    def view_ps(start, *dims):
        return bass.AP(ps, start, [[8 * HALF, P]] + [list(d) for d in dims])

    def nmax(n, i):
        return st[:, 0, 2 * (n % 2) + i:2 * (n % 2) + i + 1]

    def den(h, t):
        return st[:, 1, h % 2 * NT + t:h % 2 * NT + t + 1]

    s = Semaphores(nc)

    def phase_end(eng, at, own):
        eng.drain().then_inc(own, 1)
        if own is not s.pe_phase:
            eng.wait_ge(s.pe_phase, at("pe_phase"))
        if own is not s.act_phase:
            eng.wait_ge(s.act_phase, at("act_phase"))
        if own is not s.dve_phase:
            eng.wait_ge(s.dve_phase, at("dve_phase"))
        if own is not s.pool_phase:
            eng.wait_ge(s.pool_phase, at("pool_phase"))
        eng.sem_inc(s.passed, 1)

    with nc.Block() as block:

        @block.sync
        def _(sp):
            at = Counts("sync", sp)
            sp.dma_start(x[:, 0:NTP, :], x_prompt.rearrange("b (t p) d -> p (b t) d", p=P)).then_inc(s.x_in, 16)
            sp.dma_start(x[:, NTP:NT, :], x_sample.rearrange("b (t p) d -> p (b t) d", p=P)).then_inc(s.x_in, 16)
            sp.dma_start(ident[:], identity).then_inc(s.x_in, 16)
            sp.dma_start(mask_raw[:], masks).then_inc(s.x_in, 16)

            def load_group(w, layer, col, width=HALF, blocks=KT):
                ld = w.shape[2]
                for k in range(blocks):
                    sp.wait_ge(s.w_lo_done, at("w_lo_done"))
                    src = bass.AP(w.tensor, layer * (D * ld) + col + k * P * ld, [[ld, P], [1, width]])
                    sp.dma_start(w_raw[:, k % RING, 0:width], src).then_inc(s.w_slot[k % RING], 16)

            with at.repeat(DEPTH, "layer") as layer:
                load_group(w_in, layer, C_GATES, P)
                with at.repeat(4, "gla projections") as g:
                    load_group(w_in, layer, g * HALF + C_QKV)
                with at.repeat(GH, "gla background") as h:
                    for i in range(2):
                        load_group(w_in, layer, h * (2 * BGW) + C_QB + i * BGW, BGW)
                for i in range(2):
                    load_group(w_in, layer, C_ZB + (2 + i) * BGW, BGW)
                with at.repeat(4, "rope background") as i:
                    load_group(w_in, layer, i * BGW + C_ZA, BGW)
                with at.repeat(KVH, "attention background") as g:
                    for i in range(2):
                        load_group(w_in, layer, g * (2 * BGW) + C_MA + i * BGW, BGW)
                for w, name in ((w_branch_a, "gla branch"), (w_branch_b, "attention branch"), (w_out, "output")):
                    with at.repeat(2, name) as g:
                        load_group(w, layer, g * HALF)
            load_group(w_in, 0, C_GATES, P, blocks=SKEW)
            sp.wait_ge(s.y_ready, at("y_ready", NT))
            sp.dma_start(y_prompt.rearrange("b (t p) d -> p (b t) d", p=P), y_out[:, 0:NTP, :]).then_inc(s.out_done, 16)
            sp.dma_start(y_sample.rearrange("b (t p) d -> p (b t) d", p=P), y_out[:, NTP:NT, :]).then_inc(s.out_done, 16)
            sp.wait_ge(s.out_done, 32)

        @block.tensor
        def _(pe):
            at = Counts("tensor", pe, w_lo_done=RING, drained=8)
            mm = nc.tensor.matmul

            def three_passes(out, s_hi, s_lo, m_hi, m_lo, first, last):
                mm(out, s_hi, m_hi, start=first, stop=False)
                mm(out, s_hi, m_lo, start=False, stop=False)
                return mm(out, s_lo, m_hi, start=False, stop=last)

            def gemm_tokens(a_hi, a_lo):
                for k in range(KT):
                    pe.wait_ge(s.w_lo_done, at("w_lo_done"))
                    for t in range(NT):
                        if k == 0:
                            pe.wait_ge(s.drained, at.peek("drained", t + 1 - NT))
                        tok = slice(t * P, (t + 1) * P)
                        last = three_passes(bank(t), a_hi[:, k, tok], a_lo[:, k, tok], w_hi[:, k % RING, :],
                                            w_lo[:, k % RING, :], k == 0, k == KT - 1)
                        if k == KT - 1:
                            last.then_inc(s.gemm_ready, 1)
                    (last if k < KT - 1 else pe.drain()).then_inc(s.w_used, 1)
                at.skip("drained", NT)

            def background(i):
                k = i % KT
                pe.wait_ge(s.w_lo_done, at("w_lo_done"))
                if k == 0:
                    pe.wait_ge(s.bg_free, at("bg_free"))
                for t in range(NT):
                    out = ps[:, BG_BANK * HALF + t * BGW:BG_BANK * HALF + (t + 1) * BGW]
                    tok = slice(t * P, (t + 1) * P)
                    mm(out, act_hi[:, k, tok], w_hi[:, k % RING, 0:BGW], start=(k == 0 and t % 2 == 0), stop=False, skip_group_check=True)
                    mm(out, act_hi[:, k, tok], w_lo[:, k % RING, 0:BGW], start=False, stop=False, skip_group_check=True)
                    last = mm(out, act_lo[:, k, tok], w_hi[:, k % RING, 0:BGW], start=False, stop=(k == KT - 1), skip_group_check=True)
                last.then_inc(s.w_used, 1)

            def gemm_features(blocks):
                for k in range(KT):
                    pe.wait_ge(s.w_lo_done, at("w_lo_done"))
                    for b in range(8 - 2 * blocks, 8):
                        if k == 0:
                            pe.wait_ge(s.drained, at.peek("drained", b + 1 - 8))
                        col = slice((b // 2 + blocks - 4) * P, (b // 2 + blocks - 3) * P)
                        tok = slice(b % 2 * FH, (b % 2 + 1) * FH)
                        last = three_passes(bank(b, FH), w_hi[:, k % RING, col], w_lo[:, k % RING, col],
                                            act_hi[:, k, tok], act_lo[:, k, tok], k == 0, k == KT - 1)
                        if k == KT - 1:
                            last.then_inc(s.gemm_ready, 1)
                    (last if k < KT - 1 else pe.drain()).then_inc(s.w_used, 1)
                at.skip("drained", 2 * blocks)

            def turn(src, scaled=False):
                for n in range(2 * NT):
                    t = n // 2
                    if scaled and n % 2 == 0:
                        pe.wait_ge(s.hn_ready, at("hn_ready"))
                    pe.wait_ge(s.turn_free, at("turn_free"))
                    for j in range(4):
                        k = n % 2 * 4 + j
                        last = nc.tensor.transpose(ps[:, n % 4 * HALF + j * P:n % 4 * HALF + (j + 1) * P],
                                                   src(t)[:, k * P:(k + 1) * P], ident[:])
                    last.then_inc(s.turned, 1)

            def gla_head(h):
                background(0)
                pe.wait_ge(s.gla_fix, at("gla_fix"))
                for b in range(4):
                    last = mm(bank(b, FH), wg_fix[:, b // 2, :], gl_t[:, b % 2 * FH:(b % 2 + 1) * FH], start=True, stop=True)
                last.then_inc(s.gate_ready, 1)
                for i in (1, 2, 3):
                    background(i)
                for n in range(len(LEVELS) + 1):
                    pe.wait_ge(s.prod_free, at("prod_free"))
                    li = max(n - 1, 0)
                    if n != 1:
                        pe.wait_ge(s.q_ready, at("q_ready"))
                        pe.wait_ge(s.k_ready, at("k_ready"))
                    kk = view(qk, (li % 2) * 2 * TOK + TOK, (1, TOK))
                    qq = view(qk, (li % 2) * 2 * TOK, (1, TOK))
                    span = LEVELS[li]
                    if span == 256:
                        for j in range(NTP):
                            i0 = 2 * P if j < 2 else 0
                            last = mm(ps[:, j * 2 * P:(j + 1) * 2 * P], kk[:, j * P:(j + 1) * P],
                                      qq[:, i0:i0 + 2 * P], start=True, stop=True)
                    else:
                        for j in range(NT):
                            i = j ^ 1 if span == 128 else j
                            rhs = view(qk_t, h * (2 * TOK) + i * P, (1, P)) if n == 0 else qq[:, i * P:(i + 1) * P]
                            last = mm(ps[:, j * P:(j + 1) * P], kk[:, j * P:(j + 1) * P], rhs, start=True, stop=True)
                    last.then_inc(s.prod, 1)
                    background(4 + n)
                background(14)
                pe.wait_ge(s.a_ready, at("a_ready"))
                for i in range(NT):
                    out = ps[:, 2 * HALF + i * GV:2 * HALF + (i + 1) * GV]
                    terms = [(amat[:, i, :], i), (aoff1[:, i ^ 1, :], i ^ 1)]
                    if i < NTP:
                        terms += [(aoff2[:, j, i % 2, :], j) for j in ((2, 3) if i < 2 else (0, 1))]
                    for n, (a, j) in enumerate(terms):
                        last = mm(out, a, view(va, h * GV + j * D, (1, GV)), start=(n == 0), stop=(n == len(terms) - 1))
                last.then_inc(s.gla_o, 1)
                background(15)
                phase_end(pe, at, s.pe_phase)

            def attention_group():
                def turn_stack(stage, col, tiles):
                    for t in tiles:
                        last = nc.tensor.transpose(ps[:, col + (t - tiles[0]) * P:col + (t - tiles[0] + 1) * P],
                                                   stage(t).bitcast(F32), ident[:])
                    return last

                def q_turn_first(h):
                    pe.wait_ge(s.q_staged, at("q_staged"))
                    turn_stack(lambda t: view(q_st, h % 2 * TOK + t * P, (1, P)), 4 * HALF, range(4)).then_inc(s.q_turned, 1)

                def q_turn_second(h):
                    pe.wait_ge(s.q_stack, at("q_stack"))
                    turn_stack(lambda t: view(q_st, h % 2 * TOK + t * P, (1, P)), 4 * HALF, range(4, NT)).then_inc(s.q_turned, 1)

                def scores(n):
                    h, u = divmod(n, UNITS)
                    if u == 0:
                        pe.wait_ge(s.q_stack, at("q_stack"))
                    out = bank(n % 2)
                    if u < NTP:
                        parts = [(out, u, slice(0, SEQS[0]))]
                    else:
                        parts = [(out[:, i * 256:(i + 1) * 256], NTP + i, slice(SEQS[0], TOK)) for i in range(2)]
                    for o, t, keys in parts:
                        lhs = q_hl[:, h % 2, t * P:(t + 1) * P]
                        mm(o, lhs, k_hh[:, keys], start=True, stop=False)
                        last = mm(o, lhs, k_ll[:, keys], start=False, stop=True)
                    last.then_inc(s.score, 1)

                def turn_p(n):
                    pe.wait_ge(s.exp_done, at("exp_done"))
                    for j in range(4):
                        last = nc.tensor.transpose(ps[:, 2 * HALF + j * P:2 * HALF + (j + 1) * P],
                                                   pr[:, n % 2, j * P:(j + 1) * P], ident[:])
                    last.then_inc(s.pr_turned, 1)

                def values(n):
                    h, u = divmod(n, UNITS)
                    if n % 2 == 0:
                        pe.wait_ge(s.pr_t_even, at("pr_t_even"))
                    else:
                        pe.wait_ge(s.pr_t_odd, at("pr_t_odd"))
                    if u == 0:
                        pe.wait_ge(s.o_drained, at("o_drained"))
                    for i in range(1 if u < NTP else 2):
                        t = u + i
                        nk = 4 if u < NTP else 2
                        for j in range(nk):
                            key = j if u < NTP else NTP + j
                            last = mm(ps[:, 3 * HALF + t * DH:3 * HALF + (t + 1) * DH],
                                      pr_t[:, n % 2, (i * 2 + j) * P:(i * 2 + j + 1) * P], v_grp[:, key, :],
                                      start=(j == 0), stop=(j == nk - 1))
                    last.then_inc(s.pv_done, 1)

                background(0)
                background(1)
                for part in range(2):
                    pe.wait_ge(s.k_staged, at("k_staged"))
                    turn_stack(lambda t: view(k_st, part * TOK + t * P, (1, P)), part * 2 * HALF, range(NT)).then_inc(s.k_turned, 1)
                q_turn_first(0)
                q_turn_second(0)
                pe.wait_ge(s.k_stack, at("k_stack", 2))
                total = GROUP * UNITS
                scores(0)
                for n in range(total):
                    h = n // UNITS + 1
                    if n % UNITS == 1 and h < GROUP:
                        q_turn_first(h)
                    if n % UNITS == 2 and h < GROUP:
                        q_turn_second(h)
                    if n + 1 < total:
                        scores(n + 1)
                    turn_p(n)
                    if n in BG_STEPS:
                        background(2 + BG_STEPS.index(n))
                    values(n)
                phase_end(pe, at, s.pe_phase)

            pe.sem_inc(s.w_used, RING)
            pe.wait_ge(s.x_in, at("x_in", 64))
            with at.repeat(DEPTH, "layer"):
                turn(lambda t: hn[:, t % 2, :], scaled=True)
                phase_end(pe, at, s.pe_phase)
                gemm_features(1)
                with at.repeat(2, "gla qk"):
                    gemm_features(4)
                with at.repeat(2, "gla v"):
                    gemm_tokens(act_hi, act_lo)
                phase_end(pe, at, s.pe_phase)
                with at.repeat(GH, "gla head") as h:
                    gla_head(h)
                with at.repeat(6, "rope background"):
                    for k in range(KT):
                        background(k)
                phase_end(pe, at, s.pe_phase)
                with at.repeat(KVH, "attention group"):
                    attention_group()
                turn(lambda t: va[:, t, :])
                phase_end(pe, at, s.pe_phase)
                with at.repeat(2, "gla branch"):
                    gemm_tokens(o_hi, o_lo)
                phase_end(pe, at, s.pe_phase)
                turn(lambda t: q[:, t, :])
                phase_end(pe, at, s.pe_phase)
                with at.repeat(2, "attention branch"):
                    gemm_tokens(act_hi, act_lo)
                phase_end(pe, at, s.pe_phase)
                turn(lambda t: merged[:, t, :])
                phase_end(pe, at, s.pe_phase)
                with at.repeat(2, "output"):
                    gemm_tokens(o_hi, o_lo)
                phase_end(pe, at, s.pe_phase)

        @block.scalar
        def _(act):
            at = Counts("scalar", act, drained=8, bg_free=1)
            act.sem_inc(s.bg_free, 1)
            act.sem_inc(s.stored, 16)
            A = nc.scalar.activation

            def split(k, width=HALF):
                slot = (k + SKEW) % RING
                act.wait_ge(s.w_slot[slot], at(f"w_slot{slot}", 16))
                act.wait_ge(s.w_used, at("w_used"))
                A(w_hi[:, slot, 0:width], w_raw[:, slot, 0:width], ACT.Copy).then_inc(s.w_hi_done, 1)

            def store(j):
                act.wait_ge(s.w_used, at.peek("w_used", 1))
                act.wait_ge(s.stored, at("stored", 16))
                A(stg[:].rearrange("p a b -> p (a b)"), bg_sums, ACT.Copy).then_inc(s.bg_free, 1)
                act.wait_ge(s.bg_free, at("bg_free"))
                act.dma_start(bass.AP(proj, j * (NT * BGW), [[NBG * NT * BGW, P], [1, NT * BGW]]),
                              stg[:].rearrange("p a b -> p (a b)")).then_inc(s.stored, 16)

            def all_stored():
                act.wait_ge(s.stored, at.peek("stored", 16))

            def fetch(dst, j, start, row, n, sem):
                for c in range(n):
                    act.dma_start(view(dst, start + c * BGW, (row, NT), (1, BGW)),
                                  bass.AP(proj, (j + c) * (NT * BGW), [[NBG * NT * BGW, P], [BGW, NT], [1, BGW]])).then_inc(sem, 16)

            bg_sums = ps[:, BG_BANK * HALF:BG_BANK * HALF + NT * BGW]

            def param(dst, src):
                act.dma_start(dst, src).then_inc(s.param, 16)

            def rsqrt_seed(n):
                act.wait_ge(s.stat_v, at("stat_v"))
                A(st[:, 2, 0:n], st[:, 1, 0:n], ACT.Ln).then_inc(s.act_chain, 1)
                act.wait_ge(s.act_chain, at("act_chain"))
                A(st[:, 2, 0:n], st[:, 2, 0:n], ACT.Exp, scale=-0.5).then_inc(s.stat_y0, 1)

            def sum_squares():
                for t in range(NT):
                    last = A(y_out[:, t, :], x[:, t, :], ACT.Square, accum_out=st[:, 0, t:t + 1])
                last.then_inc(s.stat_sum, 1)
                rsqrt_seed(NT)

            def turn_hi(dst):
                for n in range(2 * NT):
                    t, k0 = n // 2, n % 2 * 4
                    act.wait_ge(s.turned, at("turned"))
                    A(dst[:, k0:k0 + 4, t * P:(t + 1) * P],
                                      ps[:, n % 4 * HALF:(n % 4 + 1) * HALF].rearrange("p (a b) -> p a b", a=4), ACT.Copy).then_inc(s.turn_hi, 1)

            def skip_banks(n):
                at.skip("gemm_ready", n)
                at.skip("drained", n)

            def splits():
                for k in range(KT):
                    split(k)

            def gla_head(h):
                act.wait_ge(s.gla_fix, at("gla_fix"))
                act.wait_ge(s.gate_ready, at("gate_ready"))
                for d in range(2):
                    A(view(lev, (2 + d) * TOK, (FH, 2), (1, FH)), view_ps(d * 2 * HALF, (HALF, 2), (1, FH)),
                      ACT.Abs, bias=bg_fix[:, d:d + 1]).then_inc(s.gate_abs, 1)
                split(0, BGW)
                act.wait_ge(s.gate_abs, at("gate_abs", 2))
                a = view(lev, 2 * TOK, (1, 2 * TOK))
                A(a, a, ACT.Exp, scale=-1.0).then_inc(s.act_chain, 1)
                split(1, BGW)
                act.wait_ge(s.act_chain, at("act_chain"))
                A(a, a, ACT.Ln, bias=1.0).then_inc(s.gate_log, 1)
                split(2, BGW)
                split(3, BGW)
                for li, span in enumerate(LEVELS):
                    n = TOK if span < 256 else SEQS[0]
                    act.wait_ge(s.lev_diff, at("lev_diff"))
                    y = view(lev, li % 2 * 2 * TOK, (TOK, 2), (1, n))
                    A(y, y, ACT.Exp, scale=1.0 / GATE_NORM).then_inc(s.lev_exp, 1)
                    if li == 4:
                        store(2 * h)
                    split(4 + li, BGW)
                for i in (13, 14, 15):
                    split(i, BGW)
                act.wait_ge(s.gla_o, at("gla_o"))
                for t in range(NT):
                    last = A(junk_gla[:, t, :], ps[:, 2 * HALF + t * GV:2 * HALF + (t + 1) * GV], ACT.Square,
                             scale=GK ** -0.5, accum_out=st[:, 1, t:t + 1])
                last.then_inc(s.stat_sum, 1)
                A(view(va, h * GV, (D, NT), (1, GV)), view_ps(2 * HALF, (GV, NT), (1, GV)), ACT.Copy, scale=GK ** -0.5)
                store(2 * h + 1)
                phase_end(act, at, s.act_phase)

            def attention_group(g):
                def exp_scores(n):
                    h, u = divmod(n, UNITS)
                    act.wait_ge(s.neg_max, at("neg_max"))
                    if n >= 2:
                        act.wait_ge(s.pr_turned, at.peek("pr_turned", 0))
                    for i in range(1 if u < NTP else 2):
                        w = HALF if u < NTP else HALF // 2
                        last = A(pr[:, n % 2, i * w:(i + 1) * w], ps[:, n % 2 * HALF + i * w:n % 2 * HALF + (i + 1) * w],
                                 ACT.Exp, scale=DH ** -0.5, bias=nmax(n, i), accum_out=den(h, u + i))
                    act.drain().then_inc(s.exp_done, 1)

                def copy_pt(n):
                    if n % 2 == 0:
                        act.wait_ge(s.pr_turned, at("pr_turned"))
                        if n >= 2:
                            act.wait_ge(s.pv_done, at.peek("pv_done", -1))
                        A(pr_t[:, 0, :], bank(2), ACT.Copy).then_inc(s.pr_t_even, 1)
                    else:
                        at.skip("pr_turned", 1)
                    at.skip("pv_done", 1)

                split(0, BGW)
                split(1, BGW)
                total = GROUP * UNITS
                exp_scores(0)
                for n in range(total):
                    if n + 1 < total:
                        exp_scores(n + 1)
                    copy_pt(n)
                    if n in BG_STEPS:
                        i = 2 + BG_STEPS.index(n)
                        split(i, BGW if i + SKEW < 2 * KT else HALF)
                    if n in (8, 19):
                        store(g * 2 + J_MA + (n == 19))
                phase_end(act, at, s.act_phase)

            act.wait_ge(s.x_in, 64)
            for k in range(SKEW):
                act.wait_ge(s.w_used, at("w_used"))
                act.wait_ge(s.w_slot[k], at(f"w_slot{k}", 16))
                A(w_hi[:, k, 0:P], w_raw[:, k, 0:P], ACT.Copy).then_inc(s.w_hi_done, 1)
            with at.repeat(DEPTH, "layer") as layer:
                param(g_row[:], rows_of(norm_g, layer * D, D))
                for d, b_gate in enumerate((b_gate_f, b_gate_b)):
                    for h in range(GH):
                        param(bg[:, d, h:h + 1], bass.AP(b_gate.tensor, layer * (GH * GK) + h * GK, [[1, P], [1, 1]]))
                sum_squares()
                turn_hi(act_hi)
                phase_end(act, at, s.act_phase)
                param(wg[0:RANK, 0, :], bass.AP(w_gate_f.tensor, layer * (RANK * GH * GK), [[GH * GK, RANK], [1, GH * GK]]))
                param(wg[RANK:2 * RANK, 1, :], bass.AP(w_gate_b.tensor, layer * (RANK * GH * GK), [[GH * GK, RANK], [1, GH * GK]]))
                for k in range(KT):
                    split(k, P if k + SKEW < KT else HALF)
                with at.repeat(4, "gla projections"):
                    splits()
                skip_banks(2 + 2 * 8 + 2 * NT)
                phase_end(act, at, s.act_phase)
                with at.repeat(GH, "gla head") as h:
                    gla_head(h)
                all_stored()
                fetch(q, J_Q, 0, D, 4, s.qkv_in)
                fetch(kv, J_K, 0, HALF, 2, s.qkv_in)
                param(gv_row[:], rows_of(gla_norm_g, layer * GV, GV))
                param(cs_raw[:, 0, :, :], rope_cos)
                param(cs_raw[:, 1, :, :], rope_sin)
                param(g_qk[:, 0, :], rows_of(q_norm_g, layer * DH, DH))
                param(g_qk[:, 1, :], rows_of(k_norm_g, layer * DH, DH))
                rsqrt_seed(NT * GH)
                for i in range(6 * KT):
                    split(i % KT, BGW)
                    if i == 8:
                        act.wait_ge(s.qkv_in, at("qkv_in", 6 * 16))
                    if 8 <= i < 8 + 3 * NT // 2:
                        for n in (2 * i - 16, 2 * i - 15):
                            t, part = n // 3, n % 3
                            src = view(q, t * D + part * HALF, (1, HALF)) if part < 2 else view(kv, t * HALF, (1, KVH * DH))
                            act.wait_ge(s.sq_used, at("sq_used"))
                            A(view(sq, n % 2 * HALF, (1, HALF if part < 2 else KVH * DH)), src, ACT.Square).then_inc(s.sq_ready, 1)
                    if i == 8 + 3 * NT // 2:
                        rsqrt_seed(NSTAT)
                    if i % KT == KT - 1:
                        if i < 2 * KT:
                            store(J_ZB + 2 + i // KT)
                        else:
                            act.wait_ge(s.w_used, at.peek("w_used", 1))
                            if i < 3 * KT:
                                all_stored()
                            else:
                                act.wait_ge(s.sil_used, at("sil_used"))
                            A(stg[:].rearrange("p a b -> p (a b)"), bg_sums, ACT.Silu).then_inc(s.bg_free, 1)
                            act.wait_ge(s.bg_free, at("bg_free"))
                            act.sem_inc(s.sil_ready, 1)
                at.skip("sil_used", 1)
                phase_end(act, at, s.act_phase)
                with at.repeat(KVH, "attention group") as g:
                    attention_group(g)
                all_stored()
                fetch(ma, J_MA, 0, D, 4, s.gates_in)
                fetch(zb, J_ZB, 0, D, 4, s.gates_in)
                turn_hi(o_hi)
                phase_end(act, at, s.act_phase)
                act.wait_ge(s.gates_in, at("gates_in", 8 * 16))
                with at.repeat(2, "gla branch") as g:
                    for k in range(KT):
                        split(k)
                        if k in (1, 2):
                            some = view(ma, g * HALF + (k - 1) * (NT // 2) * D, (D, NT // 2), (1, HALF))
                            A(some, some, ACT.Sigmoid).then_inc(s.sig_ready, 1)
                        if k in (4, 5):
                            some = view(zb, g * HALF + (k - 4) * (NT // 2) * D, (D, NT // 2), (1, HALF))
                            A(some, some, ACT.Silu).then_inc(s.zb_ready, 1)
                skip_banks(2 * NT)
                phase_end(act, at, s.act_phase)
                turn_hi(act_hi)
                phase_end(act, at, s.act_phase)
                fetch(mb, J_MB, 0, D, 4, s.gates_in)
                act.wait_ge(s.gates_in, at("gates_in", 4 * 16))
                with at.repeat(2, "attention branch") as g:
                    for k in range(KT):
                        split(k)
                        if k in (3, 5):
                            some = view(mb, g * HALF + (k // 2 - 1) * (NT // 2) * D, (D, NT // 2), (1, HALF))
                            A(some, some, ACT.Sigmoid).then_inc(s.sig_ready, 1)
                skip_banks(2 * NT)
                phase_end(act, at, s.act_phase)
                turn_hi(o_hi)
                phase_end(act, at, s.act_phase)
                splits()
                for k in range(KT):
                    split(k, HALF if k + SKEW < KT else P)
                skip_banks(2 * NT)
                phase_end(act, at, s.act_phase)
            param(g_row[:], rows_of(final_norm_g, 0, D))
            sum_squares()

        @block.gpsimd
        def _(pool):
            at = Counts("gpsimd", pool)
            G = nc.gpsimd

            def split(k, width=HALF):
                slot = (k + SKEW) % RING
                pool.wait_ge(s.w_hi_done, at("w_hi_done"))
                G.tensor_tensor(w_lo[:, slot, 0:width], w_raw[:, slot, 0:width],
                                                  w_hi[:, slot, 0:width].bitcast(F32), ALU.subtract).then_inc(s.w_lo_done, 1)

            def splits():
                for k in range(KT):
                    split(k)

            def phase_ends(n=1):
                for _ in range(n):
                    phase_end(pool, at, s.pool_phase)

            def gla_head(h):
                G.tensor_copy(wg_fix[:], view_32(wg, h * GK, (GH * GK, 2), (1, GK)))
                G.tensor_copy(bg_fix[:], view(bg, h, (GH, 2)))
                pool.drain().then_inc(s.gla_fix, 1)
                for i in range(4):
                    split(i, BGW)
                for li, span in enumerate(LEVELS):
                    n = TOK if span < 256 else SEQS[0]
                    pool.wait_ge(s.lev_exp, at("lev_exp"))
                    if li == 2:
                        pool.wait_ge(s.prod, at("prod", 2))
                    elif li > 2:
                        pool.wait_ge(s.prod, at("prod"))
                    pool.sem_inc(s.passed, 1)
                    G.tensor_tensor(view(qk, (li % 2 * 2 + 1) * TOK, (1, n)), view(lev, (li % 2 * 2 + 1) * TOK, (1, n)),
                                    view(qk_t, h * (2 * TOK) + TOK, (1, n)), ALU.mult).then_inc(s.k_ready, 1)
                    split(4 + li, BGW)
                at.skip("prod", 2)
                for i in (13, 14, 15):
                    split(i, BGW)
                phase_ends()

            def view_32(t, start, *dims):
                return bass.AP(t, start, [[2 * GH * GK, 2 * RANK]] + [list(d) for d in dims])

            def rope_swapped(n):
                t, part = n // 3, n % 3
                heads = 8 if part < 2 else KVH
                src, row = (q, t * D + part * HALF) if part < 2 else (kv, t * HALF)
                pool.wait_ge(s.rot2_free, at("rot2_free"))
                for half in range(2):
                    G.tensor_tensor(
                        view(rot2, half * 16, (DH, heads), (32, 2), (1, 16)),
                        view(src, row + (1 - half) * 16, (DH, heads), (32, 2), (1, 16)),
                        view(cs, ((part == 2) * 2 + 1) * NT * DH + t * DH + half * 16, (0, heads), (32, 2), (1, 16)),
                        ALU.mult)
                pool.drain().then_inc(s.rot2_ready, 1)

            def attention_group(g):
                G.tensor_copy(v_grp[:], view(kv, KVH * DH + g * DH, (HALF, NT), (1, DH)))
                k_src = view(kv, g * DH, (HALF, NT), (1, DH))
                for dup in range(2):
                    last = G.tensor_copy(k_st[:, 0, :, dup, :], k_src)
                last.then_inc(s.k_staged, 1)
                pool.wait_ge(s.k_staged, at("k_staged"))
                pool.sem_inc(s.passed, 1)
                for dup in range(2):
                    G.tensor_tensor(k_st[:, 1, :, dup, :], k_src, k_st[:, 0, :, dup, :].bitcast(F32), ALU.subtract)
                pool.drain().then_inc(s.k_staged, 1)
                at.skip("k_staged", 1)

                def stage_q(h):
                    if h >= 2:
                        pool.wait_ge(s.q_turned, at("q_turned", 2))
                    q_src = view(q, g * (GROUP * DH) + h * DH, (D, NT), (1, DH))
                    G.tensor_copy(q_st[:, h % 2, :, 0, :], q_src).then_inc(s.pool_chain, 1)
                    pool.wait_ge(s.pool_chain, at("pool_chain"))
                    pool.sem_inc(s.passed, 1)
                    G.tensor_tensor(q_st[:, h % 2, :, 1, :], q_src,
                                    q_st[:, h % 2, :, 0, :].bitcast(F32), ALU.subtract).then_inc(s.q_staged, 1)

                stage_q(0)
                for i in range(2 * KT):
                    if i in (1, 5, 9):
                        stage_q(i // 4 + 1)
                    split(i, BGW if i + SKEW < 2 * KT else HALF)
                at.skip("q_turned", 4)
                phase_ends()

            pool.sem_inc(s.w_lo_done, RING)
            for k in range(SKEW):
                split(k - SKEW, P)
            with at.repeat(DEPTH, "layer"):
                G.memset(wg[:], 0.0)
                phase_ends()
                for k in range(KT):
                    split(k, P if k + SKEW < KT else HALF)
                with at.repeat(4, "gla projections"):
                    splits()
                phase_ends()
                with at.repeat(GH, "gla head") as h:
                    gla_head(h)
                for i in range(6 * KT):
                    if i == 12:
                        pool.wait_ge(s.tables, at("tables"))
                        pool.wait_ge(s.qkv_in, at("qkv_in", 6 * 16))
                    if i >= 12 and i % 2 == 0:
                        rope_swapped((i - 12) // 2)
                    split(i % KT, BGW)
                phase_ends()
                with at.repeat(KVH, "attention group") as g:
                    attention_group(g)
                phase_ends()
                with at.repeat(2, "gla branch"):
                    splits()
                phase_ends(2)
                with at.repeat(2, "attention branch"):
                    splits()
                phase_ends(2)
                splits()
                for k in range(KT):
                    split(k, HALF if k + SKEW < KT else P)
                phase_ends()

        @block.vector
        def _(dve):
            at = Counts("vector", dve, prod_free=1, rot2_free=1)
            V = nc.vector

            def rsqrt_of(n, size, dst, settled=False):
                if not settled:
                    dve.drain().then_inc(s.dve_chain, 1)
                    dve.wait_ge(s.dve_chain, at("dve_chain"))
                V.tensor_scalar(st[:, 1, 0:n], st[:, 0, 0:n], 1.0 / size, EPS, ALU.mult, ALU.add).then_inc(s.stat_v, 1)
                dve.wait_ge(s.stat_y0, at("stat_y0"))
                V.tensor_tensor(st[:, 3, 0:n], st[:, 2, 0:n], st[:, 2, 0:n], ALU.mult).then_inc(s.dve_chain, 1)
                dve.wait_ge(s.dve_chain, at("dve_chain"))
                V.tensor_tensor(st[:, 3, 0:n], st[:, 3, 0:n], st[:, 1, 0:n], ALU.mult).then_inc(s.dve_chain, 1)
                dve.wait_ge(s.dve_chain, at("dve_chain"))
                V.tensor_scalar(st[:, 3, 0:n], st[:, 3, 0:n], -0.5, 1.5, ALU.mult, ALU.add).then_inc(s.dve_chain, 1)
                dve.wait_ge(s.dve_chain, at("dve_chain"))
                V.tensor_tensor(dst, st[:, 3, 0:n], st[:, 2, 0:n], ALU.mult).then_inc(s.dve_chain, 1)
                dve.wait_ge(s.dve_chain, at("dve_chain"))

            def scaled_tokens(t):
                V.scalar_tensor_tensor(hn[:, t % 2, :], x[:, t, :], st[:, 4, t:t + 1], g_row[:],
                                                        ALU.mult, ALU.mult).then_inc(s.hn_ready, 1)

            def turn_lo(hi, lo, steps=range(2 * NT)):
                for n in steps:
                    t, k0 = n // 2, n % 2 * 4
                    dve.wait_ge(s.turn_hi, at("turn_hi"))
                    V.tensor_tensor(
                        lo[:, k0:k0 + 4, t * P:(t + 1) * P],
                        ps[:, n % 4 * HALF:(n % 4 + 1) * HALF].rearrange("p (a b) -> p a b", a=4),
                        hi[:, k0:k0 + 4, t * P:(t + 1) * P].bitcast(F32), ALU.subtract).then_inc(s.turn_free, 1)

            def normalise(params):
                dve.wait_ge(s.stat_sum, at("stat_sum"))
                rsqrt_of(NT, D, st[:, 4, 0:NT], settled=True)
                dve.wait_ge(s.param, at("param", 16 * params))
                dve.sem_inc(s.passed, 1)

            def gla_head(h):
                dve.wait_ge(s.gla_fix, at("gla_fix"))
                dve.wait_ge(s.gate_ready, at("gate_ready"))
                for d in range(2):
                    dve.wait_ge(s.gate_abs, at("gate_abs"))
                    V.tensor_scalar(view(lev, d * TOK, (FH, 2), (1, FH)), view_ps(d * 2 * HALF, (HALF, 2), (1, FH)),
                                    bg_fix[:, d:d + 1], 0.0, ALU.add, ALU.min)
                V.memset(view(ce, TOK, (SEQS[0], 2)), 0.0).then_inc(s.dve_chain, 1)
                dve.wait_ge(s.dve_chain, at("dve_chain"))
                dve.wait_ge(s.gate_log, at("gate_log"))
                for d in range(2):
                    for start, n in ((0, SEQS[0]), (SEQS[0], SEQS[1])):
                        V.tensor_tensor_scan(view(ce, d * TOK + start + d, (1, n - d)),
                                             view(lev, d * TOK + start, (1, n - d)),
                                             view(lev, (2 + d) * TOK + start, (1, n - d)), 0.0, ALU.add, ALU.subtract)
                dve.drain().then_inc(s.dve_chain, 1)
                dve.wait_ge(s.dve_chain, at("dve_chain"))

                def differences(li):
                    span = LEVELS[li]
                    nb = (TOK if span < 256 else SEQS[0]) // (2 * span)
                    base = li % 2 * 2 * TOK
                    blocks, within, mid = (2 * span, nb), (1, span), (0, span)
                    ref = view(ce, span - 1, (TOK + 1, 2), blocks, mid)
                    V.tensor_tensor(view(lev, base + span, (TOK, 2), blocks, within),
                                    view(ce, span, (TOK, 2), blocks, within), ref, ALU.subtract)
                    V.tensor_tensor(view(lev, base + TOK, (-TOK, 2), blocks, within), ref,
                                                     view(ce, 0, (TOK, 2), blocks, within), ALU.subtract).then_inc(s.lev_diff, 1)

                def scaled(li):
                    n = TOK if LEVELS[li] < 256 else SEQS[0]
                    dve.wait_ge(s.lev_exp, at("lev_exp"))
                    V.tensor_tensor(view(qk, li % 2 * 2 * TOK, (1, n)), view(lev, li % 2 * 2 * TOK, (1, n)),
                                    view(qk_t, h * (2 * TOK), (1, n)), ALU.mult).then_inc(s.q_ready, 1)

                def collect(n):
                    dve.wait_ge(s.prod, at("prod"))
                    dve.sem_inc(s.passed, 1)
                    if n == 0:
                        last = V.tensor_copy(amat[:], ps[:, 0:TOK].rearrange("p (a b) -> p a b", a=NT))
                    elif n <= NMASK:
                        last = V.copy_predicated(amat[:], mask[:, n - 1, :].unsqueeze(1).to_broadcast([P, NT, P]),
                                                 ps[:, 0:TOK].rearrange("p (a b) -> p a b", a=NT))
                    elif n == NMASK + 1:
                        last = V.tensor_copy(aoff1[:], ps[:, 0:TOK].rearrange("p (a b) -> p a b", a=NT))
                    else:
                        last = V.tensor_copy(aoff2[:], ps[:, 0:2 * HALF].rearrange("p (a b c) -> p a b c", a=NTP, b=2))
                    last.then_inc(s.prod_free, 1)
                    dve.wait_ge(s.prod_free, at("prod_free"))
                    if n == len(LEVELS):
                        dve.sem_inc(s.passed, 1)

                nl = len(LEVELS)
                differences(0)
                for li in range(nl):
                    if li + 1 < nl:
                        if li >= 1:
                            dve.wait_ge(s.k_ready, at("k_ready"))
                        differences(li + 1)
                    scaled(li)
                    collect(li)
                at.skip("k_ready", 2)
                collect(nl)
                dve.drain().then_inc(s.a_ready, 1)
                dve.wait_ge(s.stat_sum, at("stat_sum"))
                V.tensor_copy(view(st, h, (GH, NT)), st[:, 1, 0:NT])
                phase_end(dve, at, s.dve_phase)

            def drain_banks(write):
                for t in range(NT):
                    dve.wait_ge(s.gemm_ready, at("gemm_ready"))
                    write(t).then_inc(s.drained, 1)

            def merge(g, add):
                m = mb if add else ma
                if not add:
                    for some in range(2):
                        dve.wait_ge(s.zb_ready, at("zb_ready"))
                        out = view(q, g * HALF + some * (NT // 2) * D, (D, NT // 2), (1, HALF))
                        V.tensor_tensor(out, out, view(zb, g * HALF + some * (NT // 2) * D, (D, NT // 2), (1, HALF)), ALU.mult)
                dve.wait_ge(s.sig_ready, at("sig_ready", 2))
                for t in range(NT):
                    dve.wait_ge(s.gemm_ready, at("gemm_ready"))
                    out = view(merged, t * D + g * HALF, (1, HALF))
                    sig = view(m, t * D + g * HALF, (1, HALF))
                    if add:
                        V.tensor_tensor(sig, bank(t), sig, ALU.mult).then_inc(s.dve_chain, 1)
                        dve.wait_ge(s.dve_chain, at("dve_chain"))
                        last = V.tensor_tensor(out, out, sig, ALU.add)
                    else:
                        last = V.tensor_tensor(out, bank(t), sig, ALU.mult)
                    last.then_inc(s.drained, 1)

            def rope_tables():
                for i in range(2):
                    for half in range(2):
                        V.tensor_tensor(view(cs, i * 2 * NT * DH + half * 16, (DH, NT), (32, 2), (1, 16)),
                                        view(cs_raw, half * 16, (DH, NT), (32, 2), (1, 16)),
                                        view(g_qk, i * DH + half * 16, (0, NT), (32, 2), (1, 16)), ALU.mult)
                        V.tensor_tensor(view(cs, (i * 2 + 1) * NT * DH + half * 16, (DH, NT), (32, 2), (1, 16)),
                                        view(cs_raw, NT * DH + half * 16, (DH, NT), (32, 2), (1, 16)),
                                        view(g_qk, i * DH + (1 - half) * 16, (0, NT), (32, 2), (1, 16)), ALU.mult)
                dve.drain().then_inc(s.tables, 1)
                dve.wait_ge(s.tables, at("tables"))

            def square_sums():
                for n in range(3 * NT):
                    t, part = n // 3, n % 3
                    heads = 8 if part < 2 else KVH
                    stat = t * AH + part * 8 if part < 2 else NT * AH + t * KVH
                    dve.wait_ge(s.sq_ready, at("sq_ready"))
                    V.tensor_reduce(view(st, stat, (1, heads)), view(sq, n % 2 * HALF, (DH, heads), (1, DH)),
                                    AX.X, ALU.add).then_inc(s.sq_used, 1)

            def gate_columns(c):
                dve.wait_ge(s.sil_ready, at("sil_ready"))
                out = view(va, c * BGW, (D, NT), (1, BGW))
                V.tensor_tensor(out, out, stg[:], ALU.mult).then_inc(s.sil_used, 1)

            def rope(n):
                t, part = n // 3, n % 3
                heads = 8 if part < 2 else KVH
                src, row = (q, t * D + part * HALF) if part < 2 else (kv, t * HALF)
                stat = t * AH + part * 8 if part < 2 else NT * AH + t * KVH
                data = view(src, row, (DH, heads), (1, DH))
                turned = view(rot1, 0, (DH, heads), (1, DH))
                V.tensor_tensor(turned, data, view(cs, (part == 2) * 2 * NT * DH + t * DH, (0, heads), (1, DH)),
                                ALU.mult).then_inc(s.dve_chain, 1)
                dve.wait_ge(s.dve_chain, at("dve_chain"))
                dve.wait_ge(s.rot2_ready, at("rot2_ready"))
                V.tensor_tensor(turned, turned, view(rot2, 0, (DH, heads), (1, DH)), ALU.add).then_inc(s.dve_chain, 1)
                dve.wait_ge(s.dve_chain, at("dve_chain"))
                V.tensor_tensor(data, turned, view(st, 4 * NSTAT + stat, (1, heads), (0, DH)), ALU.mult).then_inc(s.rot2_free, 1)
                dve.wait_ge(s.rot2_free, at("rot2_free"))

            def attention_group(g):
                for part, dst in enumerate((k_hh, k_ll)):
                    dve.wait_ge(s.k_turned, at("k_turned"))
                    V.tensor_copy(dst[:], ps[:, part * 2 * HALF:part * 2 * HALF + TOK]).then_inc(s.k_stack, 1)

                def stack_q(h, first):
                    dve.wait_ge(s.q_turned, at("q_turned"))
                    start, n = (0, 4 * P) if first else (4 * P, 2 * P)
                    V.tensor_copy(q_hl[:, h % 2, start:start + n], bank(4, n)).then_inc(s.q_stack, 1)

                def row_max(n):
                    h, u = divmod(n, UNITS)
                    dve.wait_ge(s.score, at("score"))
                    k = 1 if u < NTP else 2
                    out = view(st, 2 * (n % 2), (1, k))
                    V.tensor_reduce(out, view_ps(n % 2 * HALF, (HALF // k, k), (1, HALF // k)), AX.X, ALU.max, negate=True).then_inc(s.dve_chain, 1)
                    dve.wait_ge(s.dve_chain, at("dve_chain"))
                    V.tensor_scalar(out, out, DH ** -0.5, None, ALU.mult).then_inc(s.neg_max, 1)

                def copy_pt(n):
                    if n % 2:
                        dve.wait_ge(s.pr_turned, at("pr_turned"))
                        if n >= 2:
                            dve.wait_ge(s.pv_done, at.peek("pv_done", -1))
                        V.tensor_copy(pr_t[:, 1, :], bank(2)).then_inc(s.pr_t_odd, 1)
                    else:
                        at.skip("pr_turned", 1)
                    at.skip("pv_done", 1)

                def head_out(h):
                    dve.wait_ge(s.pv_done, at.peek("pv_done", 0))
                    V.reciprocal(st[:, 2, 0:NT], st[:, 1, h % 2 * NT:h % 2 * NT + NT]).then_inc(s.dve_chain, 1)
                    dve.wait_ge(s.dve_chain, at("dve_chain"))
                    V.tensor_tensor(view(q, g * (GROUP * DH) + h * DH, (D, NT), (1, DH)),
                                                      view_ps(3 * HALF, (DH, NT), (1, DH)),
                                                      view(st, 2 * NSTAT, (1, NT), (0, DH)), ALU.mult).then_inc(s.o_drained, 1)

                stack_q(0, True)
                stack_q(0, False)
                total = GROUP * UNITS
                row_max(0)
                for n in range(total):
                    h = n // UNITS + 1
                    if n % UNITS in (1, 2) and h < GROUP:
                        stack_q(h, n % UNITS == 1)
                    if n + 1 < total:
                        row_max(n + 1)
                    if n % UNITS == 0 and n > 0:
                        head_out(h - 2)
                    copy_pt(n)
                head_out(GROUP - 1)
                phase_end(dve, at, s.dve_phase)

            dve.sem_inc(s.drained, 8)
            dve.sem_inc(s.turn_free, 4)
            dve.sem_inc(s.prod_free, 1)
            dve.sem_inc(s.sq_used, 2)
            dve.sem_inc(s.rot2_free, 1)
            dve.sem_inc(s.o_drained, 1)
            dve.wait_ge(s.x_in, 64)
            V.tensor_copy(mask[:], mask_raw[:])
            with at.repeat(DEPTH, "layer"):
                normalise(9)
                scaled_tokens(0)
                scaled_tokens(1)
                for t in range(NT):
                    turn_lo(act_hi, act_lo, (2 * t, 2 * t + 1))
                    if t + 2 < NT:
                        scaled_tokens(t + 2)
                phase_end(dve, at, s.dve_phase)
                for half in range(2):
                    dve.wait_ge(s.gemm_ready, at("gemm_ready"))
                    V.tensor_copy(gl_t[:, half * FH:(half + 1) * FH], ps[0:2 * RANK, (6 + half) * HALF:(6 + half) * HALF + FH]).then_inc(s.drained, 1)
                with at.repeat(2, "gla qk") as g:
                    for b in range(8):
                        dve.wait_ge(s.gemm_ready, at("gemm_ready"))
                        V.tensor_copy(view(qk_t, g * TOK + b // 2 * 2 * TOK + b % 2 * FH, (1, FH)), bank(b, FH)).then_inc(s.drained, 1)
                with at.repeat(2, "gla v") as g:
                    drain_banks(lambda t: V.tensor_copy(view(va, t * D + g * HALF, (1, HALF)), bank(t)))
                dve.wait_ge(s.param, at("param", 2 * 16))
                dve.sem_inc(s.passed, 1)
                phase_end(dve, at, s.dve_phase)
                with at.repeat(GH, "gla head") as h:
                    gla_head(h)
                rsqrt_of(NT * GH, GV, st[:, 4, 0:NT * GH])
                dve.wait_ge(s.param, at("param", 5 * 16))
                dve.sem_inc(s.passed, 1)
                for t in range(NT):
                    for h in range(GH):
                        out = view(va, t * D + h * GV, (1, GV))
                        V.scalar_tensor_tensor(out, out, st[:, 4, t * GH + h:t * GH + h + 1], gv_row[:], ALU.mult, ALU.mult)
                rope_tables()
                square_sums()
                rsqrt_of(NSTAT, DH, st[:, 4, 0:NSTAT])
                for n in range(3 * NT):
                    rope(n)
                    if n in (7, 11, 15):
                        gate_columns((n - 7) // 4)
                dve.sem_inc(s.passed, 1)
                gate_columns(3)
                phase_end(dve, at, s.dve_phase)
                with at.repeat(KVH, "attention group") as g:
                    attention_group(g)
                turn_lo(o_hi, o_lo)
                phase_end(dve, at, s.dve_phase)
                with at.repeat(2, "gla branch") as g:
                    merge(g, False)
                phase_end(dve, at, s.dve_phase)
                turn_lo(act_hi, act_lo)
                phase_end(dve, at, s.dve_phase)
                with at.repeat(2, "attention branch") as g:
                    merge(g, True)
                phase_end(dve, at, s.dve_phase)
                turn_lo(o_hi, o_lo)
                phase_end(dve, at, s.dve_phase)
                with at.repeat(2, "output") as g:
                    def residual(t):
                        out = view(x, t * D + g * HALF, (1, HALF))
                        return V.tensor_tensor(out, out, bank(t), ALU.add)
                    drain_banks(residual)
                phase_end(dve, at, s.dve_phase)
            normalise(1)
            for t in range(NT):
                V.scalar_tensor_tensor(y_out[:, t, :], x[:, t, :], st[:, 4, t:t + 1], g_row[:], ALU.mult, ALU.mult).then_inc(s.y_ready, 1)


INPUTS = ["x_prompt", "x_sample", "norm_g", "w_in", "w_gate_f", "b_gate_f", "w_gate_b", "b_gate_b", "gla_norm_g",
          "q_norm_g", "k_norm_g", "w_branch_a", "w_branch_b", "w_out", "final_norm_g"]


def shape_constants():
    tok = np.arange(P)
    masks = np.zeros((P, NMASK, P), np.float32)
    for li in range(NMASK):
        s = LEVELS[li]
        same = tok[:, None] // (2 * s) == tok[None, :] // (2 * s)
        masks[:, li, :] = same & (tok[:, None] // s != tok[None, :] // s)
    nf = DH // 4
    inv = ROPE_THETA ** (-np.arange(nf, dtype=np.float32) / np.float32(nf))
    place = np.concatenate([np.arange(n) for n in SEQS])
    angles = [(place // GRID_W).astype(np.float32)[:, None] * inv, (place % GRID_W).astype(np.float32)[:, None] * inv]
    cos = np.concatenate([np.cos(a) for a in angles for _ in range(2)], axis=1)
    sin = np.concatenate([sign * np.sin(a) for a in angles for sign in (-1, 1)], axis=1)
    by_tile = lambda a: np.ascontiguousarray(a.astype(np.float32).reshape(NT, P, DH).transpose(1, 0, 2))
    return {"identity": np.eye(P, dtype=np.float32), "masks": masks, "rope_cos": by_tile(cos), "rope_sin": by_tile(sin)}


def kernel(**inputs):
    import concourse.bacc as bacc
    from concourse.bass_utils import run_bass_kernel_spmd

    nc = bacc.Bacc("TRN2", target_bir_lowering=False, num_devices=1)
    arrays = {name: np.ascontiguousarray(inputs[name]) for name in INPUTS} | shape_constants()
    arrays = {f"in_{name}": a for name, a in arrays.items()}
    aps = [nc.dram_tensor(name, a.shape, mybir.dt.from_np(a.dtype), kind="ExternalInput").ap()
           for name, a in arrays.items()]
    outs = [nc.dram_tensor(name, (1, n, D), F32, kind="ExternalOutput").ap()
            for name, n in zip(("y_prompt", "y_sample"), SEQS)]
    trunk(nc, *aps, *outs)
    assert not WRONG, WRONG
    result = run_bass_kernel_spmd(nc, [arrays], core_ids=[0]).results[0]
    return result["y_prompt"], result["y_sample"]
```

```python
from contextlib import contextmanager

import numpy as np

import concourse.bass as bass
from concourse import mybir

F32 = mybir.dt.float32
F32R = mybir.dt.float32r
U8 = mybir.dt.uint8
ALU = mybir.AluOpType
ACT = mybir.ActivationFunctionType
AX = mybir.AxisListType

P = 128
D = 1024
KT = D // P
SEQS = (512, 256)
TOK = sum(SEQS)
NT = TOK // P
NTP = SEQS[0] // P
DEPTH = 2
EPS = 1e-6
HALF = 512
FH = TOK // 2
GH, GK, GV = 4, 128, 256
RANK = 16
GATE_NORM = 16.0
LEVELS = (1, 2, 4, 8, 16, 32, 64, 128, 256)
NMASK = 7
AH, KVH, DH = 16, 4, 64
GROUP = AH // KVH
GRID_W, ROPE_THETA = 64, 10000.0
UNITS = NTP + 1
C_QKV, C_GATES, C_ZA, C_QB, C_ZB, C_MA, C_MB = 0, 2048, 2080, 3104, 4640, 5664, 6688
RING = 4
SKEW = 3
BGW = 256
BG_BANK = 5
J_Q, J_K, J_V, J_ZB, J_ZA, J_MA, J_MB, NBG = 0, 4, 5, 6, 10, 10, 14, 18
BG_BLOCKS = 2 * KT
BG_TILES = BG_BLOCKS * NT


def spread(first, steps, *parts):
    done, at_step = [], 0
    for last, tiles in parts:
        n = last - at_step
        done += [first + -(-(tiles - first) * (i + 1) // n) for i in range(n)]
        at_step, first = last, tiles
    assert len(done) == steps
    return done


def start_steps(block, first, done, blocks):
    return {i: -1 if i * NT < first else next((n for n, d in enumerate(done) if i * NT < d), len(done))
            for i in range(block, block + blocks)}


GLA_FIRST, ATT_FIRST = 6 * NT, 22
GLA_MID, GLA_BEHIND = 9, 9
GLA_STEPS = len(LEVELS) + 1
GLA_DONE = spread(GLA_FIRST, GLA_STEPS, (2, KT * NT), (8, BG_TILES),
                  (GLA_STEPS, BG_TILES + GLA_FIRST - GLA_MID - GLA_BEHIND))
GLA_LAST_DONE = spread(GLA_FIRST, GLA_STEPS, (2, KT * NT), (GLA_STEPS, BG_TILES))
ATT_DONE = spread(ATT_FIRST, GROUP * UNITS, (7, KT * NT), (GROUP * UNITS, BG_TILES))
ATT_START = start_steps(0, ATT_FIRST, ATT_DONE, BG_BLOCKS)
GLA_START = start_steps(GLA_FIRST // NT, GLA_FIRST, GLA_DONE, BG_BLOCKS)
GLA_LAST_START = start_steps(GLA_FIRST // NT, GLA_FIRST, GLA_LAST_DONE, BG_BLOCKS - GLA_FIRST // NT)

BASE = 16512
R_X = BASE
R_ACT = R_X + NT * D * 4
R_W = R_ACT + 2 * KT * TOK * 4
R_V = R_W + 3 * RING * HALF * 4
R_M = R_V + NT * D * 4
R_O = R_M + NT * D * 4
R_G = R_O + 2 * KT * TOK * 4
R_S = R_G + NT * HALF * 4
ROW = TOK * 4


PER_TURN = {
    "sync gla projections": {
        "w_lo_done": 8},
    "sync gla background": {
        "w_lo_done": 16},
    "sync rope background": {
        "w_lo_done": 8},
    "sync attention background": {
        "w_lo_done": 16},
    "sync gla branch": {
        "w_lo_done": 8},
    "sync attention branch": {
        "w_lo_done": 8},
    "sync output": {
        "w_lo_done": 8},
    "sync layer": {
        "w_lo_done": 264},
    "tensor gla qk": {
        "w_lo_done": 8, "drained": 8},
    "tensor gla v": {
        "w_lo_done": 8, "drained": 6},
    "tensor gla head": {
        "w_lo_done": 16, "prod_free": 10, "gla_fix": 1, "bg_free": 6, "gate_used": 1, "q_ready": 9, "k_ready":
        9, "a_ready": 1},
    "tensor rope background": {
        "w_lo_done": 16, "bg_free": 6},
    "tensor attention group": {
        "w_lo_done": 16, "bg_free": 6, "k_staged": 2, "q_staged": 4, "k_stack": 2, "q_stack": 8, "exp_done": 20,
        "v_ready": 1, "pr_t_ready": 20, "o_drained": 4},
    "tensor gla branch": {
        "w_lo_done": 8, "drained": 6},
    "tensor attention branch": {
        "w_lo_done": 8, "drained": 6},
    "tensor output": {
        "w_lo_done": 8, "drained": 6},
    "tensor layer": {
        "hn_ready": 6, "turn_free": 48, "act_phase": 11, "dve_phase": 11, "pool_phase": 11, "w_lo_done": 264,
        "drained": 66, "prod_free": 40, "gla_fix": 4, "bg_free": 66, "gate_used": 4, "q_ready": 36, "k_ready":
        36, "a_ready": 4, "k_staged": 8, "q_staged": 16, "k_stack": 8, "q_stack": 32, "exp_done": 80, "v_ready":
        4, "pr_t_ready": 80, "o_drained": 16},
    "scalar gla projections": {
        "w_used": 8, "w_slot0": 32, "w_slot1": 32, "w_slot2": 32, "w_slot3": 32},
    "scalar gla head": {
        "w_used": 16, "w_slot0": 64, "w_slot1": 64, "w_slot2": 64, "act_chain": 3, "w_slot3": 64, "gla_fix": 1,
        "gate_ready": 1, "gate_abs": 2, "lev_diff": 9, "stored": 32, "bg_free": 6, "gla_o": 1},
    "scalar attention group": {
        "w_used": 16, "w_slot0": 64, "w_slot1": 64, "w_slot2": 64, "w_slot3": 64, "stored": 32, "bg_free": 6,
        "neg_max": 20, "pr_turned": 20, "pv_done": 20},
    "scalar gla branch": {
        "w_used": 8, "w_slot0": 32, "w_slot1": 32, "w_slot2": 32, "w_slot3": 32},
    "scalar attention branch": {
        "w_used": 8, "w_slot0": 32, "w_slot1": 32, "w_slot2": 32, "w_slot3": 32},
    "scalar layer": {
        "w_used": 264, "w_slot0": 1056, "w_slot1": 1056, "w_slot2": 1056, "stat_v": 3, "act_chain": 15,
        "turned": 48, "pe_phase": 11, "dve_phase": 11, "pool_phase": 11, "w_slot3": 1056, "gemm_ready": 66,
        "drained": 66, "gla_fix": 4, "gate_ready": 4, "gate_abs": 8, "lev_diff": 36, "stored": 288, "bg_free":
        66, "gla_o": 4, "qkv_in": 96, "sq_used": 18, "sil_used": 4, "neg_max": 80, "pr_turned": 80, "pv_done":
        80, "gates_in": 192},
    "gpsimd gla projections": {
        "w_hi_done": 8},
    "gpsimd gla head": {
        "w_hi_done": 16, "lev_exp": 9, "prod": 10},
    "gpsimd attention group": {
        "w_hi_done": 16, "group_free": 2, "pool_chain": 4, "q_turned": 8},
    "gpsimd gla branch": {
        "w_hi_done": 8},
    "gpsimd attention branch": {
        "w_hi_done": 8},
    "gpsimd layer": {
        "w_hi_done": 264, "pe_phase": 11, "act_phase": 11, "dve_phase": 11, "lev_exp": 36, "prod": 40, "tables":
        1, "qkv_in": 96, "rot2_free": 18, "group_free": 8, "pool_chain": 16, "q_turned": 32},
    "vector gla qk": {
        "gemm_ready": 8},
    "vector gla v": {
        "gemm_ready": 6},
    "vector gla head": {
        "dve_chain": 2, "gla_fix": 1, "gate_ready": 1, "gate_abs": 2, "gate_used": 1, "gate_log": 1, "lev_exp":
        9, "prod": 10, "prod_free": 10, "k_ready": 9},
    "vector attention group": {
        "dve_chain": 4, "k_staged": 2, "k_turned": 2, "q_turned": 8, "score": 20, "pv_done": 20},
    "vector gla branch": {
        "gemm_ready": 6, "zb_ready": 2, "sig_ready": 2},
    "vector attention branch": {
        "dve_chain": 6, "gemm_ready": 6, "sig_ready": 2},
    "vector output": {
        "gemm_ready": 6},
    "vector layer": {
        "stat_sum": 1, "stat_y0": 3, "dve_chain": 87, "param": 256, "turn_hi": 48, "pe_phase": 11, "act_phase":
        11, "pool_phase": 11, "gemm_ready": 66, "gla_fix": 4, "gate_ready": 4, "gate_abs": 8, "gate_used": 4,
        "gate_log": 4, "lev_exp": 36, "prod": 40, "prod_free": 40, "k_ready": 36, "tables": 1, "sq_ready": 18,
        "rot2_ready": 18, "rot2_free": 18, "sil_ready": 4, "k_staged": 8, "k_turned": 8, "q_turned": 32,
        "score": 80, "pv_done": 80, "zb_ready": 4, "sig_ready": 8},
}

WRONG = {}


class Counts:

    def __init__(self, who, eng, **start):
        self.who, self.eng, self.start = who, eng, start
        self.base, self.n = {}, {}

    def __call__(self, name, by=1):
        self.skip(name, by)
        return self.base[name] + self.n[name]

    def skip(self, name, by):
        self.base.setdefault(name, self.start.get(name, 0))
        self.n[name] = self.n.get(name, 0) + by

    def peek(self, name, more):
        self.skip(name, 0)
        return self.base[name] + (self.n[name] + more)

    @contextmanager
    def repeat(self, times, loop):
        per = PER_TURN.get(f"{self.who} {loop}", {})
        with self.eng.Fori(0, times) as i:
            for name in per:
                self.skip(name, 0)
            base, n = dict(self.base), dict(self.n)
            for name, by in per.items():
                self.base[name] = base[name] + n[name] + i * by
                self.n[name] = 0
            yield i
            found = {}
            for name in self.n:
                by = self.n[name] - (0 if name in per else n.get(name, 0))
                if by:
                    found[name] = by
            if found != per:
                WRONG[f"{self.who} {loop}"] = found
        for name in self.n:
            self.base[name] = base.get(name, self.start.get(name, 0))
            self.n[name] = n.get(name, 0) + times * found.get(name, 0)


class Semaphores:

    def __init__(self, nc):
        sem = nc.alloc_semaphore
        self.pe_phase = sem("pe_phase")
        self.act_phase = sem("act_phase")
        self.dve_phase = sem("dve_phase")
        self.pool_phase = sem("pool_phase")
        self.passed = sem("passed")
        self.w_hi_done = sem("w_hi_done")
        self.w_lo_done = sem("w_lo_done")
        self.w_used = sem("w_used")
        self.gemm_ready = sem("gemm_ready")
        self.drained = sem("drained")
        self.bg_free = sem("bg_free")
        self.stored = sem("stored")
        self.sil_ready = sem("sil_ready")
        self.sil_used = sem("sil_used")
        self.qkv_in = sem("qkv_in")
        self.gates_in = sem("gates_in")
        self.x_in = sem("x_in")
        self.param = sem("param")
        self.y_ready = sem("y_ready")
        self.out_done = sem("out_done")
        self.act_chain = sem("act_chain")
        self.dve_chain = sem("dve_chain")
        self.pool_chain = sem("pool_chain")
        self.stat_sum = sem("stat_sum")
        self.stat_v = sem("stat_v")
        self.stat_y0 = sem("stat_y0")
        self.hn_ready = sem("hn_ready")
        self.turned = sem("turned")
        self.turn_hi = sem("turn_hi")
        self.turn_free = sem("turn_free")
        self.gla_fix = sem("gla_fix")
        self.gate_ready = sem("gate_ready")
        self.gate_abs = sem("gate_abs")
        self.gate_used = sem("gate_used")
        self.gate_log = sem("gate_log")
        self.lev_diff = sem("lev_diff")
        self.lev_exp = sem("lev_exp")
        self.q_ready = sem("q_ready")
        self.k_ready = sem("k_ready")
        self.prod = sem("prod")
        self.prod_free = sem("prod_free")
        self.a_ready = sem("a_ready")
        self.gla_o = sem("gla_o")
        self.zb_ready = sem("zb_ready")
        self.sig_ready = sem("sig_ready")
        self.sq_ready = sem("sq_ready")
        self.sq_used = sem("sq_used")
        self.tables = sem("tables")
        self.rot2_ready = sem("rot2_ready")
        self.rot2_free = sem("rot2_free")
        self.group_free = sem("group_free")
        self.v_ready = sem("v_ready")
        self.k_staged = sem("k_staged")
        self.k_turned = sem("k_turned")
        self.k_stack = sem("k_stack")
        self.q_staged = sem("q_staged")
        self.q_turned = sem("q_turned")
        self.q_stack = sem("q_stack")
        self.score = sem("score")
        self.neg_max = sem("neg_max")
        self.exp_done = sem("exp_done")
        self.pr_turned = sem("pr_turned")
        self.pr_t_ready = sem("pr_t_ready")
        self.pv_done = sem("pv_done")
        self.o_drained = sem("o_drained")
        self.w_slot = [sem(f"w_slot{i}") for i in range(RING)]


def trunk(nc, x_prompt, x_sample, norm_g, w_in, w_gate_f, b_gate_f, w_gate_b, b_gate_b, gla_norm_g,
          q_norm_g, k_norm_g, w_branch_a, w_branch_b, w_out, final_norm_g,
          identity, masks, rope_cos, rope_sin, y_prompt, y_sample):
    def sb(name, shape, offset, dtype=F32):
        return nc.alloc_sbuf_tensor_at(name, shape, dtype, offset=offset)

    def view(t, start, *dims):
        row = 1
        for n in t.shape[1:]:
            row *= n
        return bass.AP(t, start, [[row, P]] + [list(d) for d in dims])

    def rows_of(a, start, n):
        return bass.AP(a.tensor, start, [[0, P], [1, n]])

    x = sb("x", [P, NT, D], R_X)
    act_hi = sb("act_hi", [P, KT, TOK], R_ACT, F32R)
    act_lo = sb("act_lo", [P, KT, TOK], R_ACT + KT * ROW, F32R)
    w_raw = sb("w_raw", [P, RING, HALF], R_W)
    w_hi = sb("w_hi", [P, RING, HALF], R_W + RING * HALF * 4, F32R)
    w_lo = sb("w_lo", [P, RING, HALF], R_W + 2 * RING * HALF * 4, F32R)
    va = sb("va", [P, NT, D], R_V)
    qk_t = sb("qk_t", [P, GH, 2, TOK], R_M)
    q = sb("q", [P, NT, D], R_M)
    ma = sb("ma", [P, NT, D], R_ACT)
    zb = sb("zb", [P, NT, D], R_ACT + NT * D * 4)
    mb = sb("mb", [P, NT, D], R_M)
    merged = sb("merged", [P, NT, D], R_V)
    stg = sb("stg", [P, NT, BGW], R_G)
    proj = nc.dram_tensor("proj", [P, NBG, NT, BGW], F32, kind="Internal")
    o_hi = sb("o_hi", [P, KT, TOK], R_O, F32R)
    o_lo = sb("o_lo", [P, KT, TOK], R_O + KT * ROW, F32R)
    g_row = sb("g_row", [P, D], R_O)
    hn = sb("hn", [P, 2, D], R_O + D * 4)
    y_out = sb("y_out", [P, NT, D], R_O + 4 * D * 4)
    mask_raw = sb("mask_raw", [P, NMASK, P], R_V)
    ce = sb("ce", [P, 2, TOK], R_O)
    lev = sb("lev", [P, 2, 2, TOK], R_O + 2 * ROW)
    qk = sb("qk", [P, 2, 2, TOK], R_O + 6 * ROW)
    gl_t = sb("gl_t", [2 * RANK, TOK], R_O + 10 * ROW)
    amat = sb("amat", [P, NT, P], R_O + 11 * ROW)
    aoff1 = sb("aoff1", [P, NT, P], R_O + 12 * ROW)
    aoff2 = sb("aoff2", [P, NTP, 2, P], R_O + 13 * ROW)
    wg_fix = sb("wg_fix", [2 * RANK, 2, GK], R_G + NT * BGW * 4)
    wg = sb("wg", [2 * RANK, 2, GH * GK], R_G + NT * BGW * 4 + 2 * GK * 4)
    kv = sb("kv", [P, NT, 2, KVH, DH], R_O)
    k_hh = sb("k_hh", [P, TOK], R_O + 4 * ROW, F32R)
    k_ll = sb("k_ll", [P, TOK], R_O + 5 * ROW, F32R)
    q_hl = sb("q_hl", [P, 2, TOK], R_O + 6 * ROW, F32R)
    q_st = sb("q_st", [P, 2, NT, 2, DH], R_O + 8 * ROW, F32R)
    k_st = sb("k_st", [P, 2, NT, 2, DH], R_O + 10 * ROW, F32R)
    v_grp = sb("v_grp", [P, NT, DH], R_O + 12 * ROW)
    pr = sb("pr", [P, 2, HALF], R_O + 12 * ROW + NT * DH * 4)
    pr_t = sb("pr_t", [P, 2, HALF], R_O + 12 * ROW + NT * DH * 4 + 2 * HALF * 4)
    R_T = R_O + 4 * ROW
    cs = sb("cs", [P, 2, 2, NT, DH], R_T)
    cs_raw = sb("cs_raw", [P, 2, NT, DH], R_T + 4 * NT * DH * 4)
    rot1 = sb("rot1", [P, HALF], R_T + 6 * NT * DH * 4)
    rot2 = sb("rot2", [P, HALF], R_T + 6 * NT * DH * 4 + HALF * 4)
    sq = sb("sq", [P, 2, HALF], R_T + 6 * NT * DH * 4 + 2 * HALF * 4)
    g_qk = sb("g_qk", [P, 2, DH], R_T + 6 * NT * DH * 4 + 4 * HALF * 4)
    gv_row = sb("gv_row", [P, GV], R_T + 6 * NT * DH * 4 + 4 * HALF * 4 + 2 * DH * 4)
    NSTAT = NT * (AH + KVH)
    ident = sb("ident", [P, P], R_S)
    mask = sb("mask", [P, NMASK, P], R_S + P * 4, U8)
    st = sb("st", [P, 5, NSTAT], R_S + P * 4 + NMASK * P)
    bg = sb("bg", [P, 2, GH], R_S + P * 4 + NMASK * P + 5 * NSTAT * 4)
    bg_fix = sb("bg_fix", [P, 2], R_S + P * 4 + NMASK * P + 5 * NSTAT * 4 + 32)
    ps = nc.alloc_psum_tensor("ps", [P, 8 * HALF], F32)

    def bank(b, n=HALF):
        return ps[:, b * HALF:b * HALF + n]

    def view_ps(start, *dims):
        return bass.AP(ps, start, [[8 * HALF, P]] + [list(d) for d in dims])

    def nmax(n, i):
        return st[:, 0, 2 * (n % 2) + i:2 * (n % 2) + i + 1]

    def den(h, t):
        return st[:, 1, h % 2 * NT + t:h % 2 * NT + t + 1]

    s = Semaphores(nc)

    def phase_end(eng, at, own):
        eng.drain().then_inc(own, 1)
        if own is not s.pe_phase:
            eng.wait_ge(s.pe_phase, at("pe_phase"))
        if own is not s.act_phase:
            eng.wait_ge(s.act_phase, at("act_phase"))
        if own is not s.dve_phase:
            eng.wait_ge(s.dve_phase, at("dve_phase"))
        if own is not s.pool_phase:
            eng.wait_ge(s.pool_phase, at("pool_phase"))
        eng.sem_inc(s.passed, 1)

    with nc.Block() as block:

        @block.sync
        def _(sp):
            at = Counts("sync", sp)
            sp.dma_start(x[:, 0:NTP, :], x_prompt.rearrange("b (t p) d -> p (b t) d", p=P)).then_inc(s.x_in, 16)
            sp.dma_start(x[:, NTP:NT, :], x_sample.rearrange("b (t p) d -> p (b t) d", p=P)).then_inc(s.x_in, 16)
            sp.dma_start(ident[:], identity).then_inc(s.x_in, 16)
            sp.dma_start(mask_raw[:], masks).then_inc(s.x_in, 16)

            def load_group(w, layer, col, width=HALF, blocks=KT):
                ld = w.shape[2]
                for k in range(blocks):
                    sp.wait_ge(s.w_lo_done, at("w_lo_done"))
                    src = bass.AP(w.tensor, layer * (D * ld) + col + k * P * ld, [[ld, P], [1, width]])
                    sp.dma_start(w_raw[:, k % RING, 0:width], src).then_inc(s.w_slot[k % RING], 16)

            with at.repeat(DEPTH, "layer") as layer:
                load_group(w_in, layer, C_GATES, P)
                with at.repeat(4, "gla projections") as g:
                    load_group(w_in, layer, g * HALF + C_QKV)
                with at.repeat(GH, "gla background") as h:
                    for i in range(2):
                        load_group(w_in, layer, h * (2 * BGW) + C_QB + i * BGW, BGW)
                for i in range(2):
                    load_group(w_in, layer, C_ZB + (2 + i) * BGW, BGW)
                with at.repeat(4, "rope background") as i:
                    load_group(w_in, layer, i * BGW + C_ZA, BGW)
                with at.repeat(KVH, "attention background") as g:
                    for i in range(2):
                        load_group(w_in, layer, g * (2 * BGW) + C_MA + i * BGW, BGW)
                for w, name in ((w_branch_a, "gla branch"), (w_branch_b, "attention branch"), (w_out, "output")):
                    with at.repeat(2, name) as g:
                        load_group(w, layer, g * HALF)
            load_group(w_in, 0, C_GATES, P, blocks=SKEW)
            sp.wait_ge(s.y_ready, at("y_ready", NT))
            sp.dma_start(y_prompt.rearrange("b (t p) d -> p (b t) d", p=P), y_out[:, 0:NTP, :]).then_inc(s.out_done, 16)
            sp.dma_start(y_sample.rearrange("b (t p) d -> p (b t) d", p=P), y_out[:, NTP:NT, :]).then_inc(s.out_done, 16)
            sp.wait_ge(s.out_done, 32)

        @block.tensor
        def _(pe):
            at = Counts("tensor", pe, w_lo_done=RING, drained=8)
            mm = nc.tensor.matmul

            def three_passes(out, s_hi, s_lo, m_hi, m_lo, first, last):
                mm(out, s_hi, m_hi, start=first, stop=False)
                mm(out, s_hi, m_lo, start=False, stop=False)
                return mm(out, s_lo, m_hi, start=False, stop=last)

            def gemm_tokens(a_hi, a_lo):
                for k in range(KT):
                    pe.wait_ge(s.w_lo_done, at("w_lo_done"))
                    for t in range(NT):
                        if k == 0:
                            pe.wait_ge(s.drained, at.peek("drained", t + 1 - NT))
                        tok = slice(t * P, (t + 1) * P)
                        last = three_passes(bank(t), a_hi[:, k, tok], a_lo[:, k, tok], w_hi[:, k % RING, :],
                                            w_lo[:, k % RING, :], k == 0, k == KT - 1)
                        if k == KT - 1:
                            last.then_inc(s.gemm_ready, 1)
                    (last if k < KT - 1 else pe.drain()).then_inc(s.w_used, 1)
                at.skip("drained", NT)

            def background(start, stop, bank0=BG_BANK, spare=0):
                for u in range(start, stop):
                    i, t = divmod(u, NT)
                    k = i % KT
                    if t == 0:
                        pe.wait_ge(s.w_lo_done, at("w_lo_done"))
                    if k == 0 and t % 2 == 0:
                        pe.wait_ge(s.bg_free, at.peek("bg_free", 1 - 3 * spare))
                        at.skip("bg_free", 1)
                    out = ps[:, bank0 * HALF + t * BGW:bank0 * HALF + (t + 1) * BGW]
                    tok = slice(t * P, (t + 1) * P)
                    mm(out, act_hi[:, k, tok], w_hi[:, k % RING, 0:BGW], start=(k == 0 and t % 2 == 0), stop=False, skip_group_check=True)
                    mm(out, act_hi[:, k, tok], w_lo[:, k % RING, 0:BGW], start=False, stop=False, skip_group_check=True)
                    last = mm(out, act_lo[:, k, tok], w_hi[:, k % RING, 0:BGW], start=False, stop=(k == KT - 1), skip_group_check=True)
                    if t == NT - 1:
                        last.then_inc(s.w_used, 1)

            def gemm_features(blocks):
                for k in range(KT):
                    pe.wait_ge(s.w_lo_done, at("w_lo_done"))
                    for b in range(8 - 2 * blocks, 8):
                        if k == 0:
                            pe.wait_ge(s.drained, at.peek("drained", b + 1 - 8))
                        col = slice((b // 2 + blocks - 4) * P, (b // 2 + blocks - 3) * P)
                        tok = slice(b % 2 * FH, (b % 2 + 1) * FH)
                        last = three_passes(bank(b, FH), w_hi[:, k % RING, col], w_lo[:, k % RING, col],
                                            act_hi[:, k, tok], act_lo[:, k, tok], k == 0, k == KT - 1)
                        if k == KT - 1:
                            last.then_inc(s.gemm_ready, 1)
                    (last if k < KT - 1 else pe.drain()).then_inc(s.w_used, 1)
                at.skip("drained", 2 * blocks)

            def turn(src, scaled=False):
                for n in range(2 * NT):
                    t = n // 2
                    if scaled and n % 2 == 0:
                        pe.wait_ge(s.hn_ready, at("hn_ready"))
                    pe.wait_ge(s.turn_free, at("turn_free"))
                    for j in range(4):
                        k = n % 2 * 4 + j
                        last = nc.tensor.transpose(ps[:, n % 4 * HALF + j * P:n % 4 * HALF + (j + 1) * P],
                                                   src(t)[:, k * P:(k + 1) * P], ident[:])
                    last.then_inc(s.turned, 1)

            def gla_gates():
                pe.wait_ge(s.prod_free, at("prod_free"))
                pe.wait_ge(s.gla_fix, at("gla_fix"))
                for b in range(4):
                    last = mm(bank(b, FH), wg_fix[:, b // 2, :], gl_t[:, b % 2 * FH:(b % 2 + 1) * FH], start=True, stop=True)
                last.then_inc(s.gate_ready, 1)

            def gla_levels(h, done):
                for n in range(GLA_STEPS):
                    if n > 0:
                        pe.wait_ge(s.prod_free, at("prod_free"))
                    li = max(n - 1, 0)
                    if n != 1:
                        pe.wait_ge(s.q_ready, at("q_ready"))
                        pe.wait_ge(s.k_ready, at("k_ready"))
                    kk = view(qk, (li % 2) * 2 * TOK + TOK, (1, TOK))
                    qq = view(qk, (li % 2) * 2 * TOK, (1, TOK))
                    span = LEVELS[li]
                    if span == 256:
                        for j in range(NTP):
                            i0 = 2 * P if j < 2 else 0
                            last = mm(ps[:, j * 2 * P:(j + 1) * 2 * P], kk[:, j * P:(j + 1) * P],
                                      qq[:, i0:i0 + 2 * P], start=True, stop=True)
                    else:
                        for j in range(NT):
                            i = j ^ 1 if span == 128 else j
                            rhs = view(qk_t, h * (2 * TOK) + i * P, (1, P)) if n == 0 else qq[:, i * P:(i + 1) * P]
                            last = mm(ps[:, j * P:(j + 1) * P], kk[:, j * P:(j + 1) * P], rhs, start=True, stop=True)
                    last.then_inc(s.prod, 1)
                    background(done[n - 1] if n else GLA_FIRST, done[n])

            def gla_values(h):
                pe.wait_ge(s.a_ready, at("a_ready"))
                for i in range(NT):
                    out = ps[:, 2 * HALF + i * GV:2 * HALF + (i + 1) * GV]
                    terms = [(amat[:, i, :], i), (aoff1[:, i ^ 1, :], i ^ 1)]
                    if i < NTP:
                        terms += [(aoff2[:, j, i % 2, :], j) for j in ((2, 3) if i < 2 else (0, 1))]
                    for n, (a, j) in enumerate(terms):
                        last = mm(out, a, view(va, h * GV + j * D, (1, GV)), start=(n == 0), stop=(n == len(terms) - 1))
                last.then_inc(s.gla_o, 1)

            def attention_group():
                def turn_stack(stage, col, tiles):
                    for t in tiles:
                        last = nc.tensor.transpose(ps[:, col + (t - tiles[0]) * P:col + (t - tiles[0] + 1) * P],
                                                   stage(t).bitcast(F32), ident[:])
                    return last

                def q_turn_first(h):
                    pe.wait_ge(s.q_staged, at("q_staged"))
                    turn_stack(lambda t: view(q_st, h % 2 * TOK + t * P, (1, P)), 4 * HALF, range(4)).then_inc(s.q_turned, 1)

                def q_turn_second(h):
                    pe.wait_ge(s.q_stack, at("q_stack"))
                    turn_stack(lambda t: view(q_st, h % 2 * TOK + t * P, (1, P)), 4 * HALF, range(4, NT)).then_inc(s.q_turned, 1)

                def scores(n):
                    h, u = divmod(n, UNITS)
                    if u == 0:
                        pe.wait_ge(s.q_stack, at("q_stack"))
                    out = bank(n % 2)
                    if u < NTP:
                        parts = [(out, u, slice(0, SEQS[0]))]
                    else:
                        parts = [(out[:, i * 256:(i + 1) * 256], NTP + i, slice(SEQS[0], TOK)) for i in range(2)]
                    for o, t, keys in parts:
                        lhs = q_hl[:, h % 2, t * P:(t + 1) * P]
                        mm(o, lhs, k_hh[:, keys], start=True, stop=False)
                        last = mm(o, lhs, k_ll[:, keys], start=False, stop=True)
                    last.then_inc(s.score, 1)

                def turn_p(n):
                    pe.wait_ge(s.exp_done, at("exp_done"))
                    for j in range(4):
                        last = nc.tensor.transpose(ps[:, 2 * HALF + j * P:2 * HALF + (j + 1) * P],
                                                   pr[:, n % 2, j * P:(j + 1) * P], ident[:])
                    last.then_inc(s.pr_turned, 1)

                def values(n):
                    h, u = divmod(n, UNITS)
                    if n == 0:
                        pe.wait_ge(s.v_ready, at("v_ready"))
                    pe.wait_ge(s.pr_t_ready, at("pr_t_ready"))
                    if u == 0:
                        pe.wait_ge(s.o_drained, at("o_drained"))
                    for i in range(1 if u < NTP else 2):
                        t = u + i
                        nk = 4 if u < NTP else 2
                        for j in range(nk):
                            key = j if u < NTP else NTP + j
                            last = mm(ps[:, 3 * HALF + t * DH:3 * HALF + (t + 1) * DH],
                                      pr_t[:, n % 2, (i * 2 + j) * P:(i * 2 + j + 1) * P], v_grp[:, key, :],
                                      start=(j == 0), stop=(j == nk - 1))
                    last.then_inc(s.pv_done, 1)

                background(0, 8)
                for part in range(2):
                    pe.wait_ge(s.k_staged, at("k_staged"))
                    if part == 1:
                        pe.wait_ge(s.k_stack, at("k_stack"))
                    turn_stack(lambda t: view(k_st, part * TOK + t * P, (1, P)), 0, range(NT)).then_inc(s.k_turned, 1)
                    background(8 + part * 3, 11 + part * 3)
                    if part == 0:
                        q_turn_first(0)
                q_turn_second(0)
                background(14, 16)
                pe.wait_ge(s.k_stack, at("k_stack"))
                total = GROUP * UNITS
                scores(0)
                background(16, ATT_FIRST)
                for n in range(total):
                    h = n // UNITS + 1
                    if n % UNITS == 1 and h < GROUP:
                        q_turn_first(h)
                    if n % UNITS == 2 and h < GROUP:
                        q_turn_second(h)
                    if n + 1 < total:
                        scores(n + 1)
                    turn_p(n)
                    background(ATT_DONE[n - 1] if n else ATT_FIRST, ATT_DONE[n])
                    values(n)

            pe.sem_inc(s.w_used, RING)
            pe.wait_ge(s.x_in, at("x_in", 64))
            with at.repeat(DEPTH, "layer"):
                turn(lambda t: hn[:, t % 2, :], scaled=True)
                phase_end(pe, at, s.pe_phase)
                gemm_features(1)
                with at.repeat(2, "gla qk"):
                    gemm_features(4)
                with at.repeat(2, "gla v"):
                    gemm_tokens(act_hi, act_lo)
                phase_end(pe, at, s.pe_phase)
                gla_gates()
                background(0, GLA_FIRST)
                pe.wait_ge(s.gate_used, at("gate_used"))
                pe.sem_inc(s.passed, 1)
                with at.repeat(GH - 1, "gla head") as h:
                    gla_levels(h, GLA_DONE)
                    gla_gates()
                    background(GLA_DONE[-1], GLA_DONE[-1] + GLA_MID)
                    pe.wait_ge(s.gate_used, at("gate_used"))
                    gla_values(h)
                    background(GLA_DONE[-1] + GLA_MID, BG_TILES + GLA_FIRST)
                gla_levels(GH - 1, GLA_LAST_DONE)
                gla_values(GH - 1)
                phase_end(pe, at, s.pe_phase)
                with at.repeat(3, "rope background"):
                    background(0, KT * NT, spare=1)
                    background(0, KT * NT, BG_BANK - 3, spare=1)
                phase_end(pe, at, s.pe_phase)
                with at.repeat(KVH, "attention group"):
                    attention_group()
                phase_end(pe, at, s.pe_phase)
                turn(lambda t: va[:, t, :])
                phase_end(pe, at, s.pe_phase)
                with at.repeat(2, "gla branch"):
                    gemm_tokens(o_hi, o_lo)
                phase_end(pe, at, s.pe_phase)
                turn(lambda t: q[:, t, :])
                phase_end(pe, at, s.pe_phase)
                with at.repeat(2, "attention branch"):
                    gemm_tokens(act_hi, act_lo)
                phase_end(pe, at, s.pe_phase)
                turn(lambda t: merged[:, t, :])
                phase_end(pe, at, s.pe_phase)
                with at.repeat(2, "output"):
                    gemm_tokens(o_hi, o_lo)
                phase_end(pe, at, s.pe_phase)

        @block.scalar
        def _(act):
            at = Counts("scalar", act, drained=8, bg_free=3)
            act.sem_inc(s.bg_free, 3)
            act.sem_inc(s.stored, 16)
            A = nc.scalar.activation

            def split(k, width=HALF):
                slot = (k + SKEW) % RING
                act.wait_ge(s.w_slot[slot], at(f"w_slot{slot}", 16))
                act.wait_ge(s.w_used, at("w_used"))
                A(w_hi[:, slot, 0:width], w_raw[:, slot, 0:width], ACT.Copy).then_inc(s.w_hi_done, 1)

            def copy_sums(func, bank0):
                for b in range(3):
                    A(stg[:, 2 * b:2 * b + 2, :].rearrange("p a b -> p (a b)"), bank(bank0 + b), func).then_inc(s.bg_free, 1)
                act.wait_ge(s.bg_free, at("bg_free", 3))

            def store(j, bank0=BG_BANK):
                act.wait_ge(s.w_used, at.peek("w_used", 1))
                act.wait_ge(s.stored, at("stored", 16))
                copy_sums(ACT.Copy, bank0)
                act.dma_start(bass.AP(proj, j * (NT * BGW), [[NBG * NT * BGW, P], [1, NT * BGW]]),
                              stg[:].rearrange("p a b -> p (a b)")).then_inc(s.stored, 16)

            def all_stored():
                act.wait_ge(s.stored, at.peek("stored", 16))

            def fetch(dst, j, start, row, n, sem):
                for c in range(n):
                    act.dma_start(view(dst, start + c * BGW, (row, NT), (1, BGW)),
                                  bass.AP(proj, (j + c) * (NT * BGW), [[NBG * NT * BGW, P], [BGW, NT], [1, BGW]])).then_inc(sem, 16)

            def param(dst, src):
                act.dma_start(dst, src).then_inc(s.param, 16)

            def rsqrt_seed(n):
                act.wait_ge(s.stat_v, at("stat_v"))
                A(st[:, 2, 0:n], st[:, 1, 0:n], ACT.Ln).then_inc(s.act_chain, 1)
                act.wait_ge(s.act_chain, at("act_chain"))
                A(st[:, 2, 0:n], st[:, 2, 0:n], ACT.Exp, scale=-0.5).then_inc(s.stat_y0, 1)

            def sum_squares():
                for t in range(NT):
                    last = A(y_out[:, t, :], x[:, t, :], ACT.Square, accum_out=st[:, 0, t:t + 1])
                last.then_inc(s.stat_sum, 1)
                rsqrt_seed(NT)

            def turn_hi(dst):
                for n in range(2 * NT):
                    t, k0 = n // 2, n % 2 * 4
                    act.wait_ge(s.turned, at("turned"))
                    A(dst[:, k0:k0 + 4, t * P:(t + 1) * P],
                                      ps[:, n % 4 * HALF:(n % 4 + 1) * HALF].rearrange("p (a b) -> p a b", a=4), ACT.Copy).then_inc(s.turn_hi, 1)

            def skip_banks(n):
                at.skip("gemm_ready", n)
                at.skip("drained", n)

            def splits():
                for k in range(KT):
                    split(k)

            def gla_gates(first):
                act.wait_ge(s.gla_fix, at("gla_fix"))
                act.wait_ge(s.gate_ready, at("gate_ready"))
                for d in range(2):
                    A(view(lev, (2 + d) * TOK, (FH, 2), (1, FH)), view_ps(d * 2 * HALF, (HALF, 2), (1, FH)),
                      ACT.Abs, bias=bg_fix[:, d:d + 1]).then_inc(s.gate_abs, 1)
                split(first, BGW)
                act.wait_ge(s.gate_abs, at("gate_abs", 2))
                a = view(lev, 2 * TOK, (1, 2 * TOK))
                A(a, a, ACT.Exp, scale=-1.0).then_inc(s.act_chain, 1)
                split(first + 1, BGW)
                act.wait_ge(s.act_chain, at("act_chain"))
                A(a, a, ACT.Ln, bias=1.0).then_inc(s.gate_log, 1)
                split(first + 2, BGW)

            def gla_exp(li):
                n = TOK if LEVELS[li] < 256 else SEQS[0]
                act.wait_ge(s.lev_diff, at("lev_diff"))
                y = view(lev, li % 2 * 2 * TOK, (TOK, 2), (1, n))
                A(y, y, ACT.Exp, scale=1.0 / GATE_NORM).then_inc(s.lev_exp, 1)

            def gla_levels(h, start):
                for li in range(len(LEVELS)):
                    if li > 0:
                        gla_exp(li)
                    if start[KT] == li:
                        store(2 * h)
                    if start.get(2 * KT) == li:
                        store(2 * h + 1)
                    for i in start:
                        if start[i] == li:
                            split(i, BGW)

            def gla_out(h):
                act.wait_ge(s.gla_o, at("gla_o"))
                A(view(va, h * GV, (D, NT), (1, GV)), view_ps(2 * HALF, (GV, NT), (1, GV)), ACT.Copy, scale=GK ** -0.5).then_inc(s.act_chain, 1)
                act.wait_ge(s.act_chain, at("act_chain"))
                for t in range(NT):
                    o = ps[:, 2 * HALF + t * GV:2 * HALF + (t + 1) * GV]
                    last = A(o, o, ACT.Square, scale=GK ** -0.5, accum_out=st[:, 1, t:t + 1])
                last.then_inc(s.act_chain, 1)
                act.wait_ge(s.act_chain, at("act_chain"))
                A(view(st, h, (GH, NT)), st[:, 1, 0:NT], ACT.Copy)

            def attention_group(g):
                def exp_scores(n):
                    h, u = divmod(n, UNITS)
                    act.wait_ge(s.neg_max, at("neg_max"))
                    for i in range(1 if u < NTP else 2):
                        w = HALF if u < NTP else HALF // 2
                        last = A(pr[:, n % 2, i * w:(i + 1) * w], ps[:, n % 2 * HALF + i * w:n % 2 * HALF + (i + 1) * w],
                                 ACT.Exp, bias=nmax(n, i), accum_out=den(h, u + i))
                    act.drain().then_inc(s.exp_done, 1)

                def copy_pt(n):
                    act.wait_ge(s.pr_turned, at("pr_turned"))
                    if n >= 2:
                        act.wait_ge(s.pv_done, at.peek("pv_done", -1))
                    A(pr_t[:, n % 2, :], bank(2), ACT.Copy).then_inc(s.pr_t_ready, 1)
                    at.skip("pv_done", 1)

                def wide_split(i):
                    split(i, BGW if i + SKEW < BG_BLOCKS else HALF)

                A(k_st[:, 0, :, :, :], view(kv, g * DH, (HALF, NT), (0, 2), (1, DH)), ACT.Copy).then_inc(s.k_staged, 1)
                for i in range(3):
                    wide_split(i)
                total = GROUP * UNITS
                exp_scores(0)
                for i in range(3, BG_BLOCKS):
                    if ATT_START[i] < 0:
                        wide_split(i)
                for n in range(total):
                    copy_pt(n)
                    if n + 1 < total:
                        exp_scores(n + 1)
                    for i in range(3, BG_BLOCKS):
                        if ATT_START[i] == n:
                            wide_split(i)
                    if ATT_DONE[n] in (BG_TILES // 2, BG_TILES):
                        store(g * 2 + J_MA + ATT_DONE[n] // BG_TILES)

            act.wait_ge(s.x_in, 64)
            for k in range(SKEW):
                act.wait_ge(s.w_used, at("w_used"))
                act.wait_ge(s.w_slot[k], at(f"w_slot{k}", 16))
                A(w_hi[:, k, 0:P], w_raw[:, k, 0:P], ACT.Copy).then_inc(s.w_hi_done, 1)
            with at.repeat(DEPTH, "layer") as layer:
                param(g_row[:], rows_of(norm_g, layer * D, D))
                for d, b_gate in enumerate((b_gate_f, b_gate_b)):
                    for h in range(GH):
                        param(bg[:, d, h:h + 1], bass.AP(b_gate.tensor, layer * (GH * GK) + h * GK, [[1, P], [1, 1]]))
                sum_squares()
                turn_hi(act_hi)
                phase_end(act, at, s.act_phase)
                param(wg[0:RANK, 0, :], bass.AP(w_gate_f.tensor, layer * (RANK * GH * GK), [[GH * GK, RANK], [1, GH * GK]]))
                param(wg[RANK:2 * RANK, 1, :], bass.AP(w_gate_b.tensor, layer * (RANK * GH * GK), [[GH * GK, RANK], [1, GH * GK]]))
                for k in range(KT):
                    split(k, P if k + SKEW < KT else HALF)
                with at.repeat(4, "gla projections"):
                    splits()
                skip_banks(2 + 2 * 8 + 2 * NT)
                phase_end(act, at, s.act_phase)
                gla_gates(0)
                for i in (3, 4):
                    split(i, BGW)
                gla_exp(0)
                split(5, BGW)
                behind = [i for i in GLA_START if GLA_START[i] >= len(LEVELS)]
                with at.repeat(GH - 1, "gla head") as h:
                    gla_levels(h, GLA_START)
                    for i in behind[:-3]:
                        split(i, BGW)
                    gla_gates(behind[-3])
                    gla_exp(0)
                    gla_out(h)
                gla_levels(GH - 1, GLA_LAST_START)
                for i in GLA_LAST_START:
                    if GLA_LAST_START[i] >= len(LEVELS):
                        split(i, BGW)
                store(2 * GH - 1)
                gla_out(GH - 1)
                phase_end(act, at, s.act_phase)
                all_stored()
                fetch(q, J_Q, 0, D, 4, s.qkv_in)
                fetch(kv, J_K, 0, HALF, 2, s.qkv_in)
                param(gv_row[:], rows_of(gla_norm_g, layer * GV, GV))
                param(cs_raw[:, 0, :, :], rope_cos)
                param(cs_raw[:, 1, :, :], rope_sin)
                param(g_qk[:, 0, :], rows_of(q_norm_g, layer * DH, DH))
                param(g_qk[:, 1, :], rows_of(k_norm_g, layer * DH, DH))
                rsqrt_seed(NT * GH)
                for i in range(6 * KT):
                    split(i % KT, BGW)
                    if i == 8:
                        act.wait_ge(s.qkv_in, at("qkv_in", 6 * 16))
                    if 8 <= i < 8 + 3 * NT // 2:
                        for n in (2 * i - 16, 2 * i - 15):
                            t, part = n // 3, n % 3
                            src = view(q, t * D + part * HALF, (1, HALF)) if part < 2 else view(kv, t * HALF, (1, KVH * DH))
                            act.wait_ge(s.sq_used, at("sq_used"))
                            A(view(sq, n % 2 * HALF, (1, HALF if part < 2 else KVH * DH)), src, ACT.Square).then_inc(s.sq_ready, 1)
                    if i == 8 + 3 * NT // 2:
                        rsqrt_seed(NSTAT)
                    if i % KT == KT - 1:
                        if i < 2 * KT:
                            store(J_ZB + 2 + i // KT, BG_BANK - i // KT % 2 * 3)
                        else:
                            act.wait_ge(s.w_used, at.peek("w_used", 1))
                            if i < 3 * KT:
                                all_stored()
                            else:
                                act.wait_ge(s.sil_used, at("sil_used"))
                            copy_sums(ACT.Silu, BG_BANK - i // KT % 2 * 3)
                            act.sem_inc(s.sil_ready, 1)
                at.skip("sil_used", 1)
                phase_end(act, at, s.act_phase)
                with at.repeat(KVH, "attention group") as g:
                    attention_group(g)
                phase_end(act, at, s.act_phase)
                all_stored()
                fetch(ma, J_MA, 0, D, 4, s.gates_in)
                fetch(zb, J_ZB, 0, D, 4, s.gates_in)
                turn_hi(o_hi)
                phase_end(act, at, s.act_phase)
                act.wait_ge(s.gates_in, at("gates_in", 8 * 16))
                with at.repeat(2, "gla branch") as g:
                    for k in range(KT):
                        split(k)
                        if k in (1, 2):
                            some = view(ma, g * HALF + (k - 1) * (NT // 2) * D, (D, NT // 2), (1, HALF))
                            A(some, some, ACT.Sigmoid).then_inc(s.sig_ready, 1)
                        if k in (4, 5):
                            some = view(zb, g * HALF + (k - 4) * (NT // 2) * D, (D, NT // 2), (1, HALF))
                            A(some, some, ACT.Silu).then_inc(s.zb_ready, 1)
                skip_banks(2 * NT)
                phase_end(act, at, s.act_phase)
                turn_hi(act_hi)
                phase_end(act, at, s.act_phase)
                fetch(mb, J_MB, 0, D, 4, s.gates_in)
                act.wait_ge(s.gates_in, at("gates_in", 4 * 16))
                with at.repeat(2, "attention branch") as g:
                    for k in range(KT):
                        split(k)
                        if k in (3, 5):
                            some = view(mb, g * HALF + (k // 2 - 1) * (NT // 2) * D, (D, NT // 2), (1, HALF))
                            A(some, some, ACT.Sigmoid).then_inc(s.sig_ready, 1)
                skip_banks(2 * NT)
                phase_end(act, at, s.act_phase)
                turn_hi(o_hi)
                phase_end(act, at, s.act_phase)
                splits()
                for k in range(KT):
                    split(k, HALF if k + SKEW < KT else P)
                skip_banks(2 * NT)
                phase_end(act, at, s.act_phase)
            param(g_row[:], rows_of(final_norm_g, 0, D))
            sum_squares()

        @block.gpsimd
        def _(pool):
            at = Counts("gpsimd", pool)
            G = nc.gpsimd

            def split(k, width=HALF):
                slot = (k + SKEW) % RING
                pool.wait_ge(s.w_hi_done, at("w_hi_done"))
                G.tensor_tensor(w_lo[:, slot, 0:width], w_raw[:, slot, 0:width],
                                                  w_hi[:, slot, 0:width].bitcast(F32), ALU.subtract).then_inc(s.w_lo_done, 1)

            def splits():
                for k in range(KT):
                    split(k)

            def phase_ends(n=1):
                for _ in range(n):
                    phase_end(pool, at, s.pool_phase)

            def gla_fix(h):
                G.tensor_copy(wg_fix[:], view_32(wg, h * GK, (GH * GK, 2), (1, GK)))
                G.tensor_copy(bg_fix[:], view(bg, h, (GH, 2)))
                pool.drain().then_inc(s.gla_fix, 1)

            def gla_levels(h, start, more):
                for li, span in enumerate(LEVELS):
                    n = TOK if span < 256 else SEQS[0]
                    pool.wait_ge(s.lev_exp, at("lev_exp"))
                    if li == 2:
                        pool.wait_ge(s.prod, at("prod", 2))
                    elif li > 2:
                        pool.wait_ge(s.prod, at("prod"))
                    pool.sem_inc(s.passed, 1)
                    G.tensor_tensor(view(qk, (li % 2 * 2 + 1) * TOK, (1, n)), view(lev, (li % 2 * 2 + 1) * TOK, (1, n)),
                                    view(qk_t, h * (2 * TOK) + TOK, (1, n)), ALU.mult).then_inc(s.k_ready, 1)
                    if more and li == 4:
                        gla_fix(h + 1)
                    for i in start:
                        if start[i] == li:
                            split(i, BGW)
                at.skip("prod", 2)
                for i in start:
                    if start[i] >= len(LEVELS):
                        split(i, BGW)

            def view_32(t, start, *dims):
                return bass.AP(t, start, [[2 * GH * GK, 2 * RANK]] + [list(d) for d in dims])

            def rope_swapped(n):
                t, part = n // 3, n % 3
                heads = 8 if part < 2 else KVH
                src, row = (q, t * D + part * HALF) if part < 2 else (kv, t * HALF)
                pool.wait_ge(s.rot2_free, at("rot2_free"))
                for half in range(2):
                    G.tensor_tensor(
                        view(rot2, half * 16, (DH, heads), (32, 2), (1, 16)),
                        view(src, row + (1 - half) * 16, (DH, heads), (32, 2), (1, 16)),
                        view(cs, ((part == 2) * 2 + 1) * NT * DH + t * DH + half * 16, (0, heads), (32, 2), (1, 16)),
                        ALU.mult)
                pool.drain().then_inc(s.rot2_ready, 1)

            def attention_group(g):
                pool.wait_ge(s.group_free, at("group_free"))
                pool.sem_inc(s.passed, 1)
                def stage_q(h):
                    if h >= 2:
                        pool.wait_ge(s.q_turned, at("q_turned", 2))
                    q_src = view(q, g * (GROUP * DH) + h * DH, (D, NT), (1, DH))
                    G.tensor_copy(q_st[:, h % 2, :, 0, :], q_src).then_inc(s.pool_chain, 1)
                    pool.wait_ge(s.pool_chain, at("pool_chain"))
                    pool.sem_inc(s.passed, 1)
                    G.tensor_tensor(q_st[:, h % 2, :, 1, :], q_src,
                                    q_st[:, h % 2, :, 0, :].bitcast(F32), ALU.subtract).then_inc(s.q_staged, 1)

                stage_q(0)
                stage_q(1)
                pool.wait_ge(s.group_free, at("group_free"))
                pool.sem_inc(s.passed, 1)
                G.tensor_copy(v_grp[:], view(kv, KVH * DH + g * DH, (HALF, NT), (1, DH))).then_inc(s.v_ready, 1)
                h = 2
                for i in range(BG_BLOCKS):
                    if h < GROUP and (i == 3 if h == 2 else ATT_START[i] > 2):
                        stage_q(h)
                        h += 1
                    split(i, BGW if i + SKEW < BG_BLOCKS else HALF)
                assert h == GROUP
                at.skip("q_turned", 4)

            pool.sem_inc(s.w_lo_done, RING)
            for k in range(SKEW):
                split(k - SKEW, P)
            with at.repeat(DEPTH, "layer"):
                G.memset(wg[:], 0.0)
                phase_ends()
                for k in range(KT):
                    split(k, P if k + SKEW < KT else HALF)
                with at.repeat(4, "gla projections"):
                    splits()
                phase_ends()
                gla_fix(0)
                for i in range(GLA_FIRST // NT):
                    split(i, BGW)
                with at.repeat(GH - 1, "gla head") as h:
                    gla_levels(h, GLA_START, True)
                gla_levels(GH - 1, GLA_LAST_START, False)
                phase_ends()
                for i in range(6 * KT):
                    if i == 12:
                        pool.wait_ge(s.tables, at("tables"))
                        pool.wait_ge(s.qkv_in, at("qkv_in", 6 * 16))
                    if i >= 12 and i % 2 == 0:
                        rope_swapped((i - 12) // 2)
                    split(i % KT, BGW)
                phase_ends()
                with at.repeat(KVH, "attention group") as g:
                    attention_group(g)
                phase_ends(2)
                with at.repeat(2, "gla branch"):
                    splits()
                phase_ends(2)
                with at.repeat(2, "attention branch"):
                    splits()
                phase_ends(2)
                splits()
                for k in range(KT):
                    split(k, HALF if k + SKEW < KT else P)
                phase_ends()

        @block.vector
        def _(dve):
            at = Counts("vector", dve, prod_free=1, rot2_free=1)
            V = nc.vector

            def rsqrt_of(n, size, dst, settled=False):
                if not settled:
                    dve.drain().then_inc(s.dve_chain, 1)
                    dve.wait_ge(s.dve_chain, at("dve_chain"))
                V.tensor_scalar(st[:, 1, 0:n], st[:, 0, 0:n], 1.0 / size, EPS, ALU.mult, ALU.add).then_inc(s.stat_v, 1)
                dve.wait_ge(s.stat_y0, at("stat_y0"))
                V.tensor_tensor(st[:, 3, 0:n], st[:, 2, 0:n], st[:, 2, 0:n], ALU.mult).then_inc(s.dve_chain, 1)
                dve.wait_ge(s.dve_chain, at("dve_chain"))
                V.tensor_tensor(st[:, 3, 0:n], st[:, 3, 0:n], st[:, 1, 0:n], ALU.mult).then_inc(s.dve_chain, 1)
                dve.wait_ge(s.dve_chain, at("dve_chain"))
                V.tensor_scalar(st[:, 3, 0:n], st[:, 3, 0:n], -0.5, 1.5, ALU.mult, ALU.add).then_inc(s.dve_chain, 1)
                dve.wait_ge(s.dve_chain, at("dve_chain"))
                V.tensor_tensor(dst, st[:, 3, 0:n], st[:, 2, 0:n], ALU.mult).then_inc(s.dve_chain, 1)
                dve.wait_ge(s.dve_chain, at("dve_chain"))

            def scaled_tokens(t):
                V.scalar_tensor_tensor(hn[:, t % 2, :], x[:, t, :], st[:, 4, t:t + 1], g_row[:],
                                                        ALU.mult, ALU.mult).then_inc(s.hn_ready, 1)

            def turn_lo(hi, lo, steps=range(2 * NT)):
                for n in steps:
                    t, k0 = n // 2, n % 2 * 4
                    dve.wait_ge(s.turn_hi, at("turn_hi"))
                    V.tensor_tensor(
                        lo[:, k0:k0 + 4, t * P:(t + 1) * P],
                        ps[:, n % 4 * HALF:(n % 4 + 1) * HALF].rearrange("p (a b) -> p a b", a=4),
                        hi[:, k0:k0 + 4, t * P:(t + 1) * P].bitcast(F32), ALU.subtract).then_inc(s.turn_free, 1)

            def normalise(params):
                dve.wait_ge(s.stat_sum, at("stat_sum"))
                rsqrt_of(NT, D, st[:, 4, 0:NT], settled=True)
                dve.wait_ge(s.param, at("param", 16 * params))
                dve.sem_inc(s.passed, 1)

            def gla_gates():
                dve.wait_ge(s.gla_fix, at("gla_fix"))
                dve.wait_ge(s.gate_ready, at("gate_ready"))
                for d in range(2):
                    dve.wait_ge(s.gate_abs, at("gate_abs"))
                    V.tensor_scalar(view(lev, d * TOK, (FH, 2), (1, FH)), view_ps(d * 2 * HALF, (HALF, 2), (1, FH)),
                                    bg_fix[:, d:d + 1], 0.0, ALU.add, ALU.min)
                dve.drain().then_inc(s.gate_used, 1)
                dve.wait_ge(s.gate_used, at("gate_used"))
                V.memset(view(ce, TOK, (SEQS[0], 2)), 0.0).then_inc(s.dve_chain, 1)
                dve.wait_ge(s.dve_chain, at("dve_chain"))
                dve.wait_ge(s.gate_log, at("gate_log"))
                for d in range(2):
                    for start, n in ((0, SEQS[0]), (SEQS[0], SEQS[1])):
                        V.tensor_tensor_scan(view(ce, d * TOK + start + d, (1, n - d)),
                                             view(lev, d * TOK + start, (1, n - d)),
                                             view(lev, (2 + d) * TOK + start, (1, n - d)), 0.0, ALU.add, ALU.subtract)
                dve.drain().then_inc(s.dve_chain, 1)
                dve.wait_ge(s.dve_chain, at("dve_chain"))

                differences(0)

            def differences(li):
                span = LEVELS[li]
                nb = (TOK if span < 256 else SEQS[0]) // (2 * span)
                base = li % 2 * 2 * TOK
                blocks, within, mid = (2 * span, nb), (1, span), (0, span)
                ref = view(ce, span - 1, (TOK + 1, 2), blocks, mid)
                V.tensor_tensor(view(lev, base + span, (TOK, 2), blocks, within),
                                view(ce, span, (TOK, 2), blocks, within), ref, ALU.subtract)
                V.tensor_tensor(view(lev, base + TOK, (-TOK, 2), blocks, within), ref,
                                                 view(ce, 0, (TOK, 2), blocks, within), ALU.subtract).then_inc(s.lev_diff, 1)

            def scaled(li, h):
                n = TOK if LEVELS[li] < 256 else SEQS[0]
                dve.wait_ge(s.lev_exp, at("lev_exp"))
                V.tensor_tensor(view(qk, li % 2 * 2 * TOK, (1, n)), view(lev, li % 2 * 2 * TOK, (1, n)),
                                view(qk_t, h * (2 * TOK), (1, n)), ALU.mult).then_inc(s.q_ready, 1)

            def collect(n):
                dve.wait_ge(s.prod, at("prod"))
                dve.sem_inc(s.passed, 1)
                if n == 0:
                    last = V.tensor_copy(amat[:], ps[:, 0:TOK].rearrange("p (a b) -> p a b", a=NT))
                elif n <= NMASK:
                    last = V.copy_predicated(amat[:], mask[:, n - 1, :].unsqueeze(1).to_broadcast([P, NT, P]),
                                             ps[:, 0:TOK].rearrange("p (a b) -> p a b", a=NT))
                elif n == NMASK + 1:
                    last = V.tensor_copy(aoff1[:], ps[:, 0:TOK].rearrange("p (a b) -> p a b", a=NT))
                else:
                    last = V.tensor_copy(aoff2[:], ps[:, 0:2 * HALF].rearrange("p (a b c) -> p a b c", a=NTP, b=2))
                last.then_inc(s.prod_free, 1)
                dve.wait_ge(s.prod_free, at("prod_free"))
                if n == len(LEVELS):
                    dve.sem_inc(s.passed, 1)

            def gla_levels(h):
                nl = len(LEVELS)
                for li in range(nl):
                    if li + 1 < nl:
                        if li >= 1:
                            dve.wait_ge(s.k_ready, at("k_ready"))
                        differences(li + 1)
                    scaled(li, h)
                    collect(li)
                at.skip("k_ready", 2)
                collect(nl)
                dve.drain().then_inc(s.a_ready, 1)

            def drain_banks(write):
                for t in range(NT):
                    dve.wait_ge(s.gemm_ready, at("gemm_ready"))
                    write(t).then_inc(s.drained, 1)

            def merge(g, add):
                m = mb if add else ma
                if not add:
                    for some in range(2):
                        dve.wait_ge(s.zb_ready, at("zb_ready"))
                        out = view(q, g * HALF + some * (NT // 2) * D, (D, NT // 2), (1, HALF))
                        V.tensor_tensor(out, out, view(zb, g * HALF + some * (NT // 2) * D, (D, NT // 2), (1, HALF)), ALU.mult)
                dve.wait_ge(s.sig_ready, at("sig_ready", 2))
                for t in range(NT):
                    dve.wait_ge(s.gemm_ready, at("gemm_ready"))
                    out = view(merged, t * D + g * HALF, (1, HALF))
                    sig = view(m, t * D + g * HALF, (1, HALF))
                    if add:
                        V.tensor_tensor(sig, bank(t), sig, ALU.mult).then_inc(s.dve_chain, 1)
                        dve.wait_ge(s.dve_chain, at("dve_chain"))
                        last = V.tensor_tensor(out, out, sig, ALU.add)
                    else:
                        last = V.tensor_tensor(out, bank(t), sig, ALU.mult)
                    last.then_inc(s.drained, 1)

            def rope_tables():
                for i in range(2):
                    for half in range(2):
                        V.tensor_tensor(view(cs, i * 2 * NT * DH + half * 16, (DH, NT), (32, 2), (1, 16)),
                                        view(cs_raw, half * 16, (DH, NT), (32, 2), (1, 16)),
                                        view(g_qk, i * DH + half * 16, (0, NT), (32, 2), (1, 16)), ALU.mult)
                        V.tensor_tensor(view(cs, (i * 2 + 1) * NT * DH + half * 16, (DH, NT), (32, 2), (1, 16)),
                                        view(cs_raw, NT * DH + half * 16, (DH, NT), (32, 2), (1, 16)),
                                        view(g_qk, i * DH + (1 - half) * 16, (0, NT), (32, 2), (1, 16)), ALU.mult)
                dve.drain().then_inc(s.tables, 1)
                dve.wait_ge(s.tables, at("tables"))

            def square_sums():
                for n in range(3 * NT):
                    t, part = n // 3, n % 3
                    heads = 8 if part < 2 else KVH
                    stat = t * AH + part * 8 if part < 2 else NT * AH + t * KVH
                    dve.wait_ge(s.sq_ready, at("sq_ready"))
                    V.tensor_reduce(view(st, stat, (1, heads)), view(sq, n % 2 * HALF, (DH, heads), (1, DH)),
                                    AX.X, ALU.add).then_inc(s.sq_used, 1)

            def gate_columns(c):
                dve.wait_ge(s.sil_ready, at("sil_ready"))
                out = view(va, c * BGW, (D, NT), (1, BGW))
                V.tensor_tensor(out, out, stg[:], ALU.mult).then_inc(s.sil_used, 1)

            def rope(n):
                t, part = n // 3, n % 3
                heads = 8 if part < 2 else KVH
                src, row = (q, t * D + part * HALF) if part < 2 else (kv, t * HALF)
                stat = t * AH + part * 8 if part < 2 else NT * AH + t * KVH
                data = view(src, row, (DH, heads), (1, DH))
                turned = view(rot1, 0, (DH, heads), (1, DH))
                V.tensor_tensor(turned, data, view(cs, (part == 2) * 2 * NT * DH + t * DH, (0, heads), (1, DH)),
                                ALU.mult).then_inc(s.dve_chain, 1)
                dve.wait_ge(s.dve_chain, at("dve_chain"))
                dve.wait_ge(s.rot2_ready, at("rot2_ready"))
                V.tensor_tensor(turned, turned, view(rot2, 0, (DH, heads), (1, DH)), ALU.add).then_inc(s.dve_chain, 1)
                dve.wait_ge(s.dve_chain, at("dve_chain"))
                V.tensor_tensor(data, turned, view(st, 4 * NSTAT + stat, (1, heads), (0, DH)), ALU.mult).then_inc(s.rot2_free, 1)
                dve.wait_ge(s.rot2_free, at("rot2_free"))

            def attention_group(g):
                def stack_q(h, first):
                    dve.wait_ge(s.q_turned, at("q_turned"))
                    start, n = (0, 4 * P) if first else (4 * P, 2 * P)
                    V.tensor_copy(q_hl[:, h % 2, start:start + n], bank(4, n)).then_inc(s.q_stack, 1)

                dve.wait_ge(s.k_staged, at("k_staged"))
                V.tensor_tensor(k_st[:, 1, :, :, :], view(kv, g * DH, (HALF, NT), (0, 2), (1, DH)),
                                k_st[:, 0, :, :, :].bitcast(F32), ALU.subtract).then_inc(s.k_staged, 1)
                at.skip("k_staged", 1)
                for part, dst in enumerate((k_hh, k_ll)):
                    dve.wait_ge(s.k_turned, at("k_turned"))
                    V.tensor_copy(dst[:], ps[:, 0:TOK]).then_inc(s.k_stack, 1)
                    if part == 0:
                        stack_q(0, True)

                def row_max(n):
                    h, u = divmod(n, UNITS)
                    dve.wait_ge(s.score, at("score"))
                    k = 1 if u < NTP else 2
                    out = view(st, 2 * (n % 2), (1, k))
                    V.tensor_reduce(out, view_ps(n % 2 * HALF, (HALF // k, k), (1, HALF // k)), AX.X, ALU.max, negate=True).then_inc(s.neg_max, 1)

                def head_out(h):
                    dve.wait_ge(s.pv_done, at.peek("pv_done", 0))
                    V.reciprocal(st[:, 2, 0:NT], st[:, 1, h % 2 * NT:h % 2 * NT + NT]).then_inc(s.dve_chain, 1)
                    dve.wait_ge(s.dve_chain, at("dve_chain"))
                    V.tensor_tensor(view(q, g * (GROUP * DH) + h * DH, (D, NT), (1, DH)),
                                                      view_ps(3 * HALF, (DH, NT), (1, DH)),
                                                      view(st, 2 * NSTAT, (1, NT), (0, DH)), ALU.mult).then_inc(s.o_drained, 1)

                stack_q(0, False)
                total = GROUP * UNITS
                row_max(0)
                for n in range(total):
                    h = n // UNITS + 1
                    if n % UNITS in (1, 2) and h < GROUP:
                        stack_q(h, n % UNITS == 1)
                        if h == GROUP - 1 and n % UNITS == 2:
                            dve.sem_inc(s.group_free, 1)
                    if n + 1 < total:
                        row_max(n + 1)
                    if n % UNITS == 0 and n > 0:
                        head_out(h - 2)
                    at.skip("pv_done", 1)
                head_out(GROUP - 1)
                dve.sem_inc(s.group_free, 1)
            dve.sem_inc(s.drained, 8)
            dve.sem_inc(s.turn_free, 4)
            dve.sem_inc(s.prod_free, 1)
            dve.sem_inc(s.sq_used, 2)
            dve.sem_inc(s.rot2_free, 1)
            dve.sem_inc(s.o_drained, 1)
            dve.sem_inc(s.group_free, 2)
            dve.wait_ge(s.x_in, 64)
            V.tensor_copy(mask[:], mask_raw[:])
            with at.repeat(DEPTH, "layer"):
                normalise(9)
                scaled_tokens(0)
                scaled_tokens(1)
                for t in range(NT):
                    turn_lo(act_hi, act_lo, (2 * t, 2 * t + 1))
                    if t + 2 < NT:
                        scaled_tokens(t + 2)
                phase_end(dve, at, s.dve_phase)
                for half in range(2):
                    dve.wait_ge(s.gemm_ready, at("gemm_ready"))
                    V.tensor_copy(gl_t[:, half * FH:(half + 1) * FH], ps[0:2 * RANK, (6 + half) * HALF:(6 + half) * HALF + FH]).then_inc(s.drained, 1)
                with at.repeat(2, "gla qk") as g:
                    for b in range(8):
                        dve.wait_ge(s.gemm_ready, at("gemm_ready"))
                        V.tensor_copy(view(qk_t, g * TOK + b // 2 * 2 * TOK + b % 2 * FH, (1, FH)), bank(b, FH)).then_inc(s.drained, 1)
                with at.repeat(2, "gla v") as g:
                    drain_banks(lambda t: V.tensor_copy(view(va, t * D + g * HALF, (1, HALF)), bank(t)))
                dve.wait_ge(s.param, at("param", 2 * 16))
                dve.sem_inc(s.passed, 1)
                phase_end(dve, at, s.dve_phase)
                gla_gates()
                with at.repeat(GH - 1, "gla head") as h:
                    gla_levels(h)
                    gla_gates()
                gla_levels(GH - 1)
                phase_end(dve, at, s.dve_phase)
                rsqrt_of(NT * GH, GV, st[:, 4, 0:NT * GH])
                dve.wait_ge(s.param, at("param", 5 * 16))
                dve.sem_inc(s.passed, 1)
                for t in range(NT):
                    for h in range(GH):
                        out = view(va, t * D + h * GV, (1, GV))
                        V.scalar_tensor_tensor(out, out, st[:, 4, t * GH + h:t * GH + h + 1], gv_row[:], ALU.mult, ALU.mult)
                rope_tables()
                square_sums()
                rsqrt_of(NSTAT, DH, st[:, 4, 0:NSTAT])
                V.tensor_scalar(st[:, 4, 0:NT * AH], st[:, 4, 0:NT * AH], DH ** -0.5, None, ALU.mult).then_inc(s.dve_chain, 1)
                dve.wait_ge(s.dve_chain, at("dve_chain"))
                for n in range(3 * NT):
                    rope(n)
                    if n in (7, 11, 15):
                        gate_columns((n - 7) // 4)
                dve.sem_inc(s.passed, 1)
                gate_columns(3)
                phase_end(dve, at, s.dve_phase)
                with at.repeat(KVH, "attention group") as g:
                    attention_group(g)
                phase_end(dve, at, s.dve_phase)
                turn_lo(o_hi, o_lo)
                phase_end(dve, at, s.dve_phase)
                with at.repeat(2, "gla branch") as g:
                    merge(g, False)
                phase_end(dve, at, s.dve_phase)
                turn_lo(act_hi, act_lo)
                phase_end(dve, at, s.dve_phase)
                with at.repeat(2, "attention branch") as g:
                    merge(g, True)
                phase_end(dve, at, s.dve_phase)
                turn_lo(o_hi, o_lo)
                phase_end(dve, at, s.dve_phase)
                with at.repeat(2, "output") as g:
                    def residual(t):
                        out = view(x, t * D + g * HALF, (1, HALF))
                        return V.tensor_tensor(out, out, bank(t), ALU.add)
                    drain_banks(residual)
                phase_end(dve, at, s.dve_phase)
            normalise(1)
            for t in range(NT):
                V.scalar_tensor_tensor(y_out[:, t, :], x[:, t, :], st[:, 4, t:t + 1], g_row[:], ALU.mult, ALU.mult).then_inc(s.y_ready, 1)


INPUTS = ["x_prompt", "x_sample", "norm_g", "w_in", "w_gate_f", "b_gate_f", "w_gate_b", "b_gate_b", "gla_norm_g",
          "q_norm_g", "k_norm_g", "w_branch_a", "w_branch_b", "w_out", "final_norm_g"]


def shape_constants():
    tok = np.arange(P)
    masks = np.zeros((P, NMASK, P), np.float32)
    for li in range(NMASK):
        s = LEVELS[li]
        same = tok[:, None] // (2 * s) == tok[None, :] // (2 * s)
        masks[:, li, :] = same & (tok[:, None] // s != tok[None, :] // s)
    nf = DH // 4
    inv = ROPE_THETA ** (-np.arange(nf, dtype=np.float32) / np.float32(nf))
    place = np.concatenate([np.arange(n) for n in SEQS])
    angles = [(place // GRID_W).astype(np.float32)[:, None] * inv, (place % GRID_W).astype(np.float32)[:, None] * inv]
    cos = np.concatenate([np.cos(a) for a in angles for _ in range(2)], axis=1)
    sin = np.concatenate([sign * np.sin(a) for a in angles for sign in (-1, 1)], axis=1)
    by_tile = lambda a: np.ascontiguousarray(a.astype(np.float32).reshape(NT, P, DH).transpose(1, 0, 2))
    return {"identity": np.eye(P, dtype=np.float32), "masks": masks, "rope_cos": by_tile(cos), "rope_sin": by_tile(sin)}


def kernel(**inputs):
    import concourse.bacc as bacc
    from concourse.bass_utils import run_bass_kernel_spmd

    nc = bacc.Bacc("TRN2", target_bir_lowering=False, num_devices=1)
    arrays = {name: np.ascontiguousarray(inputs[name]) for name in INPUTS} | shape_constants()
    arrays = {f"in_{name}": a for name, a in arrays.items()}
    aps = [nc.dram_tensor(name, a.shape, mybir.dt.from_np(a.dtype), kind="ExternalInput").ap()
           for name, a in arrays.items()]
    outs = [nc.dram_tensor(name, (1, n, D), F32, kind="ExternalOutput").ap()
            for name, n in zip(("y_prompt", "y_sample"), SEQS)]
    trunk(nc, *aps, *outs)
    assert not WRONG, WRONG
    result = run_bass_kernel_spmd(nc, [arrays], core_ids=[0]).results[0]
    return result["y_prompt"], result["y_sample"]
```

```python
from contextlib import contextmanager

import numpy as np

import concourse.bass as bass
from concourse import mybir

F32 = mybir.dt.float32
F32R = mybir.dt.float32r
U8 = mybir.dt.uint8
ALU = mybir.AluOpType
ACT = mybir.ActivationFunctionType
AX = mybir.AxisListType

P = 128
D = 1024
KT = D // P
SEQS = (512, 256)
TOK = sum(SEQS)
NT = TOK // P
NTP = SEQS[0] // P
DEPTH = 2
EPS = 1e-6
HALF = 512
FH = TOK // 2
GH, GK, GV = 4, 128, 256
RANK = 16
GATE_NORM = 16.0
LEVELS = (1, 2, 4, 8, 16, 32, 64, 128, 256)
NMASK = 7
AH, KVH, DH = 16, 4, 64
GROUP = AH // KVH
GRID_W, ROPE_THETA = 64, 10000.0
UNITS = NTP + 1
C_QKV, C_GATES, C_ZA, C_QB, C_ZB, C_MA, C_MB = 0, 2048, 2080, 3104, 4640, 5664, 6688
RING = 4
SKEW = 3
BGW = 256
BG_BANK = 5
J_Q, J_K, J_V, J_ZB, J_MA, J_MB, NBG = 0, 4, 5, 6, 10, 14, 18
BG_BLOCKS = 2 * KT
BG_TILES = BG_BLOCKS * NT

ROPE_BLOCK = 3 * KT


def spread(first, steps, *parts):
    done, at_step = [], 0
    for last, tiles in parts:
        n = last - at_step
        done += [first + -(-(tiles - first) * (i + 1) // n) for i in range(n)]
        at_step, first = last, tiles
    assert len(done) == steps
    return done


def start_steps(block, first, done, blocks):
    return {i: -1 if i * NT < first else next((n for n, d in enumerate(done) if i * NT < d), len(done))
            for i in range(block, block + blocks)}


GLA_FIRST, ATT_FIRST = 6 * NT, 20
GLA_MID, GLA_BEHIND = 9, 9
GLA_LAST_BEHIND = 9
GLA_STEPS = len(LEVELS) + 1
GLA_DONE = spread(GLA_FIRST, GLA_STEPS, (2, KT * NT), (8, BG_TILES),
                  (GLA_STEPS, BG_TILES + GLA_FIRST - GLA_MID - GLA_BEHIND))
GLA_LAST_DONE = spread(GLA_FIRST, GLA_STEPS, (2, KT * NT), (GLA_STEPS, BG_TILES - GLA_LAST_BEHIND))
ATT_DONE = spread(ATT_FIRST, GROUP * UNITS, (7, KT * NT), (GROUP * UNITS, BG_TILES))
ATT_START = start_steps(0, ATT_FIRST, ATT_DONE, BG_BLOCKS)
GLA_START = start_steps(GLA_FIRST // NT, GLA_FIRST, GLA_DONE, BG_BLOCKS)
GLA_LAST_START = start_steps(GLA_FIRST // NT, GLA_FIRST, GLA_LAST_DONE, BG_BLOCKS - GLA_FIRST // NT)

BASE = 16512
R_X = BASE
R_ACT = R_X + NT * D * 4
R_W = R_ACT + 2 * KT * TOK * 4
R_V = R_W + 3 * RING * HALF * 4
R_M = R_V + NT * D * 4
R_O = R_M + NT * D * 4
R_G = R_O + 2 * KT * TOK * 4
R_S = R_G + NT * HALF * 4
ROW = TOK * 4


PER_TURN = {
    "sync gla projections": {
        "w_lo_done": 8},
    "sync gla background": {
        "w_lo_done": 16},
    "sync rope background": {
        "w_lo_done": 8},
    "sync attention background": {
        "w_lo_done": 16},
    "sync gla branch": {
        "w_lo_done": 8},
    "sync attention branch": {
        "w_lo_done": 8},
    "sync output": {
        "w_lo_done": 8},
    "sync layer": {
        "w_lo_done": 264},
    "tensor gla qk": {
        "w_lo_done": 8, "drained": 8},
    "tensor gla v": {
        "w_lo_done": 8, "drained": 6},
    "tensor gla head": {
        "w_lo_done": 16, "prod_free": 10, "gla_fix": 1, "bg_free": 6, "gate_used": 1, "q_ready": 9, "k_ready":
        9, "a_ready": 1},
    "tensor rope background": {
        "w_lo_done": 16, "bg_free": 6},
    "tensor attention group": {
        "w_lo_done": 16, "bg_free": 6, "k_staged": 2, "q_staged": 4, "k_stack": 2, "q_stack": 8, "exp_done": 20,
        "v_ready": 1, "pr_t_ready": 20, "o_drained": 4},
    "tensor layer": {
        "hn_ready": 6, "turn_free": 48, "act_phase": 5, "dve_phase": 5, "pool_phase": 5, "w_lo_done": 264,
        "drained": 66, "prod_free": 40, "gla_fix": 4, "bg_free": 66, "gate_used": 4, "q_ready": 36, "k_ready":
        36, "a_ready": 4, "o_read": 1, "k_staged": 8, "q_staged": 16, "k_stack": 8, "q_stack": 32, "exp_done":
        80, "v_ready": 4, "pr_t_ready": 80, "o_drained": 16, "ob_ready": 1, "merged_ready": 12},
    "scalar gla projections": {
        "w_used": 8, "w_slot0": 32, "w_slot1": 32, "w_slot2": 32, "w_slot3": 32},
    "scalar gla head": {
        "w_used": 16, "w_slot0": 64, "w_slot1": 64, "w_slot2": 64, "w_slot3": 64, "gla_fix": 1, "gate_ready": 1,
        "gate_abs": 2, "act_chain": 3, "lev_diff": 9, "stored": 32, "bg_free": 6, "gla_o": 1},
    "scalar attention group": {
        "w_used": 16, "w_slot0": 64, "w_slot1": 64, "w_slot2": 64, "w_slot3": 64, "stored": 32, "bg_free": 6,
        "neg_max": 20, "pr_turned": 20, "pv_done": 20},
    "scalar layer": {
        "w_used": 264, "w_slot0": 1056, "w_slot1": 1056, "w_slot2": 1056, "stat_v": 3, "turned": 48, "pe_phase":
        5, "dve_phase": 5, "pool_phase": 5, "w_slot3": 1056, "gemm_ready": 66, "drained": 66, "gla_fix": 4,
        "gate_ready": 4, "gate_abs": 8, "act_chain": 12, "lev_diff": 36, "stored": 288, "bg_free": 66, "gla_o":
        4, "qkv_in": 96, "sq_used": 18, "sil_used": 4, "neg_max": 80, "pr_turned": 80, "pv_done": 80, "zb_in":
        64, "m_in0": 64, "m_in1": 64},
    "gpsimd gla projections": {
        "w_hi_done": 8},
    "gpsimd gla head": {
        "w_hi_done": 16, "lev_exp": 9, "prod": 10},
    "gpsimd attention group": {
        "w_hi_done": 16, "group_free": 2, "pool_chain": 4, "q_turned": 8},
    "gpsimd groups": {
        "w_hi_done": 8},
    "gpsimd layer": {
        "w_hi_done": 264, "pe_phase": 5, "act_phase": 5, "dve_phase": 5, "param": 240, "lev_exp": 36, "prod":
        40, "tables": 1, "qkv_in": 96, "rot2_free": 18, "group_free": 8, "pool_chain": 16, "q_turned": 32},
    "vector gla qk": {
        "gemm_ready": 8, "drained": 8},
    "vector gla v": {
        "gemm_ready": 6, "drained": 6},
    "vector gla head": {
        "dve_chain": 2, "gla_fix": 1, "gate_ready": 1, "gate_abs": 2, "gate_used": 1, "gate_log": 1, "lev_exp":
        9, "prod": 10, "prod_free": 10, "k_ready": 9},
    "vector attention group": {
        "dve_chain": 4, "k_staged": 2, "k_turned": 2, "q_turned": 8, "score": 20, "pv_done": 20},
    "vector output": {
        "gemm_ready": 6, "drained": 6},
    "vector layer": {
        "stat_sum": 1, "dve_chain": 79, "stat_root": 3, "g_in": 16, "turn_hi": 48, "pe_phase": 5, "act_phase":
        5, "pool_phase": 5, "gemm_ready": 66, "drained": 66, "param": 240, "gla_fix": 4, "gate_ready": 4,
        "gate_abs": 8, "gate_used": 4, "gate_log": 4, "lev_exp": 36, "prod": 40, "prod_free": 40, "k_ready": 36,
        "tables": 1, "sq_ready": 18, "rot2_ready": 18, "rot2_free": 18, "sil_ready": 4, "k_staged": 8,
        "k_turned": 8, "q_turned": 32, "score": 80, "pv_done": 80, "zb_ready": 4, "sig_ready": 8},
}

WRONG = {}


class Counts:

    def __init__(self, who, eng, **start):
        self.who, self.eng, self.start = who, eng, start
        self.base, self.n = {}, {}

    def __call__(self, name, by=1):
        self.skip(name, by)
        return self.base[name] + self.n[name]

    def skip(self, name, by):
        self.base.setdefault(name, self.start.get(name, 0))
        self.n[name] = self.n.get(name, 0) + by

    def peek(self, name, more):
        self.skip(name, 0)
        return self.base[name] + (self.n[name] + more)

    @contextmanager
    def repeat(self, times, loop):
        per = PER_TURN.get(f"{self.who} {loop}", {})
        with self.eng.Fori(0, times) as i:
            for name in per:
                self.skip(name, 0)
            base, n = dict(self.base), dict(self.n)
            for name, by in per.items():
                self.base[name] = base[name] + n[name] + i * by
                self.n[name] = 0
            yield i
            found = {}
            for name in self.n:
                by = self.n[name] - (0 if name in per else n.get(name, 0))
                if by:
                    found[name] = by
            if found != per:
                WRONG[f"{self.who} {loop}"] = found
        for name in self.n:
            self.base[name] = base.get(name, self.start.get(name, 0))
            self.n[name] = n.get(name, 0) + times * found.get(name, 0)


class Semaphores:

    def __init__(self, nc):
        sem = nc.alloc_semaphore
        self.pe_phase = sem("pe_phase")
        self.act_phase = sem("act_phase")
        self.dve_phase = sem("dve_phase")
        self.pool_phase = sem("pool_phase")
        self.passed = sem("passed")
        self.w_hi_done = sem("w_hi_done")
        self.w_lo_done = sem("w_lo_done")
        self.w_used = sem("w_used")
        self.gemm_ready = sem("gemm_ready")
        self.drained = sem("drained")
        self.bg_free = sem("bg_free")
        self.stored = sem("stored")
        self.sil_ready = sem("sil_ready")
        self.sil_used = sem("sil_used")
        self.qkv_in = sem("qkv_in")
        self.zb_in = sem("zb_in")
        self.m_in = [sem(f"m_in{i}") for i in range(2)]
        self.x_in = [sem(f"x_in{t}") for t in range(NT)]
        self.consts_in = sem("consts_in")
        self.g_in = sem("g_in")
        self.param = sem("param")
        self.y_ready = sem("y_ready")
        self.out_done = sem("out_done")
        self.act_chain = sem("act_chain")
        self.dve_chain = sem("dve_chain")
        self.pool_chain = sem("pool_chain")
        self.stat_sum = sem("stat_sum")
        self.stat_v = sem("stat_v")
        self.stat_root = sem("stat_root")
        self.hn_ready = sem("hn_ready")
        self.turned = sem("turned")
        self.turn_hi = sem("turn_hi")
        self.turn_free = sem("turn_free")
        self.gla_fix = sem("gla_fix")
        self.gate_ready = sem("gate_ready")
        self.gate_abs = sem("gate_abs")
        self.gate_used = sem("gate_used")
        self.gate_log = sem("gate_log")
        self.lev_diff = sem("lev_diff")
        self.lev_exp = sem("lev_exp")
        self.q_ready = sem("q_ready")
        self.k_ready = sem("k_ready")
        self.prod = sem("prod")
        self.prod_free = sem("prod_free")
        self.a_ready = sem("a_ready")
        self.o_read = sem("o_read")
        self.gla_o = sem("gla_o")
        self.ob_ready = sem("ob_ready")
        self.merged_ready = sem("merged_ready")
        self.zb_ready = sem("zb_ready")
        self.sig_ready = sem("sig_ready")
        self.sq_ready = sem("sq_ready")
        self.sq_used = sem("sq_used")
        self.tables = sem("tables")
        self.rot2_ready = sem("rot2_ready")
        self.rot2_free = sem("rot2_free")
        self.group_free = sem("group_free")
        self.v_ready = sem("v_ready")
        self.k_staged = sem("k_staged")
        self.k_turned = sem("k_turned")
        self.k_stack = sem("k_stack")
        self.q_staged = sem("q_staged")
        self.q_turned = sem("q_turned")
        self.q_stack = sem("q_stack")
        self.score = sem("score")
        self.neg_max = sem("neg_max")
        self.exp_done = sem("exp_done")
        self.pr_turned = sem("pr_turned")
        self.pr_t_ready = sem("pr_t_ready")
        self.pv_done = sem("pv_done")
        self.o_drained = sem("o_drained")
        self.w_slot = [sem(f"w_slot{i}") for i in range(RING)]


def trunk(nc, x_prompt, x_sample, norm_g, w_in, w_gate_f, b_gate_f, w_gate_b, b_gate_b, gla_norm_g,
          q_norm_g, k_norm_g, w_branch_a, w_branch_b, w_out, final_norm_g,
          identity, masks, rope_cos, rope_sin, y_prompt, y_sample):
    def sb(name, shape, offset, dtype=F32):
        return nc.alloc_sbuf_tensor_at(name, shape, dtype, offset=offset)

    def view(t, start, *dims):
        row = 1
        for n in t.shape[1:]:
            row *= n
        return bass.AP(t, start, [[row, P]] + [list(d) for d in dims])

    def rows_of(a, start, n):
        return bass.AP(a.tensor, start, [[0, P], [1, n]])

    x = sb("x", [P, NT, D], R_X)
    act_hi = sb("act_hi", [P, KT, TOK], R_ACT, F32R)
    act_lo = sb("act_lo", [P, KT, TOK], R_ACT + KT * ROW, F32R)
    w_raw = sb("w_raw", [P, RING, HALF], R_W)
    w_hi = sb("w_hi", [P, RING, HALF], R_W + RING * HALF * 4, F32R)
    w_lo = sb("w_lo", [P, RING, HALF], R_W + 2 * RING * HALF * 4, F32R)
    va = sb("va", [P, NT, D], R_V)
    qk_t = sb("qk_t", [P, GH, 2, TOK], R_M)
    q = sb("q", [P, NT, D], R_M)
    ma = sb("ma", [P, NT, D], R_ACT)
    zb = sb("zb", [P, NT, D], R_ACT + NT * D * 4)
    mb = sb("mb", [P, NT, D], R_M)
    merged = sb("merged", [P, NT, D], R_V)
    stg = sb("stg", [P, NT, BGW], R_G)
    proj = nc.dram_tensor("proj", [P, NBG, NT, BGW], F32, kind="Internal")
    o_hi = sb("o_hi", [P, KT, TOK], R_O, F32R)
    o_lo = sb("o_lo", [P, KT, TOK], R_O + KT * ROW, F32R)
    b_turned = [(sb(f"b_hi{i}", [P, KT // 2, TOK], at, F32R), sb(f"b_lo{i}", [P, KT // 2, TOK], at + KT // 2 * ROW, F32R))
                for i, at in enumerate((R_ACT + KT * ROW, R_ACT))]
    g_row = sb("g_row", [P, D], R_G)
    hn = sb("hn", [P, 2, D], R_O + D * 4)
    y_out = sb("y_out", [P, NT, D], R_O + 4 * D * 4)
    squares = sb("squares", [P, NT, D], R_ACT + KT * ROW)
    mask_raw = sb("mask_raw", [P, NMASK, P], R_V)
    ce = sb("ce", [P, 2, TOK], R_O)
    lev = sb("lev", [P, 2, 2, TOK], R_O + 2 * ROW)
    qk = sb("qk", [P, 2, 2, TOK], R_O + 6 * ROW)
    gl_t = sb("gl_t", [2 * RANK, TOK], R_O + 10 * ROW)
    amat = sb("amat", [P, NT, P], R_O + 11 * ROW)
    aoff1 = sb("aoff1", [P, NT, P], R_O + 12 * ROW)
    aoff2 = sb("aoff2", [P, NTP, 2, P], R_O + 13 * ROW)
    wg_fix = sb("wg_fix", [2 * RANK, 2, GK], R_G + NT * BGW * 4)
    wg = sb("wg", [2 * RANK, 2, GH * GK], R_G + NT * BGW * 4 + 2 * GK * 4)
    kv = sb("kv", [P, NT, 2, KVH, DH], R_O)
    k_hh = sb("k_hh", [P, TOK], R_O + 4 * ROW, F32R)
    k_ll = sb("k_ll", [P, TOK], R_O + 5 * ROW, F32R)
    q_hl = sb("q_hl", [P, 2, TOK], R_O + 6 * ROW, F32R)
    q_st = sb("q_st", [P, 2, NT, 2, DH], R_O + 8 * ROW, F32R)
    k_st = sb("k_st", [P, 2, NT, 2, DH], R_O + 10 * ROW, F32R)
    v_grp = sb("v_grp", [P, NT, DH], R_O + 12 * ROW)
    pr = sb("pr", [P, 2, HALF], R_O + 12 * ROW + NT * DH * 4)
    pr_t = sb("pr_t", [P, 2, HALF], R_O + 12 * ROW + NT * DH * 4 + 2 * HALF * 4)
    R_T = R_O + 4 * ROW
    cs = sb("cs", [P, 2, 2, NT, DH], R_T)
    cs_raw = sb("cs_raw", [P, 2, NT, DH], R_T + 4 * NT * DH * 4)
    rot1 = sb("rot1", [P, HALF], R_T + 6 * NT * DH * 4)
    rot2 = sb("rot2", [P, HALF], R_T + 6 * NT * DH * 4 + HALF * 4)
    sq = sb("sq", [P, 2, HALF], R_T + 6 * NT * DH * 4 + 2 * HALF * 4)
    g_qk = sb("g_qk", [P, 2, DH], R_T + 6 * NT * DH * 4 + 4 * HALF * 4)
    gv_row = sb("gv_row", [P, GV], R_T + 6 * NT * DH * 4 + 4 * HALF * 4 + 2 * DH * 4)
    NSTAT = NT * (AH + KVH)
    ident = sb("ident", [P, P], R_S)
    mask = sb("mask", [P, NMASK, P], R_S + P * 4, U8)
    st = sb("st", [P, 5, NSTAT], R_S + P * 4 + NMASK * P)
    bg = sb("bg", [P, 2, GH], R_S + P * 4 + NMASK * P + 5 * NSTAT * 4)
    bg_fix = sb("bg_fix", [P, 2], R_S + P * 4 + NMASK * P + 5 * NSTAT * 4 + 32)
    ps = nc.alloc_psum_tensor("ps", [P, 8 * HALF], F32)

    def bank(b, n=HALF):
        return ps[:, b * HALF:b * HALF + n]

    def view_ps(start, *dims):
        return bass.AP(ps, start, [[8 * HALF, P]] + [list(d) for d in dims])

    def nmax(n, i):
        return st[:, 0, 2 * (n % 2) + i:2 * (n % 2) + i + 1]

    def den(h, t):
        return st[:, 1, h % 2 * NT + t:h % 2 * NT + t + 1]

    s = Semaphores(nc)

    def phase_end(eng, at, own, free=False):
        eng.drain().then_inc(own, 1)
        if own is s.pe_phase and free:
            for name in ("act_phase", "dve_phase", "pool_phase"):
                at.skip(name, 1)
            return
        if own is not s.pe_phase:
            eng.wait_ge(s.pe_phase, at("pe_phase"))
        if own is not s.act_phase:
            eng.wait_ge(s.act_phase, at("act_phase"))
        if own is not s.dve_phase:
            eng.wait_ge(s.dve_phase, at("dve_phase"))
        if own is not s.pool_phase:
            eng.wait_ge(s.pool_phase, at("pool_phase"))
        eng.sem_inc(s.passed, 1)

    with nc.Block() as block:

        @block.sync
        def _(sp):
            at = Counts("sync", sp)
            def tile_of(prompt, sample, t):
                return (prompt, t) if t < NTP else (sample, t - NTP)

            for t in range(NT):
                src, i = tile_of(x_prompt, x_sample, t)
                sp.dma_start(x[:, t, :], src[0, i * P:(i + 1) * P, :]).then_inc(s.x_in[t], 16)
            sp.dma_start(ident[:], identity).then_inc(s.consts_in, 16)
            sp.dma_start(mask_raw[:], masks).then_inc(s.consts_in, 16)

            def load_group(w, layer, col, width=HALF, blocks=KT):
                ld = w.shape[2]
                for k in range(blocks):
                    sp.wait_ge(s.w_lo_done, at("w_lo_done"))
                    src = bass.AP(w.tensor, layer * (D * ld) + col + k * P * ld, [[ld, P], [1, width]])
                    sp.dma_start(w_raw[:, k % RING, 0:width], src).then_inc(s.w_slot[k % RING], 16)

            with at.repeat(DEPTH, "layer") as layer:
                load_group(w_in, layer, C_GATES, P)
                with at.repeat(4, "gla projections") as g:
                    load_group(w_in, layer, g * HALF + C_QKV)
                with at.repeat(GH, "gla background") as h:
                    for i in range(2):
                        load_group(w_in, layer, h * (2 * BGW) + C_QB + i * BGW, BGW)
                for i in range(2):
                    load_group(w_in, layer, C_ZB + (2 + i) * BGW, BGW)
                with at.repeat(4, "rope background") as i:
                    load_group(w_in, layer, i * BGW + C_ZA, BGW)
                with at.repeat(KVH, "attention background") as g:
                    for i in range(2):
                        load_group(w_in, layer, g * (2 * BGW) + C_MA + i * BGW, BGW)
                for w, name in ((w_branch_a, "gla branch"), (w_branch_b, "attention branch"), (w_out, "output")):
                    with at.repeat(2, name) as g:
                        load_group(w, layer, g * HALF)
            load_group(w_in, 0, C_GATES, P, blocks=SKEW)
            for t in range(NT):
                dst, i = tile_of(y_prompt, y_sample, t)
                sp.wait_ge(s.y_ready, t + 1)
                sp.dma_start(dst[0, i * P:(i + 1) * P, :], y_out[:, t, :]).then_inc(s.out_done, 16)
            sp.wait_ge(s.out_done, NT * 16)

        @block.tensor
        def _(pe):
            at = Counts("tensor", pe, w_lo_done=RING, drained=8)
            mm = nc.tensor.matmul

            def three_passes(out, s_hi, s_lo, m_hi, m_lo, first, last):
                mm(out, s_hi, m_hi, start=first, stop=False)
                mm(out, s_hi, m_lo, start=False, stop=False)
                return mm(out, s_lo, m_hi, start=False, stop=last)

            def gemm_tokens(a_hi, a_lo, turns=None, first=0, half_free=True):
                for k in range(KT):
                    pe.wait_ge(s.w_lo_done, at("w_lo_done"))
                    if k == KT // 2 and not half_free:
                        pe.wait_ge(s.turn_free, at.peek("turn_free", 2))
                    for t in range(NT):
                        if k == 0:
                            pe.wait_ge(s.drained, at.peek("drained", t + 1 - NT))
                        tok = slice(t * P, (t + 1) * P)
                        last = three_passes(bank(t), a_hi(k)[:, tok], a_lo(k)[:, tok], w_hi[:, k % RING, :],
                                            w_lo[:, k % RING, :], k == 0, k == KT - 1)
                        if k == KT - 1:
                            last.then_inc(s.gemm_ready, 1)
                        if turns and first <= k < first + 3 and t in (2, NT - 1) and (k, t) != (KT - 1, NT - 1):
                            turns(2 * (k - first) + t // 3)
                    (last if k < KT - 1 else pe.drain()).then_inc(s.w_used, 1)
                at.skip("drained", NT)

            def background(start, stop, bank0=BG_BANK, spare=0):
                for u in range(start, stop):
                    i, t = divmod(u, NT)
                    k = i % KT
                    if t == 0:
                        pe.wait_ge(s.w_lo_done, at("w_lo_done"))
                    if k == 0 and t % 2 == 0:
                        pe.wait_ge(s.bg_free, at.peek("bg_free", 1 - 3 * spare))
                        at.skip("bg_free", 1)
                    out = ps[:, bank0 * HALF + t * BGW:bank0 * HALF + (t + 1) * BGW]
                    tok = slice(t * P, (t + 1) * P)
                    mm(out, act_hi[:, k, tok], w_hi[:, k % RING, 0:BGW], start=(k == 0 and t % 2 == 0), stop=False, skip_group_check=True)
                    mm(out, act_hi[:, k, tok], w_lo[:, k % RING, 0:BGW], start=False, stop=False, skip_group_check=True)
                    last = mm(out, act_lo[:, k, tok], w_hi[:, k % RING, 0:BGW], start=False, stop=(k == KT - 1), skip_group_check=True)
                    if t == NT - 1:
                        last.then_inc(s.w_used, 1)

            def gemm_features(blocks):
                for k in range(KT):
                    pe.wait_ge(s.w_lo_done, at("w_lo_done"))
                    for b in range(8 - 2 * blocks, 8):
                        if k == 0:
                            pe.wait_ge(s.drained, at.peek("drained", b + 1 - 8))
                        col = slice((b // 2 + blocks - 4) * P, (b // 2 + blocks - 3) * P)
                        tok = slice(b % 2 * FH, (b % 2 + 1) * FH)
                        last = three_passes(bank(b, FH), w_hi[:, k % RING, col], w_lo[:, k % RING, col],
                                            act_hi[:, k, tok], act_lo[:, k, tok], k == 0, k == KT - 1)
                        if k == KT - 1:
                            last.then_inc(s.gemm_ready, 1)
                    (last if k < KT - 1 else pe.drain()).then_inc(s.w_used, 1)
                at.skip("drained", 2 * blocks)

            def turn_step(src, m):
                pe.wait_ge(s.turn_free, at("turn_free"))
                for j in range(4):
                    last = nc.tensor.transpose(ps[:, (6 + m % 2) * HALF + j * P:(6 + m % 2) * HALF + (j + 1) * P],
                                               src[:, j * P:(j + 1) * P], ident[:])
                last.then_inc(s.turned, 1)

            def merged_step(half):
                def step(t):
                    pe.wait_ge(s.merged_ready, at("merged_ready"))
                    turn_step(merged[:, t, half * HALF:(half + 1) * HALF], t)
                return step

            def half_of(src, half):
                return lambda t: turn_step(src[:, t, half * HALF:(half + 1) * HALF], t)

            def gla_gates():
                pe.wait_ge(s.prod_free, at("prod_free"))
                pe.wait_ge(s.gla_fix, at("gla_fix"))
                for b in range(4):
                    last = mm(bank(b, FH), wg_fix[:, b // 2, :], gl_t[:, b % 2 * FH:(b % 2 + 1) * FH], start=True, stop=True)
                last.then_inc(s.gate_ready, 1)

            def gla_levels(h, done):
                for n in range(GLA_STEPS):
                    if n > 0:
                        pe.wait_ge(s.prod_free, at("prod_free"))
                    li = max(n - 1, 0)
                    if n != 1:
                        pe.wait_ge(s.q_ready, at("q_ready"))
                        pe.wait_ge(s.k_ready, at("k_ready"))
                    kk = view(qk, (li % 2) * 2 * TOK + TOK, (1, TOK))
                    qq = view(qk, (li % 2) * 2 * TOK, (1, TOK))
                    span = LEVELS[li]
                    if span == 256:
                        for j in range(NTP):
                            i0 = 2 * P if j < 2 else 0
                            last = mm(ps[:, j * 2 * P:(j + 1) * 2 * P], kk[:, j * P:(j + 1) * P],
                                      qq[:, i0:i0 + 2 * P], start=True, stop=True)
                    else:
                        for j in range(NT):
                            i = j ^ 1 if span == 128 else j
                            rhs = view(qk_t, h * (2 * TOK) + i * P, (1, P)) if n == 0 else qq[:, i * P:(i + 1) * P]
                            last = mm(ps[:, j * P:(j + 1) * P], kk[:, j * P:(j + 1) * P], rhs, start=True, stop=True)
                    last.then_inc(s.prod, 1)
                    background(done[n - 1] if n else GLA_FIRST, done[n])

            def gla_values(h):
                pe.wait_ge(s.a_ready, at("a_ready"))
                for i in range(NT):
                    out = ps[:, 2 * HALF + i * GV:2 * HALF + (i + 1) * GV]
                    terms = [(amat[:, i, :], i), (aoff1[:, i ^ 1, :], i ^ 1)]
                    if i < NTP:
                        terms += [(aoff2[:, j, i % 2, :], j) for j in ((2, 3) if i < 2 else (0, 1))]
                    for n, (a, j) in enumerate(terms):
                        last = mm(out, a, view(va, h * GV + j * D, (1, GV)), start=(n == 0), stop=(n == len(terms) - 1))
                last.then_inc(s.gla_o, 1)

            def attention_group():
                def turn_stack(stage, col, tiles):
                    for t in tiles:
                        last = nc.tensor.transpose(ps[:, col + (t - tiles[0]) * P:col + (t - tiles[0] + 1) * P],
                                                   stage(t).bitcast(F32), ident[:])
                    return last

                def q_turn_first(h):
                    pe.wait_ge(s.q_staged, at("q_staged"))
                    turn_stack(lambda t: view(q_st, h % 2 * TOK + t * P, (1, P)), 4 * HALF, range(4)).then_inc(s.q_turned, 1)

                def q_turn_second(h):
                    pe.wait_ge(s.q_stack, at("q_stack"))
                    turn_stack(lambda t: view(q_st, h % 2 * TOK + t * P, (1, P)), 4 * HALF, range(4, NT)).then_inc(s.q_turned, 1)

                def scores(n):
                    h, u = divmod(n, UNITS)
                    if u == 0:
                        pe.wait_ge(s.q_stack, at("q_stack"))
                    out = bank(n % 2)
                    if u < NTP:
                        parts = [(out, u, slice(0, SEQS[0]))]
                    else:
                        parts = [(out[:, i * 256:(i + 1) * 256], NTP + i, slice(SEQS[0], TOK)) for i in range(2)]
                    for o, t, keys in parts:
                        lhs = q_hl[:, h % 2, t * P:(t + 1) * P]
                        mm(o, lhs, k_hh[:, keys], start=True, stop=False)
                        last = mm(o, lhs, k_ll[:, keys], start=False, stop=True)
                    last.then_inc(s.score, 1)

                def turn_p(n):
                    pe.wait_ge(s.exp_done, at("exp_done"))
                    for j in range(4):
                        last = nc.tensor.transpose(ps[:, 2 * HALF + j * P:2 * HALF + (j + 1) * P],
                                                   pr[:, n % 2, j * P:(j + 1) * P], ident[:])
                    last.then_inc(s.pr_turned, 1)

                def values(n):
                    h, u = divmod(n, UNITS)
                    if n == 0:
                        pe.wait_ge(s.v_ready, at("v_ready"))
                    pe.wait_ge(s.pr_t_ready, at("pr_t_ready"))
                    if u == 0:
                        pe.wait_ge(s.o_drained, at("o_drained"))
                    for i in range(1 if u < NTP else 2):
                        t = u + i
                        nk = 4 if u < NTP else 2
                        for j in range(nk):
                            key = j if u < NTP else NTP + j
                            last = mm(ps[:, 3 * HALF + t * DH:3 * HALF + (t + 1) * DH],
                                      pr_t[:, n % 2, (i * 2 + j) * P:(i * 2 + j + 1) * P], v_grp[:, key, :],
                                      start=(j == 0), stop=(j == nk - 1))
                    last.then_inc(s.pv_done, 1)

                background(0, 10)
                for part in range(2):
                    pe.wait_ge(s.k_staged, at("k_staged"))
                    if part == 1:
                        pe.wait_ge(s.k_stack, at("k_stack"))
                    turn_stack(lambda t: view(k_st, part * TOK + t * P, (1, P)), 0, range(NT)).then_inc(s.k_turned, 1)
                    background(10 + part * 2, 12 + part * 2)
                    if part == 0:
                        q_turn_first(0)
                q_turn_second(0)
                background(14, 16)
                pe.wait_ge(s.k_stack, at("k_stack"))
                total = GROUP * UNITS
                scores(0)
                background(16, ATT_FIRST)
                for n in range(total):
                    h = n // UNITS + 1
                    if n % UNITS == 1 and h < GROUP:
                        q_turn_first(h)
                    if n % UNITS == 2 and h < GROUP:
                        q_turn_second(h)
                    if n + 1 < total:
                        scores(n + 1)
                    turn_p(n)
                    background(ATT_DONE[n - 1] if n else ATT_FIRST, ATT_DONE[n])
                    values(n)

            pe.sem_inc(s.w_used, RING)
            pe.wait_ge(s.consts_in, at("consts_in", 32))
            with at.repeat(DEPTH, "layer"):
                for t in range(NT):
                    pe.wait_ge(s.hn_ready, at("hn_ready"))
                    for half in range(2):
                        turn_step(hn[:, t % 2, half * HALF:(half + 1) * HALF], half)
                phase_end(pe, at, s.pe_phase)
                gemm_features(1)
                with at.repeat(2, "gla qk"):
                    gemm_features(4)
                with at.repeat(2, "gla v"):
                    gemm_tokens(lambda k: act_hi[:, k, :], lambda k: act_lo[:, k, :])
                phase_end(pe, at, s.pe_phase, free=True)
                pe.wait_ge(s.drained, at.peek("drained", 0))
                gla_gates()
                background(0, GLA_FIRST)
                pe.wait_ge(s.gate_used, at("gate_used"))
                pe.sem_inc(s.passed, 1)
                with at.repeat(GH - 1, "gla head") as h:
                    gla_levels(h, GLA_DONE)
                    gla_gates()
                    background(GLA_DONE[-1], GLA_DONE[-1] + GLA_MID)
                    pe.wait_ge(s.gate_used, at("gate_used"))
                    gla_values(h)
                    background(GLA_DONE[-1] + GLA_MID, BG_TILES + GLA_FIRST)
                gla_levels(GH - 1, GLA_LAST_DONE)
                gla_values(GH - 1)
                phase_end(pe, at, s.pe_phase, free=True)
                background(GLA_LAST_DONE[-1], BG_TILES)
                pe.wait_ge(s.o_read, at("o_read"))
                pe.sem_inc(s.passed, 1)
                with at.repeat(3, "rope background"):
                    background(0, KT * NT, BG_BANK - 3, spare=1)
                    background(0, KT * NT, spare=1)
                phase_end(pe, at, s.pe_phase, free=True)
                with at.repeat(KVH, "attention group"):
                    attention_group()
                pe.wait_ge(s.o_drained, at.peek("o_drained", 1))
                pe.wait_ge(s.bg_free, at.peek("bg_free", 3))
                o_parts = (lambda k: o_hi[:, k, :]), (lambda k: o_lo[:, k, :])
                b_parts = [lambda k, part=part: b_turned[k // (KT // 2)][part][:, k % (KT // 2), :] for part in range(2)]
                for t in range(NT):
                    half_of(va, 0)(t)
                pe.wait_ge(s.turn_free, at.peek("turn_free", 2))
                gemm_tokens(*o_parts, half_of(va, 1), half_free=False)
                pe.wait_ge(s.ob_ready, at("ob_ready"))
                gemm_tokens(*o_parts, half_of(q, 0), first=2)
                pe.wait_ge(s.turn_free, at.peek("turn_free", 2))
                gemm_tokens(*b_parts, half_of(q, 1), half_free=False)
                gemm_tokens(*b_parts, merged_step(0), first=1)
                pe.wait_ge(s.turn_free, at.peek("turn_free", 2))
                gemm_tokens(*o_parts, merged_step(1), half_free=False)
                gemm_tokens(*o_parts)
                phase_end(pe, at, s.pe_phase)

        @block.scalar
        def _(act):
            at = Counts("scalar", act, drained=8, bg_free=3)
            act.sem_inc(s.bg_free, 3)
            act.sem_inc(s.stored, 16)
            A = nc.scalar.activation

            def split(k, width=HALF):
                slot = (k + SKEW) % RING
                act.wait_ge(s.w_slot[slot], at(f"w_slot{slot}", 16))
                act.wait_ge(s.w_used, at("w_used"))
                A(w_hi[:, slot, 0:width], w_raw[:, slot, 0:width], ACT.Copy).then_inc(s.w_hi_done, 1)

            def copy_sums(func, bank0):
                for b in range(3):
                    A(stg[:, 2 * b:2 * b + 2, :].rearrange("p a b -> p (a b)"), bank(bank0 + b), func).then_inc(s.bg_free, 1)
                act.wait_ge(s.bg_free, at("bg_free", 3))

            def store(j, bank0=BG_BANK):
                act.wait_ge(s.w_used, at.peek("w_used", 1))
                act.wait_ge(s.stored, at("stored", 16))
                copy_sums(ACT.Copy, bank0)
                act.dma_start(bass.AP(proj, j * (NT * BGW), [[NBG * NT * BGW, P], [1, NT * BGW]]),
                              stg[:].rearrange("p a b -> p (a b)")).then_inc(s.stored, 16)

            def all_stored():
                act.wait_ge(s.stored, at.peek("stored", 16))

            def fetch(dst, j, start, row, n, sem):
                for c in range(n):
                    act.dma_start(view(dst, start + c * BGW, (row, NT), (1, BGW)),
                                  bass.AP(proj, (j + c) * (NT * BGW), [[NBG * NT * BGW, P], [BGW, NT], [1, BGW]])).then_inc(sem, 16)

            def param(dst, src):
                act.dma_start(dst, src).then_inc(s.param, 16)

            def rsqrt_seed(n):
                act.wait_ge(s.stat_v, at("stat_v"))
                A(st[:, 2, 0:n], st[:, 1, 0:n], ACT.Sqrt).then_inc(s.stat_root, 1)

            def sum_squares(t, half):
                x_half = x[:, t, half * HALF:(half + 1) * HALF]
                return A(squares[:, t, half * HALF:(half + 1) * HALF], x_half, ACT.Square,
                         accum_out=st[:, 0, half * NT + t:half * NT + t + 1])

            def turn_hi(dst, m, t, k0=0):
                act.wait_ge(s.turned, at("turned"))
                A(dst[:, k0:k0 + 4, t * P:(t + 1) * P],
                  ps[:, (6 + m % 2) * HALF:(7 + m % 2) * HALF].rearrange("p (a b) -> p a b", a=4), ACT.Copy).then_inc(s.turn_hi, 1)

            def skip_banks(n):
                at.skip("gemm_ready", n)
                at.skip("drained", n)

            def splits():
                for k in range(KT):
                    split(k)

            def gla_exp(li):
                n = TOK if LEVELS[li] < 256 else SEQS[0]
                act.wait_ge(s.lev_diff, at("lev_diff"))
                y = view(lev, li % 2 * 2 * TOK, (TOK, 2), (1, n))
                A(y, y, ACT.Exp, scale=1.0 / GATE_NORM).then_inc(s.lev_exp, 1)

            def gla_gates(first):
                act.wait_ge(s.gla_fix, at("gla_fix"))
                act.wait_ge(s.gate_ready, at("gate_ready"))
                for d in range(2):
                    A(view(lev, (2 + d) * TOK, (FH, 2), (1, FH)), view_ps(d * 2 * HALF, (HALF, 2), (1, FH)),
                      ACT.Abs, bias=bg_fix[:, d:d + 1]).then_inc(s.gate_abs, 1)
                split(first, BGW)
                act.wait_ge(s.gate_abs, at("gate_abs", 2))
                a = view(lev, 2 * TOK, (1, 2 * TOK))
                A(a, a, ACT.Exp, scale=-1.0).then_inc(s.act_chain, 1)
                split(first + 1, BGW)
                act.wait_ge(s.act_chain, at("act_chain"))
                A(a, a, ACT.Ln, bias=1.0).then_inc(s.gate_log, 1)
                gla_exp(0)
                split(first + 2, BGW)

            def gla_levels(h, start):
                for li in range(len(LEVELS)):
                    if li > 0:
                        gla_exp(li)
                    if start[KT] == li:
                        store(2 * h)
                    if start.get(2 * KT) == li:
                        store(2 * h + 1)
                    for i in start:
                        if start[i] == li:
                            split(i, BGW)

            def gla_out(h):
                act.wait_ge(s.gla_o, at("gla_o"))
                A(view(va, h * GV, (D, NT), (1, GV)), view_ps(2 * HALF, (GV, NT), (1, GV)), ACT.Copy, scale=GK ** -0.5).then_inc(s.act_chain, 1)
                act.wait_ge(s.act_chain, at("act_chain"))
                for t in range(NT):
                    o = ps[:, 2 * HALF + t * GV:2 * HALF + (t + 1) * GV]
                    last = A(o, o, ACT.Square, scale=GK ** -0.5, accum_out=st[:, 1, t:t + 1])
                last.then_inc(s.act_chain, 1)
                act.wait_ge(s.act_chain, at("act_chain"))
                A(view(st, h, (GH, NT)), st[:, 1, 0:NT], ACT.Copy)

            def attention_group(g):
                def exp_scores(n):
                    h, u = divmod(n, UNITS)
                    act.wait_ge(s.neg_max, at("neg_max"))
                    for i in range(1 if u < NTP else 2):
                        w = HALF if u < NTP else HALF // 2
                        last = A(pr[:, n % 2, i * w:(i + 1) * w], ps[:, n % 2 * HALF + i * w:n % 2 * HALF + (i + 1) * w],
                                 ACT.Exp, bias=nmax(n, i), accum_out=den(h, u + i))
                    act.drain().then_inc(s.exp_done, 1)

                def copy_pt(n):
                    act.wait_ge(s.pr_turned, at("pr_turned"))
                    if n >= 2:
                        act.wait_ge(s.pv_done, at.peek("pv_done", -1))
                    A(pr_t[:, n % 2, :], bank(2), ACT.Copy).then_inc(s.pr_t_ready, 1)
                    at.skip("pv_done", 1)

                def wide_split(i):
                    split(i, BGW if i + SKEW < BG_BLOCKS else HALF)

                A(k_st[:, 0, :, :, :], view(kv, g * DH, (HALF, NT), (0, 2), (1, DH)), ACT.Copy).then_inc(s.k_staged, 1)
                for i in range(3):
                    wide_split(i)
                total = GROUP * UNITS
                exp_scores(0)
                for i in range(3, BG_BLOCKS):
                    if ATT_START[i] < 0:
                        wide_split(i)
                for n in range(total):
                    copy_pt(n)
                    if n + 1 < total:
                        exp_scores(n + 1)
                    for i in range(3, BG_BLOCKS):
                        if ATT_START[i] == n:
                            wide_split(i)
                    if ATT_DONE[n] in (BG_TILES // 2, BG_TILES):
                        store(g * 2 + J_MA + ATT_DONE[n] // BG_TILES)

            for t in range(NT):
                act.wait_ge(s.x_in[t], 16)
                for half in range(2):
                    last = sum_squares(t, half)
            last.then_inc(s.stat_sum, 1)
            for k in range(SKEW):
                act.wait_ge(s.w_used, at("w_used"))
                act.wait_ge(s.w_slot[k], at(f"w_slot{k}", 16))
                A(w_hi[:, k, 0:P], w_raw[:, k, 0:P], ACT.Copy).then_inc(s.w_hi_done, 1)
            with at.repeat(DEPTH, "layer") as layer:
                act.dma_start(g_row[:], rows_of(norm_g, layer * D, D)).then_inc(s.g_in, 16)
                rsqrt_seed(NT)
                for t in range(NT):
                    for half in range(2):
                        turn_hi(act_hi, half, t, half * 4)
                phase_end(act, at, s.act_phase)
                for k in range(KT):
                    split(k, P if k + SKEW < KT else HALF)
                param(wg[0:RANK, 0, :], bass.AP(w_gate_f.tensor, layer * (RANK * GH * GK), [[GH * GK, RANK], [1, GH * GK]]))
                param(wg[RANK:2 * RANK, 1, :], bass.AP(w_gate_b.tensor, layer * (RANK * GH * GK), [[GH * GK, RANK], [1, GH * GK]]))
                for d, b_gate in enumerate((b_gate_f, b_gate_b)):
                    for h in range(GH):
                        param(bg[:, d, h:h + 1], bass.AP(b_gate.tensor, layer * (GH * GK) + h * GK, [[1, P], [1, 1]]))
                with at.repeat(4, "gla projections"):
                    splits()
                skip_banks(2 + 2 * 8 + 2 * NT)
                phase_end(act, at, s.act_phase)
                gla_gates(0)
                for i in range(3, GLA_FIRST // NT):
                    split(i, BGW)
                behind = [i for i in GLA_START if GLA_START[i] >= len(LEVELS)]
                with at.repeat(GH - 1, "gla head") as h:
                    gla_levels(h, GLA_START)
                    for i in behind[:-3]:
                        split(i, BGW)
                    gla_gates(behind[-3])
                    gla_out(h)
                gla_levels(GH - 1, GLA_LAST_START)
                for i in GLA_LAST_START:
                    if GLA_LAST_START[i] >= len(LEVELS):
                        split(i, BGW)
                gla_out(GH - 1)
                act.drain().then_inc(s.o_read, 1)
                phase_end(act, at, s.act_phase)
                param(gv_row[:], rows_of(gla_norm_g, layer * GV, GV))
                rsqrt_seed(NT * GH)
                store(2 * GH - 1)
                for i in range(6 * KT):
                    split(i % KT, BGW)
                    if i == 0:
                        param(cs_raw[:, 0, :, :], rope_cos)
                        param(cs_raw[:, 1, :, :], rope_sin)
                        param(g_qk[:, 0, :], rows_of(q_norm_g, layer * DH, DH))
                        param(g_qk[:, 1, :], rows_of(k_norm_g, layer * DH, DH))
                    if i in (1, 3, 5, 7):
                        fetch(q, J_Q + i // 2, i // 2 * BGW, D, 1, s.qkv_in)
                    if i in (9, 11):
                        fetch(kv, J_K + (i - 9) // 2, (i - 9) // 2 * BGW, HALF, 1, s.qkv_in)
                    if i == 14:
                        act.wait_ge(s.qkv_in, at("qkv_in", 6 * 16))
                    if 14 <= i < 14 + NT:
                        for n in range(3 * (i - 14), 3 * (i - 13)):
                            t, part = n // 3, n % 3
                            src = view(q, t * D + part * HALF, (1, HALF)) if part < 2 else view(kv, t * HALF, (1, KVH * DH))
                            act.wait_ge(s.sq_used, at("sq_used"))
                            A(view(sq, n % 2 * HALF, (1, HALF if part < 2 else KVH * DH)), src, ACT.Square).then_inc(s.sq_ready, 1)
                    if i == 14 + NT:
                        rsqrt_seed(NSTAT)
                    if i % KT == KT - 1:
                        if i < 2 * KT:
                            store(J_ZB + 2 + i // KT, BG_BANK - (i // KT + 1) % 2 * 3)
                        else:
                            act.wait_ge(s.w_used, at.peek("w_used", 1))
                            if i < 3 * KT:
                                all_stored()
                            else:
                                act.wait_ge(s.sil_used, at("sil_used"))
                            copy_sums(ACT.Silu, BG_BANK - (i // KT + 1) % 2 * 3)
                            act.sem_inc(s.sil_ready, 1)
                at.skip("sil_used", 1)
                phase_end(act, at, s.act_phase)
                with at.repeat(KVH, "attention group") as g:
                    attention_group(g)
                for t in range(NT):
                    turn_hi(o_hi, t, t)
                    if t < 4:
                        fetch(zb, J_ZB + t, t * BGW, D, 1, s.zb_in)
                for k in range(KT):
                    split(k)
                    if k < 2:
                        fetch(ma, J_MA + k, k * BGW, D, 1, s.m_in[0])
                    if k < 3:
                        for t in (2 * k, 2 * k + 1):
                            turn_hi(o_hi, t, t, 4)
                    if k == 2:
                        act.wait_ge(s.zb_in, at("zb_in", 4 * 16))
                    if 2 <= k < 6:
                        some = view(zb, (k - 2) // 2 * HALF + k % 2 * (NT // 2) * D, (D, NT // 2), (1, HALF))
                        A(some, some, ACT.Silu).then_inc(s.zb_ready, 1)
                    if k in (3, 4):
                        if k == 4:
                            all_stored()
                        fetch(ma, J_MA + k - 1, (k - 1) * BGW, D, 1, s.m_in[1])
                    if k == 6:
                        act.wait_ge(s.m_in[0], at("m_in0", 2 * 16))
                    if k >= 6:
                        some = view(ma, k % 2 * (NT // 2) * D, (D, NT // 2), (1, HALF))
                        A(some, some, ACT.Sigmoid).then_inc(s.sig_ready, 1)
                for k in range(KT):
                    split(k)
                    if k == 0:
                        act.wait_ge(s.m_in[1], at("m_in1", 2 * 16))
                    if k < 2:
                        some = view(ma, HALF + k % 2 * (NT // 2) * D, (D, NT // 2), (1, HALF))
                        A(some, some, ACT.Sigmoid).then_inc(s.sig_ready, 1)
                    if 2 <= k < 5:
                        for t in (2 * k - 4, 2 * k - 3):
                            turn_hi(b_turned[0][0], t, t)
                skip_banks(2 * NT)
                for k in range(KT):
                    split(k)
                    if k == 0:
                        act.wait_ge(s.drained, at.peek("drained", 0))
                    if k < 3:
                        for t in (2 * k, 2 * k + 1):
                            turn_hi(b_turned[1][0], t, t)
                    if 2 <= k < 6:
                        fetch(mb, J_MB + k - 2, (k - 2) * BGW, D, 1, s.m_in[k // 4])
                    if k == 6:
                        act.wait_ge(s.m_in[0], at("m_in0", 2 * 16))
                    if k >= 6:
                        some = view(mb, k % 2 * (NT // 2) * D, (D, NT // 2), (1, HALF))
                        A(some, some, ACT.Sigmoid).then_inc(s.sig_ready, 1)
                for k in range(KT):
                    split(k)
                    if 1 <= k < 4:
                        for t in (2 * k - 2, 2 * k - 1):
                            turn_hi(o_hi, t, t)
                    if k == 4:
                        act.wait_ge(s.m_in[1], at("m_in1", 2 * 16))
                    if k in (4, 5):
                        some = view(mb, HALF + k % 2 * (NT // 2) * D, (D, NT // 2), (1, HALF))
                        A(some, some, ACT.Sigmoid).then_inc(s.sig_ready, 1)
                skip_banks(2 * NT)
                for k in range(KT):
                    split(k)
                    if k < 3:
                        for t in (2 * k, 2 * k + 1):
                            turn_hi(o_hi, t, t, 4)
                skip_banks(NT)
                for k in range(KT):
                    split(k, HALF if k + SKEW < KT else P)
                    if k == 1:
                        act.wait_ge(s.drained, at.peek("drained", 0))
                    if k in (1, 2, 3):
                        for t in (2 * k - 2, 2 * k - 1):
                            sum_squares(t, 0)
                for t in range(NT):
                    skip_banks(1)
                    act.wait_ge(s.drained, at.peek("drained", 0))
                    last = sum_squares(t, 1)
                last.then_inc(s.stat_sum, 1)
                phase_end(act, at, s.act_phase)
            act.dma_start(g_row[:], rows_of(final_norm_g, 0, D)).then_inc(s.g_in, 16)
            rsqrt_seed(NT)

        @block.gpsimd
        def _(pool):
            at = Counts("gpsimd", pool)
            G = nc.gpsimd

            def split(k, width=HALF):
                slot = (k + SKEW) % RING
                pool.wait_ge(s.w_hi_done, at("w_hi_done"))
                G.tensor_tensor(w_lo[:, slot, 0:width], w_raw[:, slot, 0:width],
                                                  w_hi[:, slot, 0:width].bitcast(F32), ALU.subtract).then_inc(s.w_lo_done, 1)

            def splits():
                for k in range(KT):
                    split(k)

            def phase_ends(n=1):
                for _ in range(n):
                    phase_end(pool, at, s.pool_phase)

            def gla_fix(h):
                G.tensor_copy(wg_fix[:], view_32(wg, h * GK, (GH * GK, 2), (1, GK)))
                G.tensor_copy(bg_fix[:], view(bg, h, (GH, 2)))
                pool.drain().then_inc(s.gla_fix, 1)

            def gla_levels(h, start, more):
                for li, span in enumerate(LEVELS):
                    n = TOK if span < 256 else SEQS[0]
                    pool.wait_ge(s.lev_exp, at("lev_exp"))
                    if li == 2:
                        pool.wait_ge(s.prod, at("prod", 2))
                    elif li > 2:
                        pool.wait_ge(s.prod, at("prod"))
                    pool.sem_inc(s.passed, 1)
                    G.tensor_tensor(view(qk, (li % 2 * 2 + 1) * TOK, (1, n)), view(lev, (li % 2 * 2 + 1) * TOK, (1, n)),
                                    view(qk_t, h * (2 * TOK) + TOK, (1, n)), ALU.mult).then_inc(s.k_ready, 1)
                    if more and li == 4:
                        gla_fix(h + 1)
                    for i in start:
                        if start[i] == li:
                            split(i, BGW)
                at.skip("prod", 2)
                for i in start:
                    if start[i] >= len(LEVELS):
                        split(i, BGW)

            def view_32(t, start, *dims):
                return bass.AP(t, start, [[2 * GH * GK, 2 * RANK]] + [list(d) for d in dims])

            def rope_swapped(n):
                t, part = n // 3, n % 3
                heads = 8 if part < 2 else KVH
                src, row = (q, t * D + part * HALF) if part < 2 else (kv, t * HALF)
                pool.wait_ge(s.rot2_free, at("rot2_free"))
                for half in range(2):
                    G.tensor_tensor(
                        view(rot2, half * 16, (DH, heads), (32, 2), (1, 16)),
                        view(src, row + (1 - half) * 16, (DH, heads), (32, 2), (1, 16)),
                        view(cs, ((part == 2) * 2 + 1) * NT * DH + t * DH + half * 16, (0, heads), (32, 2), (1, 16)),
                        ALU.mult)
                pool.drain().then_inc(s.rot2_ready, 1)

            def attention_group(g):
                pool.wait_ge(s.group_free, at("group_free"))
                pool.sem_inc(s.passed, 1)
                def stage_q(h):
                    if h >= 2:
                        pool.wait_ge(s.q_turned, at("q_turned", 2))
                    q_src = view(q, g * (GROUP * DH) + h * DH, (D, NT), (1, DH))
                    G.tensor_copy(q_st[:, h % 2, :, 0, :], q_src).then_inc(s.pool_chain, 1)
                    pool.wait_ge(s.pool_chain, at("pool_chain"))
                    pool.sem_inc(s.passed, 1)
                    G.tensor_tensor(q_st[:, h % 2, :, 1, :], q_src,
                                    q_st[:, h % 2, :, 0, :].bitcast(F32), ALU.subtract).then_inc(s.q_staged, 1)

                stage_q(0)
                stage_q(1)
                pool.wait_ge(s.group_free, at("group_free"))
                pool.sem_inc(s.passed, 1)
                G.tensor_copy(v_grp[:], view(kv, KVH * DH + g * DH, (HALF, NT), (1, DH))).then_inc(s.v_ready, 1)
                h = 2
                for i in range(BG_BLOCKS):
                    if h < GROUP and (i == 3 if h == 2 else ATT_START[i] > 2):
                        stage_q(h)
                        h += 1
                    split(i, BGW if i + SKEW < BG_BLOCKS else HALF)
                assert h == GROUP
                at.skip("q_turned", 4)

            pool.sem_inc(s.w_lo_done, RING)
            for k in range(SKEW):
                split(k - SKEW, P)
            with at.repeat(DEPTH, "layer"):
                G.memset(wg[:], 0.0)
                phase_ends()
                for k in range(KT):
                    split(k, P if k + SKEW < KT else HALF)
                with at.repeat(4, "gla projections"):
                    splits()
                pool.wait_ge(s.param, at("param", (2 + 2 * GH) * 16))
                pool.sem_inc(s.passed, 1)
                at.skip("param", 5 * 16)
                gla_fix(0)
                phase_ends()
                for i in range(GLA_FIRST // NT):
                    split(i, BGW)
                with at.repeat(GH - 1, "gla head") as h:
                    gla_levels(h, GLA_START, True)
                gla_levels(GH - 1, GLA_LAST_START, False)
                phase_ends()
                n = 0
                for i in range(6 * KT):
                    if i == ROPE_BLOCK:
                        pool.wait_ge(s.tables, at("tables"))
                        pool.wait_ge(s.qkv_in, at("qkv_in", 6 * 16))
                    if (i - ROPE_BLOCK) * 3 * NT >= n * (6 * KT - ROPE_BLOCK):
                        rope_swapped(n)
                        n += 1
                    split(i % KT, BGW)
                phase_ends()
                with at.repeat(KVH, "attention group") as g:
                    attention_group(g)
                with at.repeat(5, "groups"):
                    splits()
                for k in range(KT):
                    split(k, HALF if k + SKEW < KT else P)
                phase_ends()

        @block.vector
        def _(dve):
            at = Counts("vector", dve, drained=8, prod_free=1, rot2_free=1)
            V = nc.vector

            def rsqrt_of(n, size, dst, settled=False):
                if not settled:
                    dve.drain().then_inc(s.dve_chain, 1)
                    dve.wait_ge(s.dve_chain, at("dve_chain"))
                V.tensor_scalar(st[:, 1, 0:n], st[:, 0, 0:n], 1.0 / size, EPS, ALU.mult, ALU.add).then_inc(s.stat_v, 1)
                dve.wait_ge(s.stat_root, at("stat_root"))
                V.reciprocal(st[:, 2, 0:n], st[:, 2, 0:n]).then_inc(s.dve_chain, 1)
                dve.wait_ge(s.dve_chain, at("dve_chain"))
                V.tensor_tensor(st[:, 3, 0:n], st[:, 2, 0:n], st[:, 2, 0:n], ALU.mult).then_inc(s.dve_chain, 1)
                dve.wait_ge(s.dve_chain, at("dve_chain"))
                V.tensor_tensor(st[:, 3, 0:n], st[:, 3, 0:n], st[:, 1, 0:n], ALU.mult).then_inc(s.dve_chain, 1)
                dve.wait_ge(s.dve_chain, at("dve_chain"))
                V.tensor_scalar(st[:, 3, 0:n], st[:, 3, 0:n], -0.5, 1.5, ALU.mult, ALU.add).then_inc(s.dve_chain, 1)
                dve.wait_ge(s.dve_chain, at("dve_chain"))
                V.tensor_tensor(dst, st[:, 3, 0:n], st[:, 2, 0:n], ALU.mult).then_inc(s.dve_chain, 1)
                dve.wait_ge(s.dve_chain, at("dve_chain"))

            def scaled_tokens(t):
                V.scalar_tensor_tensor(hn[:, t % 2, :], x[:, t, :], st[:, 4, t:t + 1], g_row[:],
                                                        ALU.mult, ALU.mult).then_inc(s.hn_ready, 1)

            def turn_lo(hi, lo, steps, k0=0):
                for m, t in steps:
                    dve.wait_ge(s.turn_hi, at("turn_hi"))
                    V.tensor_tensor(
                        lo[:, k0:k0 + 4, t * P:(t + 1) * P],
                        ps[:, (6 + m % 2) * HALF:(7 + m % 2) * HALF].rearrange("p (a b) -> p a b", a=4),
                        hi[:, k0:k0 + 4, t * P:(t + 1) * P].bitcast(F32), ALU.subtract).then_inc(s.turn_free, 1)

            def normalise():
                dve.wait_ge(s.stat_sum, at("stat_sum"))
                V.tensor_tensor(st[:, 0, 0:NT], st[:, 0, 0:NT], st[:, 0, NT:2 * NT], ALU.add)
                rsqrt_of(NT, D, st[:, 4, 0:NT])
                dve.wait_ge(s.g_in, at("g_in", 16))
                dve.sem_inc(s.passed, 1)

            def gla_gates():
                dve.wait_ge(s.gla_fix, at("gla_fix"))
                dve.wait_ge(s.gate_ready, at("gate_ready"))
                for d in range(2):
                    dve.wait_ge(s.gate_abs, at("gate_abs"))
                    V.tensor_scalar(view(lev, d * TOK, (FH, 2), (1, FH)), view_ps(d * 2 * HALF, (HALF, 2), (1, FH)),
                                    bg_fix[:, d:d + 1], 0.0, ALU.add, ALU.min)
                dve.drain().then_inc(s.gate_used, 1)
                dve.wait_ge(s.gate_used, at("gate_used"))
                V.memset(view(ce, TOK, (SEQS[0], 2)), 0.0).then_inc(s.dve_chain, 1)
                dve.wait_ge(s.dve_chain, at("dve_chain"))
                dve.wait_ge(s.gate_log, at("gate_log"))
                for d in range(2):
                    for start, n in ((0, SEQS[0]), (SEQS[0], SEQS[1])):
                        V.tensor_tensor_scan(view(ce, d * TOK + start + d, (1, n - d)),
                                             view(lev, d * TOK + start, (1, n - d)),
                                             view(lev, (2 + d) * TOK + start, (1, n - d)), 0.0, ALU.add, ALU.subtract)
                dve.drain().then_inc(s.dve_chain, 1)
                dve.wait_ge(s.dve_chain, at("dve_chain"))

                differences(0)

            def differences(li):
                span = LEVELS[li]
                nb = (TOK if span < 256 else SEQS[0]) // (2 * span)
                base = li % 2 * 2 * TOK
                blocks, within, mid = (2 * span, nb), (1, span), (0, span)
                ref = view(ce, span - 1, (TOK + 1, 2), blocks, mid)
                V.tensor_tensor(view(lev, base + span, (TOK, 2), blocks, within),
                                view(ce, span, (TOK, 2), blocks, within), ref, ALU.subtract)
                V.tensor_tensor(view(lev, base + TOK, (-TOK, 2), blocks, within), ref,
                                                 view(ce, 0, (TOK, 2), blocks, within), ALU.subtract).then_inc(s.lev_diff, 1)

            def scaled(li, h):
                n = TOK if LEVELS[li] < 256 else SEQS[0]
                dve.wait_ge(s.lev_exp, at("lev_exp"))
                V.tensor_tensor(view(qk, li % 2 * 2 * TOK, (1, n)), view(lev, li % 2 * 2 * TOK, (1, n)),
                                view(qk_t, h * (2 * TOK), (1, n)), ALU.mult).then_inc(s.q_ready, 1)

            def collect(n):
                dve.wait_ge(s.prod, at("prod"))
                dve.sem_inc(s.passed, 1)
                if n == 0:
                    last = V.tensor_copy(amat[:], ps[:, 0:TOK].rearrange("p (a b) -> p a b", a=NT))
                elif n <= NMASK:
                    last = V.copy_predicated(amat[:], mask[:, n - 1, :].unsqueeze(1).to_broadcast([P, NT, P]),
                                             ps[:, 0:TOK].rearrange("p (a b) -> p a b", a=NT))
                elif n == NMASK + 1:
                    last = V.tensor_copy(aoff1[:], ps[:, 0:TOK].rearrange("p (a b) -> p a b", a=NT))
                else:
                    last = V.tensor_copy(aoff2[:], ps[:, 0:2 * HALF].rearrange("p (a b c) -> p a b c", a=NTP, b=2))
                last.then_inc(s.prod_free, 1)
                dve.wait_ge(s.prod_free, at("prod_free"))
                if n == len(LEVELS):
                    dve.sem_inc(s.passed, 1)

            def gla_levels(h):
                nl = len(LEVELS)
                for li in range(nl):
                    if li + 1 < nl:
                        if li >= 1:
                            dve.wait_ge(s.k_ready, at("k_ready"))
                        differences(li + 1)
                    scaled(li, h)
                    collect(li)
                at.skip("k_ready", 2)
                collect(nl)
                dve.drain().then_inc(s.a_ready, 1)

            def drain_banks(write):
                for t in range(NT):
                    dve.wait_ge(s.gemm_ready, at("gemm_ready"))
                    write(t).then_inc(s.drained, 1)
                    at.skip("drained", 1)

            def merge(g, add):
                m = mb if add else ma
                dve.wait_ge(s.sig_ready, at("sig_ready", 2))
                for t in range(NT):
                    dve.wait_ge(s.gemm_ready, at("gemm_ready"))
                    out = view(merged, t * D + g * HALF, (1, HALF))
                    sig = view(m, t * D + g * HALF, (1, HALF))
                    if add:
                        V.tensor_tensor(sig, bank(t), sig, ALU.mult).then_inc(s.drained, 1)
                        dve.wait_ge(s.drained, at("drained"))
                        V.tensor_tensor(out, out, sig, ALU.add).then_inc(s.merged_ready, 1)
                    else:
                        V.tensor_tensor(out, bank(t), sig, ALU.mult).then_inc(s.drained, 1)
                        at.skip("drained", 1)

            def rope_tables():
                for i in range(2):
                    for half in range(2):
                        V.tensor_tensor(view(cs, i * 2 * NT * DH + half * 16, (DH, NT), (32, 2), (1, 16)),
                                        view(cs_raw, half * 16, (DH, NT), (32, 2), (1, 16)),
                                        view(g_qk, i * DH + half * 16, (0, NT), (32, 2), (1, 16)), ALU.mult)
                        V.tensor_tensor(view(cs, (i * 2 + 1) * NT * DH + half * 16, (DH, NT), (32, 2), (1, 16)),
                                        view(cs_raw, NT * DH + half * 16, (DH, NT), (32, 2), (1, 16)),
                                        view(g_qk, i * DH + (1 - half) * 16, (0, NT), (32, 2), (1, 16)), ALU.mult)
                dve.drain().then_inc(s.tables, 1)
                dve.wait_ge(s.tables, at("tables"))

            def square_sums():
                for n in range(3 * NT):
                    t, part = n // 3, n % 3
                    heads = 8 if part < 2 else KVH
                    stat = t * AH + part * 8 if part < 2 else NT * AH + t * KVH
                    dve.wait_ge(s.sq_ready, at("sq_ready"))
                    V.tensor_reduce(view(st, stat, (1, heads)), view(sq, n % 2 * HALF, (DH, heads), (1, DH)),
                                    AX.X, ALU.add).then_inc(s.sq_used, 1)

            def gate_columns(c):
                dve.wait_ge(s.sil_ready, at("sil_ready"))
                out = view(va, c * BGW, (D, NT), (1, BGW))
                V.tensor_tensor(out, out, stg[:], ALU.mult).then_inc(s.sil_used, 1)

            def rope(n):
                t, part = n // 3, n % 3
                heads = 8 if part < 2 else KVH
                src, row = (q, t * D + part * HALF) if part < 2 else (kv, t * HALF)
                stat = t * AH + part * 8 if part < 2 else NT * AH + t * KVH
                data = view(src, row, (DH, heads), (1, DH))
                turned = view(rot1, 0, (DH, heads), (1, DH))
                V.tensor_tensor(turned, data, view(cs, (part == 2) * 2 * NT * DH + t * DH, (0, heads), (1, DH)),
                                ALU.mult).then_inc(s.dve_chain, 1)
                dve.wait_ge(s.dve_chain, at("dve_chain"))
                dve.wait_ge(s.rot2_ready, at("rot2_ready"))
                V.tensor_tensor(turned, turned, view(rot2, 0, (DH, heads), (1, DH)), ALU.add).then_inc(s.dve_chain, 1)
                dve.wait_ge(s.dve_chain, at("dve_chain"))
                V.tensor_tensor(data, turned, view(st, 4 * NSTAT + stat, (1, heads), (0, DH)), ALU.mult).then_inc(s.rot2_free, 1)
                dve.wait_ge(s.rot2_free, at("rot2_free"))

            def attention_group(g):
                def stack_q(h, first):
                    dve.wait_ge(s.q_turned, at("q_turned"))
                    start, n = (0, 4 * P) if first else (4 * P, 2 * P)
                    V.tensor_copy(q_hl[:, h % 2, start:start + n], bank(4, n)).then_inc(s.q_stack, 1)

                dve.wait_ge(s.k_staged, at("k_staged"))
                V.tensor_tensor(k_st[:, 1, :, :, :], view(kv, g * DH, (HALF, NT), (0, 2), (1, DH)),
                                k_st[:, 0, :, :, :].bitcast(F32), ALU.subtract).then_inc(s.k_staged, 1)
                at.skip("k_staged", 1)
                for part, dst in enumerate((k_hh, k_ll)):
                    dve.wait_ge(s.k_turned, at("k_turned"))
                    V.tensor_copy(dst[:], ps[:, 0:TOK]).then_inc(s.k_stack, 1)
                    if part == 0:
                        stack_q(0, True)

                def row_max(n):
                    h, u = divmod(n, UNITS)
                    dve.wait_ge(s.score, at("score"))
                    k = 1 if u < NTP else 2
                    out = view(st, 2 * (n % 2), (1, k))
                    V.tensor_reduce(out, view_ps(n % 2 * HALF, (HALF // k, k), (1, HALF // k)), AX.X, ALU.max, negate=True).then_inc(s.neg_max, 1)

                def head_out(h):
                    dve.wait_ge(s.pv_done, at.peek("pv_done", 0))
                    V.reciprocal(st[:, 2, 0:NT], st[:, 1, h % 2 * NT:h % 2 * NT + NT]).then_inc(s.dve_chain, 1)
                    dve.wait_ge(s.dve_chain, at("dve_chain"))
                    V.tensor_tensor(view(q, g * (GROUP * DH) + h * DH, (D, NT), (1, DH)),
                                                      view_ps(3 * HALF, (DH, NT), (1, DH)),
                                                      view(st, 2 * NSTAT, (1, NT), (0, DH)), ALU.mult).then_inc(s.o_drained, 1)

                stack_q(0, False)
                total = GROUP * UNITS
                row_max(0)
                for n in range(total):
                    h = n // UNITS + 1
                    if n % UNITS in (1, 2) and h < GROUP:
                        stack_q(h, n % UNITS == 1)
                        if h == GROUP - 1 and n % UNITS == 2:
                            dve.sem_inc(s.group_free, 1)
                    if n + 1 < total:
                        row_max(n + 1)
                    if n % UNITS == 0 and n > 0:
                        head_out(h - 2)
                    at.skip("pv_done", 1)
                head_out(GROUP - 1)
                dve.sem_inc(s.group_free, 1)
            dve.sem_inc(s.drained, 8)
            dve.sem_inc(s.turn_free, 2)
            dve.sem_inc(s.prod_free, 1)
            dve.sem_inc(s.sq_used, 2)
            dve.sem_inc(s.rot2_free, 1)
            dve.sem_inc(s.o_drained, 1)
            dve.sem_inc(s.group_free, 2)
            dve.wait_ge(s.consts_in, 32)
            V.tensor_copy(mask[:], mask_raw[:])
            with at.repeat(DEPTH, "layer"):
                normalise()
                scaled_tokens(0)
                scaled_tokens(1)
                for t in range(NT):
                    for half in range(2):
                        turn_lo(act_hi, act_lo, [(half, t)], half * 4)
                    if t + 2 < NT:
                        scaled_tokens(t + 2)
                phase_end(dve, at, s.dve_phase)
                for half in range(2):
                    dve.wait_ge(s.gemm_ready, at("gemm_ready"))
                    V.tensor_copy(gl_t[:, half * FH:(half + 1) * FH], ps[0:2 * RANK, (6 + half) * HALF:(6 + half) * HALF + FH]).then_inc(s.drained, 1)
                    at.skip("drained", 1)
                with at.repeat(2, "gla qk") as g:
                    for b in range(8):
                        dve.wait_ge(s.gemm_ready, at("gemm_ready"))
                        V.tensor_copy(view(qk_t, g * TOK + b // 2 * 2 * TOK + b % 2 * FH, (1, FH)), bank(b, FH)).then_inc(s.drained, 1)
                        at.skip("drained", 1)
                with at.repeat(2, "gla v") as g:
                    drain_banks(lambda t: V.tensor_copy(view(va, t * D + g * HALF, (1, HALF)), bank(t)))
                at.skip("param", (2 + 2 * GH) * 16)
                phase_end(dve, at, s.dve_phase)
                gla_gates()
                with at.repeat(GH - 1, "gla head") as h:
                    gla_levels(h)
                    gla_gates()
                gla_levels(GH - 1)
                phase_end(dve, at, s.dve_phase)
                rsqrt_of(NT * GH, GV, st[:, 4, 0:NT * GH])
                dve.wait_ge(s.param, at("param", 5 * 16))
                dve.sem_inc(s.passed, 1)
                for t in range(NT):
                    for h in range(GH):
                        out = view(va, t * D + h * GV, (1, GV))
                        V.scalar_tensor_tensor(out, out, st[:, 4, t * GH + h:t * GH + h + 1], gv_row[:], ALU.mult, ALU.mult)
                rope_tables()
                square_sums()
                rsqrt_of(NSTAT, DH, st[:, 4, 0:NSTAT])
                V.tensor_scalar(st[:, 4, 0:NT * AH], st[:, 4, 0:NT * AH], DH ** -0.5, None, ALU.mult).then_inc(s.dve_chain, 1)
                dve.wait_ge(s.dve_chain, at("dve_chain"))
                for n in range(3 * NT):
                    rope(n)
                    if n in (1, 7, 13):
                        gate_columns(n // 6)
                dve.sem_inc(s.passed, 1)
                phase_end(dve, at, s.dve_phase)
                gate_columns(3)
                dve.sem_inc(s.passed, 1)
                with at.repeat(KVH, "attention group") as g:
                    attention_group(g)
                tiles = [(t, t) for t in range(NT)]
                turn_lo(o_hi, o_lo, tiles)
                turn_lo(o_hi, o_lo, tiles, 4)
                for g in range(2):
                    for some in range(2):
                        dve.wait_ge(s.zb_ready, at("zb_ready"))
                        start = g * HALF + some * (NT // 2) * D
                        out = view(q, start, (D, NT // 2), (1, HALF))
                        last = V.tensor_tensor(out, out, view(zb, start, (D, NT // 2), (1, HALF)), ALU.mult)
                last.then_inc(s.ob_ready, 1)
                merge(0, False)
                turn_lo(*b_turned[0], tiles)
                merge(1, False)
                turn_lo(*b_turned[1], tiles)
                merge(0, True)
                turn_lo(o_hi, o_lo, tiles)
                merge(1, True)
                turn_lo(o_hi, o_lo, tiles, 4)
                with at.repeat(2, "output") as g:
                    def residual(t):
                        out = view(x, t * D + g * HALF, (1, HALF))
                        return V.tensor_tensor(out, out, bank(t), ALU.add)
                    drain_banks(residual)
                phase_end(dve, at, s.dve_phase)
            normalise()
            for t in range(NT):
                V.scalar_tensor_tensor(y_out[:, t, :], x[:, t, :], st[:, 4, t:t + 1], g_row[:], ALU.mult, ALU.mult).then_inc(s.y_ready, 1)


INPUTS = ["x_prompt", "x_sample", "norm_g", "w_in", "w_gate_f", "b_gate_f", "w_gate_b", "b_gate_b", "gla_norm_g",
          "q_norm_g", "k_norm_g", "w_branch_a", "w_branch_b", "w_out", "final_norm_g"]


def shape_constants():
    tok = np.arange(P)
    masks = np.zeros((P, NMASK, P), np.float32)
    for li in range(NMASK):
        s = LEVELS[li]
        same = tok[:, None] // (2 * s) == tok[None, :] // (2 * s)
        masks[:, li, :] = same & (tok[:, None] // s != tok[None, :] // s)
    nf = DH // 4
    inv = ROPE_THETA ** (-np.arange(nf, dtype=np.float32) / np.float32(nf))
    place = np.concatenate([np.arange(n) for n in SEQS])
    angles = [(place // GRID_W).astype(np.float32)[:, None] * inv, (place % GRID_W).astype(np.float32)[:, None] * inv]
    cos = np.concatenate([np.cos(a) for a in angles for _ in range(2)], axis=1)
    sin = np.concatenate([sign * np.sin(a) for a in angles for sign in (-1, 1)], axis=1)
    by_tile = lambda a: np.ascontiguousarray(a.astype(np.float32).reshape(NT, P, DH).transpose(1, 0, 2))
    return {"identity": np.eye(P, dtype=np.float32), "masks": masks, "rope_cos": by_tile(cos), "rope_sin": by_tile(sin)}


def kernel(**inputs):
    import concourse.bacc as bacc
    from concourse.bass_utils import run_bass_kernel_spmd

    nc = bacc.Bacc("TRN2", target_bir_lowering=False, num_devices=1)
    arrays = {name: np.ascontiguousarray(inputs[name]) for name in INPUTS} | shape_constants()
    arrays = {f"in_{name}": a for name, a in arrays.items()}
    aps = [nc.dram_tensor(name, a.shape, mybir.dt.from_np(a.dtype), kind="ExternalInput").ap()
           for name, a in arrays.items()]
    outs = [nc.dram_tensor(name, (1, n, D), F32, kind="ExternalOutput").ap()
            for name, n in zip(("y_prompt", "y_sample"), SEQS)]
    trunk(nc, *aps, *outs)
    assert not WRONG, WRONG
    result = run_bass_kernel_spmd(nc, [arrays], core_ids=[0]).results[0]
    return result["y_prompt"], result["y_sample"]
```
